# Optimizing a Trainium2 kernel written in Bass

```python
import math
import jax
import jax.numpy as jnp
from jax import lax
import numpy as np

D_MODEL = 1024
BATCH = 1
SEQ = 256
DEPTH = 2

N_A_LAYERS = DEPTH // 2
N_B_LAYERS = DEPTH - N_A_LAYERS
N_DENSE = (DEPTH + 1) // 2
N_MOE = DEPTH // 2
SSM_WIDTH = D_MODEL
SSM_GROUP = 16
SSM_GROUPS = SSM_WIDTH // SSM_GROUP
SSM_STATE = 64
SSM_CHUNK = 128
DT_MIN = 1e-3
DT_MAX = 1e-1
N_HEADS = 8
QK_NOPE_DIM = 128
QK_ROPE_DIM = 64
V_HEAD_DIM = 128
QK_HEAD_DIM = QK_NOPE_DIM + QK_ROPE_DIM
Q_LORA_RANK = 384
KV_LORA_RANK = 256
ROPE_THETA = 10000.0
Q_BLOCK = 128
SOFTMAX_SCALE = QK_HEAD_DIM ** -0.5
D_FF = 2816
N_EXPERTS = 8
TOP_K = 2
EXPERT_FF = 3584
MOE_BLOCK = 128
NORM_EPS = 1e-6

kernel_name = 'hybrid_s5_mla_moe_yoco'

def _rmsnorm(x, g):
    xf = x.astype(jnp.float32)
    xf = xf * lax.rsqrt(jnp.mean(xf * xf, axis=-1, keepdims=True) + NORM_EPS)
    return (xf * g.astype(jnp.float32)).astype(x.dtype)

def _modulate(x, shift, scale):
    return x * (1.0 + scale[:, None, :]) + shift[:, None, :]

def _apply_rope(x, cos, sin):
    half = x.shape[-1] // 2
    xf = x.astype(jnp.float32)
    x1, x2 = xf[..., :half], xf[..., half:]
    return jnp.concatenate([x1 * cos - x2 * sin, x1 * sin + x2 * cos], axis=-1).astype(x.dtype)

def _ssm_combine(earlier, later):
    a1r, a1i, b1r, b1i = earlier
    a2r, a2i, b2r, b2i = later
    return (a2r * a1r - a2i * a1i,
            a2r * a1i + a2i * a1r,
            a2r * b1r - a2i * b1i + b2r,
            a2r * b1i + a2i * b1r + b2i)

def _s5_mixer(h, w_in, log_step, a_re, a_im, b_re, b_im, c_re, c_im, d_skip, w_out):
    bsz, seq, _ = h.shape
    f32 = jnp.float32
    u = jnp.matmul(h, w_in, preferred_element_type=f32)
    a_re, a_im = a_re.astype(f32), a_im.astype(f32)
    delta = jnp.exp(log_step.astype(f32))[:, None]
    mag = jnp.exp(a_re * delta)
    ang = a_im * delta
    lb_re, lb_im = mag * jnp.cos(ang), mag * jnp.sin(ang)
    den = a_re * a_re + a_im * a_im
    nr, ni = lb_re - 1.0, lb_im
    coef_re = (nr * a_re + ni * a_im) / den
    coef_im = (ni * a_re - nr * a_im) / den
    b_re, b_im = b_re.astype(f32), b_im.astype(f32)
    bb_re = coef_re[..., None] * b_re - coef_im[..., None] * b_im
    bb_im = coef_re[..., None] * b_im + coef_im[..., None] * b_re
    c_re, c_im = c_re.astype(f32), c_im.astype(f32)
    n_chunks = seq // SSM_CHUNK
    u_chunks = u.reshape(bsz, n_chunks, SSM_CHUNK, SSM_GROUPS, SSM_GROUP).transpose(1, 0, 2, 3, 4)

    def chunk_step(carry, u_c):
        h_re, h_im = carry
        bu_re = jnp.einsum('btgc,gpc->btgp', u_c, bb_re)
        bu_im = jnp.einsum('btgc,gpc->btgp', u_c, bb_im)
        ar = jnp.broadcast_to(lb_re, bu_re.shape)
        ai = jnp.broadcast_to(lb_im, bu_re.shape)
        acum_re, acum_im, s_re, s_im = lax.associative_scan(_ssm_combine, (ar, ai, bu_re, bu_im), axis=1)
        st_re = acum_re * h_re[:, None] - acum_im * h_im[:, None] + s_re
        st_im = acum_re * h_im[:, None] + acum_im * h_re[:, None] + s_im
        y = jnp.einsum('btgp,gcp->btgc', st_re, c_re) - jnp.einsum('btgp,gcp->btgc', st_im, c_im)
        return (st_re[:, -1], st_im[:, -1]), y

    init = (jnp.zeros((bsz, SSM_GROUPS, SSM_STATE), f32), jnp.zeros((bsz, SSM_GROUPS, SSM_STATE), f32))
    _, y = lax.scan(chunk_step, init, u_chunks)
    y = y.transpose(1, 0, 2, 3, 4).reshape(bsz, seq, SSM_WIDTH)
    y = jax.nn.gelu(y + d_skip.astype(f32) * u).astype(h.dtype)
    z = y @ w_out
    return z[..., :D_MODEL] * jax.nn.sigmoid(z[..., D_MODEL:])

def _mla_shared_kv(s, c_act, kv_ada_w, kv_ada_b, kv_norm, w_dkv, kv_lora_norm, w_ukv, cos, sin):
    bsz, seq, _ = s.shape
    shift, scale = jnp.split(c_act @ kv_ada_w + kv_ada_b, 2, axis=-1)
    hs = _modulate(_rmsnorm(s, kv_norm), shift, scale)
    ckr = hs @ w_dkv
    ckv = _rmsnorm(ckr[..., :KV_LORA_RANK], kv_lora_norm)
    k_rope = _apply_rope(ckr[..., KV_LORA_RANK:][:, :, None, :], cos, sin)
    kv = (ckv @ w_ukv).reshape(bsz, seq, N_HEADS, QK_NOPE_DIM + V_HEAD_DIM)
    k = jnp.concatenate([kv[..., :QK_NOPE_DIM], jnp.broadcast_to(k_rope, (bsz, seq, N_HEADS, QK_ROPE_DIM))], axis=-1)
    v = kv[..., QK_NOPE_DIM:]
    return k, v

def _causal_block_attention(q, k, v):
    bsz, seq, nh, dq = q.shape
    nqb = seq // Q_BLOCK
    q_blocks = q.reshape(bsz, nqb, Q_BLOCK, nh, dq).transpose(1, 0, 2, 3, 4)
    k_idx = jnp.arange(seq)

    def one_block(args):
        q_blk, blk = args
        s = jnp.einsum('bqhd,bkhd->bhqk', q_blk, k, preferred_element_type=jnp.float32) * SOFTMAX_SCALE
        q_idx = blk * Q_BLOCK + jnp.arange(Q_BLOCK)
        s = jnp.where((k_idx[None, :] <= q_idx[:, None])[None, None], s, -jnp.inf)
        p = jax.nn.softmax(s, axis=-1).astype(v.dtype)
        return jnp.einsum('bhqk,bkhv->bqhv', p, v)

    o = lax.map(one_block, (q_blocks, jnp.arange(nqb)))
    return o.transpose(1, 0, 2, 3, 4).reshape(bsz, seq, nh * v.shape[-1])

def _mla_attend(h, k, v, w_dq, q_norm, w_uq, w_o, cos, sin):
    bsz, seq, _ = h.shape
    q = (_rmsnorm(h @ w_dq, q_norm) @ w_uq).reshape(bsz, seq, N_HEADS, QK_HEAD_DIM)
    q = jnp.concatenate([q[..., :QK_NOPE_DIM], _apply_rope(q[..., QK_NOPE_DIM:], cos, sin)], axis=-1)
    return _causal_block_attention(q, k, v) @ w_o

def _swiglu(h, w_gu, w_down):
    gu = h @ w_gu
    return (jax.nn.silu(gu[..., :D_FF]) * gu[..., D_FF:]) @ w_down

def _moe_swiglu(h, router_w, w_gu, w_down):
    bsz, seq, d = h.shape
    hf = h.reshape(bsz * seq, d)
    n = hf.shape[0]
    nk = n * TOP_K
    logits = jnp.matmul(hf, router_w, preferred_element_type=jnp.float32)
    top_logit, top_e = lax.top_k(logits, TOP_K)
    gates = jax.nn.softmax(top_logit, axis=-1).reshape(nk)
    e_flat = top_e.reshape(nk)
    tok_flat = jnp.arange(nk, dtype=jnp.int32) // TOP_K
    order = jnp.argsort(e_flat)
    e_sorted = e_flat[order]
    tok_sorted = tok_flat[order]
    counts = jnp.bincount(e_flat, length=N_EXPERTS)
    padded = (counts + MOE_BLOCK - 1) // MOE_BLOCK * MOE_BLOCK
    start = jnp.cumsum(counts) - counts
    pend = jnp.cumsum(padded)
    pstart = pend - padded
    dest = pstart[e_sorted] + jnp.arange(nk, dtype=jnp.int32) - start[e_sorted]
    n_blk = -(-nk // MOE_BLOCK) + N_EXPERTS
    buf = jnp.zeros((n_blk * MOE_BLOCK, d), hf.dtype).at[dest].set(hf[tok_sorted])
    blk_expert = jnp.minimum(jnp.searchsorted(pend, jnp.arange(n_blk, dtype=jnp.int32) * MOE_BLOCK, side='right'), N_EXPERTS - 1)

    def expert_block(args):
        xb, e = args
        gu = xb @ w_gu[e]
        return (jax.nn.silu(gu[:, :EXPERT_FF]) * gu[:, EXPERT_FF:]) @ w_down[e]

    ybuf = lax.map(expert_block, (buf.reshape(n_blk, MOE_BLOCK, d), blk_expert)).reshape(n_blk * MOE_BLOCK, d)
    y = ybuf[dest] * gates[order][:, None].astype(hf.dtype)
    out = jnp.zeros_like(hf).at[tok_sorted].add(y)
    return out.reshape(bsz, seq, d)

def setup_inputs(seed: int = 0) -> dict:
    key = jax.random.key(seed)
    ks = jax.random.split(key, 34)
    f32 = jnp.float32

    def nrm(i, shape, scale):
        return scale * jax.random.normal(ks[i], shape, f32)

    def gain(i, shape):
        return 1.0 + 0.05 * jax.random.normal(ks[i], shape, f32)

    D = D_MODEL
    G, P, GC = SSM_GROUPS, SSM_STATE, SSM_GROUP
    offs = jax.random.randint(ks[2], (BATCH, 1), 0, 2048, jnp.int32)
    positions = offs + jnp.arange(SEQ, dtype=jnp.int32)[None, :]
    a_im_init = math.pi * jnp.arange(P, dtype=f32)
    return {
        'x': nrm(0, (BATCH, SEQ, D), 1.0),
        'c': nrm(1, (BATCH, D), 1.0),
        'positions': positions,
        'ada_w': nrm(3, (DEPTH, D, 6 * D), 0.5 * D ** -0.5),
        'ada_b': nrm(4, (DEPTH, 6 * D), 0.02),
        'norm_mix_pre': gain(5, (DEPTH, D)),
        'norm_mix_post': gain(6, (DEPTH, D)),
        'norm_ffn_pre': gain(7, (DEPTH, D)),
        'norm_ffn_post': gain(8, (DEPTH, D)),
        'ssm_w_in': nrm(9, (N_A_LAYERS, D, SSM_WIDTH), D ** -0.5),
        'ssm_log_step': jax.random.uniform(ks[10], (N_A_LAYERS, G), f32, math.log(DT_MIN), math.log(DT_MAX)),
        'ssm_a_re': -0.5 + nrm(11, (N_A_LAYERS, G, P), 0.01),
        'ssm_a_im': a_im_init + nrm(12, (N_A_LAYERS, G, P), 0.01),
        'ssm_b_re': nrm(13, (N_A_LAYERS, G, P, GC), (2 * GC) ** -0.5),
        'ssm_b_im': nrm(14, (N_A_LAYERS, G, P, GC), (2 * GC) ** -0.5),
        'ssm_c_re': nrm(15, (N_A_LAYERS, G, GC, P), (2 * P) ** -0.5),
        'ssm_c_im': nrm(16, (N_A_LAYERS, G, GC, P), (2 * P) ** -0.5),
        'ssm_d': nrm(17, (N_A_LAYERS, SSM_WIDTH), 1.0),
        'ssm_w_out': nrm(18, (N_A_LAYERS, SSM_WIDTH, 2 * D), SSM_WIDTH ** -0.5),
        'kv_ada_w': nrm(19, (D, 2 * D), 0.5 * D ** -0.5),
        'kv_ada_b': nrm(20, (2 * D,), 0.02),
        'kv_norm': gain(21, (D,)),
        'mla_w_dkv': nrm(22, (D, KV_LORA_RANK + QK_ROPE_DIM), D ** -0.5),
        'mla_kv_norm': gain(23, (KV_LORA_RANK,)),
        'mla_w_ukv': nrm(24, (KV_LORA_RANK, N_HEADS * (QK_NOPE_DIM + V_HEAD_DIM)), KV_LORA_RANK ** -0.5),
        'mla_w_dq': nrm(25, (N_B_LAYERS, D, Q_LORA_RANK), D ** -0.5),
        'mla_q_norm': gain(26, (N_B_LAYERS, Q_LORA_RANK)),
        'mla_w_uq': nrm(27, (N_B_LAYERS, Q_LORA_RANK, N_HEADS * QK_HEAD_DIM), Q_LORA_RANK ** -0.5),
        'mla_w_o': nrm(28, (N_B_LAYERS, N_HEADS * V_HEAD_DIM, D), (N_HEADS * V_HEAD_DIM) ** -0.5),
        'ffn_w_gu': nrm(29, (N_DENSE, D, 2 * D_FF), D ** -0.5),
        'ffn_w_down': nrm(30, (N_DENSE, D_FF, D), D_FF ** -0.5),
        'moe_router': nrm(31, (N_MOE, D, N_EXPERTS), D ** -0.5),
        'moe_w_gu': nrm(32, (N_MOE, N_EXPERTS, D, 2 * EXPERT_FF), D ** -0.5),
        'moe_w_down': nrm(33, (N_MOE, N_EXPERTS, EXPERT_FF, D), EXPERT_FF ** -0.5),
    }

def reference(x, c, positions, ada_w, ada_b, norm_mix_pre, norm_mix_post, norm_ffn_pre, norm_ffn_post,
              ssm_w_in, ssm_log_step, ssm_a_re, ssm_a_im, ssm_b_re, ssm_b_im, ssm_c_re, ssm_c_im, ssm_d, ssm_w_out,
              kv_ada_w, kv_ada_b, kv_norm, mla_w_dkv, mla_kv_norm, mla_w_ukv,
              mla_w_dq, mla_q_norm, mla_w_uq, mla_w_o,
              ffn_w_gu, ffn_w_down, moe_router, moe_w_gu, moe_w_down):
    c_act = jax.nn.silu(c)
    ada = jnp.einsum('bd,lde->lbe', c_act, ada_w) + ada_b[:, None, :]
    inv_freq = ROPE_THETA ** (-jnp.arange(0, QK_ROPE_DIM, 2, dtype=jnp.float32) / QK_ROPE_DIM)
    ang = positions.astype(jnp.float32)[..., None] * inv_freq
    cos = jnp.cos(ang)[:, :, None, :]
    sin = jnp.sin(ang)[:, :, None, :]
    k_shared = None
    v_shared = None
    for i in range(DEPTH):
        sh_m, sc_m, g_m, sh_f, sc_f, g_f = jnp.split(ada[i], 6, axis=-1)
        h = _modulate(_rmsnorm(x, norm_mix_pre[i]), sh_m, sc_m)
        if i < N_A_LAYERS:
            y = _s5_mixer(h, ssm_w_in[i], ssm_log_step[i], ssm_a_re[i], ssm_a_im[i], ssm_b_re[i], ssm_b_im[i],
                          ssm_c_re[i], ssm_c_im[i], ssm_d[i], ssm_w_out[i])
        else:
            if i == N_A_LAYERS:
                k_shared, v_shared = _mla_shared_kv(x, c_act, kv_ada_w, kv_ada_b, kv_norm, mla_w_dkv,
                                                    mla_kv_norm, mla_w_ukv, cos, sin)
            j = i - N_A_LAYERS
            y = _mla_attend(h, k_shared, v_shared, mla_w_dq[j], mla_q_norm[j], mla_w_uq[j], mla_w_o[j], cos, sin)
        x = x + g_m[:, None, :] * _rmsnorm(y, norm_mix_post[i])
        h = _modulate(_rmsnorm(x, norm_ffn_pre[i]), sh_f, sc_f)
        if i % 2 == 0:
            y = _swiglu(h, ffn_w_gu[i // 2], ffn_w_down[i // 2])
        else:
            y = _moe_swiglu(h, moe_router[i // 2], moe_w_gu[i // 2], moe_w_down[i // 2])
        x = x + g_f[:, None, :] * _rmsnorm(y, norm_ffn_post[i])
    return x


_drawn_inputs = setup_inputs


def setup_inputs(seed=0):
    import zlib

    import numpy as np

    out = dict(_drawn_inputs(seed))
    spreads = {}
    factors = {'ssm_a_re': 200.0,
     'mla_q_norm': 3.214,
     'ssm_log_step': 57.272,
     'ssm_a_im': 31.408,
     'ssm_b_re': 26.424,
     'ssm_b_im': 25.368,
     'ssm_c_re': 27.152,
     'ssm_c_im': 44.392,
     'kv_ada_b': 2.776}
    for name, (base, spread) in spreads.items():
        noise = np.random.default_rng([zlib.crc32(name.encode()), seed]).standard_normal(out[name].shape)
        drawn = base * np.exp(spread * noise) if base else spread * noise
        out[name] = jnp.asarray(drawn.astype(out[name].dtype))
    for name, factor in factors.items():
        out[name] = (out[name] * factor).astype(out[name].dtype)
    return out
```

```python
import concourse.bass as bass
from concourse import mybir
from contextlib import ExitStack
import numpy as np

FP32 = mybir.dt.float32
I32 = mybir.dt.int32
U32 = mybir.dt.uint32
ALU = mybir.AluOpType
ACT = mybir.ActivationFunctionType
AX = mybir.AxisListType

P = 128
D = 1024
T = 256
TB = T // P
KD = D // P
BANK = 512
WCOLS = 4096
SLOTS = 7
EPS = 1e-6
GROUPS, STATES, GC = 64, 64, 16
PAIRS = GROUPS // 2
PAIRS_KT = PAIRS // KD
CHUNK = 128
HEADS, NOPE, ROPE, VD = 8, 128, 64, 128
QLORA, KVLORA = 384, 256
SCALE = float((NOPE + ROPE) ** -0.5)
HALF = ROPE // 2
DFF, EXPERTS, EFF = 2816, 8, 3584
FG = 256
F_GROUPS = DFF // FG
E_GROUPS = EFF // FG
SLOTS_E = P
ITEMS = EXPERTS + 3
E_TILES = E_GROUPS + E_GROUPS // 2

C_ID, C_MASK, C_TRI, C_ONES, C_IOTA, C_FREQ = 0, 128, 256, 384, 512, 640
C_STEP = 672
C_N = 800
V_MIXPRE, V_MIXPOST, V_FFNPRE, V_FFNPOST = 0, 16, 32, 48
V_KVNORM, V_KVLORA, V_QNORM, V_SSMD, V_ADAB, V_C = 64, 72, 74, 77, 85, 197
V_STEP, V_ARE, V_AIM = 205, 237, 269
V_N = 301
A_SHM, A_SCM, A_GM, A_SHF, A_SCF, A_GF, A_KV = 0, 8, 16, 24, 32, 40, 96

ADA_TILES = 28
MAGIC = 12582912.0
TWO_PI = 6.283185
INV_2PI = 0.15915494309189535
PI_1, PI_2, PI_3 = 6.28125, 0.0019340515136718750, 1.2556659146e-06
LN2_1, LN2_2 = 0.693359375, -2.12194440e-4
SIN_MAX = 3.1415925


WORK = 14000
COMB = (6, 7, 4, 5)


def tile_order(groups):
    order = [("gu", 0), ("gu", 1)]
    for p in range((groups + 1) // 2):
        order += [("gu", 2 * p + 2)] * (2 * p + 2 < groups) + [("dn", p)] + [("gu", 2 * p + 3)] * (2 * p + 3 < groups)
    return order


def place(groups, kind, i):
    return tile_order(groups).index((kind, i))


def four(ap):
    return ap.rearrange("p (q c t) -> p q c t", q=PAIRS_KT, c=2)


def wide(table, shape):
    return table.rearrange("p (q t) -> p q t", q=PAIRS_KT).unsqueeze(2).broadcast_to(shape)


def tile_list():
    tiles = [("ada", i, WCOLS) for i in range(4)]
    tiles += [("w_in", i, WCOLS) for i in range(2)]
    tiles += [("ada", i, WCOLS) for i in range(4, ADA_TILES)]
    tiles += [("w_out", i, WCOLS) for i in range(4)]
    tiles += [("ffn_" + kind, g, WCOLS // (1 + (kind == "dn" and 2 * g + 2 > F_GROUPS)))
              for kind, g in tile_order(F_GROUPS)]
    tiles.append(("dkv", 0, KD * (KVLORA + ROPE)))
    tiles.append(("dq", 0, KD * QLORA))
    tiles.append(("ukv", 0, WCOLS))
    tiles.append(("uqn", 0, 3 * D))
    tiles.append(("uqr", 0, 3 * 512))
    tiles += [("wo", i, WCOLS) for i in range(2)]
    return tiles



def build(nc, a, out):
    ctx = ExitStack()
    sems = {}

    def S(name):
        if name not in sems:
            sems[name] = ctx.enter_context(nc.semaphore(name))
        return sems[name]

    def sb(name, cols, dt=FP32, rows=P):
        return ctx.enter_context(nc.sbuf_tensor(name, [rows, cols], dt))

    TILES = tile_list()
    N0 = len(TILES)
    AT = {(w, i): n for n, (w, i, _) in enumerate(TILES)}

    with ctx:
        ring = sb("ring", SLOTS * WCOLS)
        cons = sb("cons", C_N)
        vec = sb("vec", V_N)
        x = sb("x", TB * D)
        xn = sb("xn", TB * D)
        hT = sb("hT", KD * T)
        hsT = sb("hsT", KD * T)
        adaC = sb("adaC", 112)
        cact = sb("cact", KD)
        rowbuf = sb("rowbuf", BANK, rows=1)
        mcol = sb("mcol", 5 * KD)
        gcol = sb("gcol", 4 * KD)
        stat = sb("stat", 64)
        routerW = sb("routerW", KD * EXPERTS)
        pos_i = sb("pos_i", TB, I32)
        rope = sb("rope", 2 * TB * HALF)
        idx8 = sb("idx8", TB * 8, U32)
        reg_i = sb("reg_i", 16, I32)
        pow_i = sb("pow_i", PAIRS, I32)
        work = sb("work", WORK)
        psum = ctx.enter_context(nc.psum_tensor("psum", [P, 8 * BANK], FP32))

        ident = cons[:, C_ID:C_ID + P]
        ones = cons[:, C_ONES:C_ONES + P]
        iota = cons[:, C_IOTA:C_IOTA + P]

        def bank(b, o=0, n=BANK, p0=0, p1=P):
            return psum[p0:p1, b * BANK + o:b * BANK + o + n]

        class Area:

            def __init__(self):
                self.at = 0

            def take(self, n):
                self.at += n
                assert self.at <= WORK, self.at
                return work[:, self.at - n:self.at]

        def cols(ap, o, n=1):
            return ap[:, o:o + n]

        m = Area()
        b_re, b_im, c_re, c_im = (m.take(1024) for _ in range(4))
        blocks = work[:, 0:4096]
        pq3, pq4 = m.take(1024), m.take(1024)
        prods = [b_re, b_im, pq3, pq4]
        bbT = [m.take(1024), m.take(1024)]
        g_re, g_im = m.take(1024), m.take(1024)
        ph_a, ph_b = m.take(512), m.take(512)
        tabs = [(m.take(512), m.take(512)) for _ in range(2)]
        turns, mag, cf_re, cf_im = (m.take(PAIRS) for _ in range(4))
        q = [m.take(PAIRS) for _ in range(12)]
        carry = m.take(6 * PAIRS_KT)
        rot = [cols(xn, 0, 1024), cols(xn, 1024, 1024), cols(hsT, 0, 1024), cols(hsT, 1024, 1024)]
        bb = [cols(hsT, 0, 1024), cols(hsT, 1024, 1024)]
        rp = [cols(g_re, 0, 64), cols(g_re, 64, 64), cols(g_re, 128, 64)]

        m = Area()
        f_sg = m.take(TB * FG)
        f_h = m.take(2 * TB * FG)
        f_hT = m.take(2 * 2 * T)

        m = Area()
        ckv = m.take(TB * (KVLORA + 2 * ROPE))
        cq = m.take(TB * QLORA)
        ckvT = m.take(2 * T)
        krT = m.take(T)
        cqT = m.take(3 * T)
        kT = m.take(HEADS * T)
        vv = m.take(TB * HEADS * VD)
        qT = m.take(HEADS * T)
        qr = m.take(TB * HEADS * ROPE)
        qrT = m.take(4 * T)
        sc_ = m.take(2 * T)
        pT = m.take(2 * T)
        ratmp = m.take(256)
        smx = m.take(64)
        oT = hsT

        m = Area()
        e_sg = m.take(2 * FG)
        e_h = m.take(2 * FG)
        e_hT = m.take(2 * 2 * P)
        xeT = m.take(KD * P)
        pm = m.take(TB * P)
        pg = m.take(TB * P)
        pgT = m.take(T)
        ye = m.take(D)
        acc = m.take(TB * D)
        lg = m.take(TB * 8)
        mx = m.take(TB * 8)
        ixf = m.take(TB * 8)
        oh1, oh2, msel, gsel, posn = (m.take(TB * 8) for _ in range(5))
        gg = m.take(3 * TB)
        cnt, over, incl, rank, ones8 = (m.take(8) for _ in range(5))
        sel = m.take(3 * 8)
        tmp8 = m.take(8)
        posj = m.take(TB * ITEMS)
        gj = m.take(TB * ITEMS)
        eid = m.take(8)

        block = ctx.enter_context(nc.Block())

        def tile_wait(eng, n):
            eng.wait_ge(S(f"tile_loaded{n % SLOTS}"), 16 * (n // SLOTS + 1))

        def tile(n, o=0, w=WCOLS):
            return ring[:, (n % SLOTS) * WCOLS + o:(n % SLOTS) * WCOLS + o + w]

        NORMS = {"mix0": 0, "mix0p": 4, "ffn0": 8, "ffn0p": 12, "mix1": 16, "kvl": 20, "ql": 24,
                 "mix1p": 28, "ffn1": 32, "ffn1p": 36}
        NORMED = ["mix0", "ffn0", "mix1", "kvl", "ql", "ffn1"]
        TURNED = ["mix0", "ffn0", "mix1", "ffn1"]
        MODULATED = ["mix0", "ffn0", "mix1", "kv", "ffn1"]
        RESIDUALS = ["mix0p", "ffn0p", "mix1p", "ffn1p"]

        ACT_SLICES, DVE_SLICES = (0, 1, 4, 5), (2, 3, 6, 7)

        @block.sync
        def _(sp):
            sp.dma_start(vec[:, :], a["vec"]).then_inc(S("vec_loaded"), 16)
            sp.dma_start(cons[:, :], a["cons"]).then_inc(S("cons_loaded"), 16)
            sp.dma_start(x[:, :].rearrange("p (b d) -> p b d", b=TB),
                         a["x"].rearrange("(b p) d -> p b d", p=P)).then_inc(S("x_loaded"), 16)
            for n, (w, i, c) in enumerate(TILES):
                if n >= SLOTS:
                    sp.wait_ge(S("tile_used"), n - SLOTS + 1)
                sp.dma_start(tile(n, 0, c), a[w][i, :, 0:c]).then_inc(S(f"tile_loaded{n % SLOTS}"), 16)
                if n == 1:
                    sp.dma_start(blocks, a["blocks"]).then_inc(S("blocks_loaded"), 16)
                    sp.dma_start(routerW[:, :], a["router"]).then_inc(S("router_loaded"), 16)
                    sp.dma_start(pos_i[:, :], a["pos"]).then_inc(S("pos_loaded"), 16)

            def expert_tiles(j, e):
                for t in range(E_TILES):
                    kind, g = tile_order(E_GROUPS)[t]
                    n = N0 + t
                    sp.wait_ge(S("tile_used"), n - SLOTS + 1 + E_TILES * j)
                    src = a["e_gu"][e, g, :, :] if kind == "gu" else a["e_dn"][e, g, :, :]
                    sp.dma_start(tile(n), src).then_inc(S(f"tile_loaded{n % SLOTS}"), 16)

            with sp.Fori(0, EXPERTS) as j:
                expert_tiles(j, j)
            sp.wait_ge(S("items_ready"), 1)
            n_items = sp.value_load(reg_i[0:1, 0:1], min_val=EXPERTS, max_val=ITEMS)
            with sp.Fori(EXPERTS, ITEMS) as j:
                with sp.If(j < n_items):
                    e = sp.value_load(reg_i[0:1, bass.ds(j, 1)], min_val=0, max_val=EXPERTS - 1)
                    expert_tiles(j, e)
                with sp.Else():
                    sp.nop()
            for b in range(TB):
                sp.wait_ge(S("result"), b + 1)
                sp.dma_start(out[b * P:(b + 1) * P, :], x[:, b * D:(b + 1) * D]).then_inc(S("stored"), 16)
            sp.wait_ge(S("stored"), 16 * TB)

        @block.scalar
        def _(act):
            def squares(tag, src, width, step, junk, wait, each):
                k = NORMS[tag]
                for b in range(TB):
                    act.wait_ge(S(wait), each[b])
                    act.activation(cols(junk, b * width, width), cols(src, b * step, width), ACT.Square,
                                   accum_out=stat[:, k + b:k + b + 1]).then_inc(S("squares"), 1)
                act.wait_ge(S("mean"), k // 4 + 1)
                act.activation(cols(stat, k, 2), cols(stat, k + 2, 2), ACT.Sqrt).then_inc(S("root"), 1)

            def modulate(turned, scale, shift, dst):
                for k in ACT_SLICES:
                    act.wait_ge(S("turned"), 4 * TURNED.index(turned) + k // 2 + 1)
                    act.activation(cols(dst, k * T, T), bank(k // 2, (k % 2) * T, T), ACT.Identity,
                                   scale=cols(mcol, scale + k), bias=cols(adaC, shift + k)
                                   ).then_inc(S("mod_act"), 1)

            def ada_row(t):
                act.wait_ge(S("tile_used"), AT["ada", t] + 1)
                if t >= 1:
                    act.wait_ge(S("ada_turned"), t)
                act.activation(rowbuf[0:1, :], bank(6, 0, BANK, 0, 1), ACT.Copy).then_inc(S("ada_row"), 1)

            act.wait_ge(S("vec_loaded"), 16)
            act.activation(cact[:, :], cols(vec, V_C, KD), ACT.Silu).then_inc(S("cact"), 1)
            squares("mix0", x, D, D, xn, "x_loaded", [16, 16])
            act.wait_ge(S("theta"), 1)
            act.activation(q[4], q[3], ACT.Sin).then_inc(S("theta_sin"), 1)
            act.activation(q[5], q[3], ACT.Sin, scale=0.5).then_inc(S("theta_sin"), 1)
            for t in range(4):
                ada_row(t)
            act.wait_ge(S("blocks_loaded"), 16)
            act.activation(c_im, c_im, ACT.Copy, scale=-1.0).then_inc(S("c_negated"), 1)
            act.wait_ge(S("mcol0"), 1)
            modulate("mix0", 0, A_SHM, hT)
            act.wait_ge(S("tile_used"), AT["w_in", 1] + 1)
            for k in ACT_SLICES:
                act.activation(cols(hT, k * T, T), bank(k // 2, (k % 2) * T, T), ACT.Copy).then_inc(S("u_act"), 1)
            act.wait_ge(S("rope_turns"), 1)
            act.activation(cols(rope, 64, 64), rp[0], ACT.Sin, scale=TWO_PI).then_inc(S("rope_tab"), 1)
            act.activation(cols(rope, 0, 64), rp[1], ACT.Sin, scale=TWO_PI).then_inc(S("rope_tab"), 1)

            def tables(k):
                cos, sin = tabs[k % 2]
                act.wait_ge(S("phase"), k + 1)
                if k >= 2:
                    act.wait_ge(S("rotated"), 3 * (k - 1))
                    act.wait_ge(S("rotated_pool"), 2 * (k - 1))
                act.activation(sin, ph_a, ACT.Sin, scale=TWO_PI).then_inc(S("table"), 1)
                act.activation(cos, ph_b, ACT.Sin, scale=TWO_PI).then_inc(S("table"), 1)

            tables(0)
            for k in range(KD):
                if k + 1 < KD:
                    tables(k + 1)
                for t in range(4 + 3 * k, 7 + 3 * k):
                    ada_row(t)
            for k in range(KD):
                act.wait_ge(S("y_skip"), k + 1)
                act.activation(cols(hT, k * T, T), cols(hT, k * T, T), ACT.Gelu_apprx_tanh
                               ).then_inc(S("y_gelu"), 1)
            for i in range(4):
                for b in range(TB):
                    if b == 0:
                        act.wait_ge(S("z0"), i + 1)
                    else:
                        act.wait_ge(S("tile_used"), AT["w_out", i] + 1)
                    if TB * i + b >= 2:
                        act.wait_ge(S("z_gated"), TB * i + b - 1)
                    act.activation(cols(f_sg, b * FG, FG), bank(4 + b, FG, FG), ACT.Sigmoid
                                   ).then_inc(S("z_sigmoid"), 1)
            squares("mix0p", xn, D, D, hsT, "z_gated", [2 * 3 + 1, 2 * 4])
            squares("ffn0", x, D, D, hsT, "residual", [1, 2])
            modulate("ffn0", 8, A_SHF, hT)

            def swiglu(tag, blocks_, groups, h_T, sg, n0, j):
                wide = blocks_ * P

                def silu(g):
                    for b in range(blocks_):
                        if b == 0 and blocks_ == 2:
                            act.wait_ge(S(tag + "_gu"), g + 1)
                        else:
                            act.wait_ge(S("tile_used"), n0 + place(groups, 'gu', g) + 1 + j * E_TILES)
                        if blocks_ == 2:
                            if g >= 1:
                                act.wait_ge(S(tag + "_h"), 2 * g - 1 + b)
                            src, dst = bank(b, 0, FG), cols(sg, b * FG, FG)
                        else:
                            if g >= 2:
                                act.wait_ge(S(tag + "_h"), g - 1 + j * groups)
                            src, dst = bank(g % 2, 0, FG), cols(sg, (g % 2) * FG, FG)
                        act.activation(dst, src, ACT.Silu).then_inc(S(tag + "_silu"), 1)

                def turned(g):
                    act.wait_ge(S(tag + "_turned"), g + 1 + j * groups)
                    if g >= 2 and g % 2 == 0:
                        act.wait_ge(S(tag + "_down"), g // 2 + j * (groups // 2))
                    elif g >= 2:
                        act.wait_ge(S("tile_used"), n0 + place(groups, 'dn', g // 2 - 1) + 1 + j * E_TILES)
                    act.activation(cols(h_T, (g % 2) * 2 * wide, 2 * wide), bank(2 + g % 2, 0, 2 * wide),
                                   ACT.Copy).then_inc(S(tag + "_hT"), 1)

                silu(0)
                for g in range(groups):
                    if g + 1 < groups:
                        silu(g + 1)
                    turned(g)

            swiglu("f", TB, F_GROUPS, f_hT, f_sg, AT["ffn_gu", 0], 0)
            act.wait_ge(S("tile_used"), AT["ffn_dn", 5] + 1)
            act.activation(cols(xn, 0, D), psum[:, 4 * BANK:6 * BANK], ACT.Copy).then_inc(S("ffn0_y"), 1)
            squares("ffn0p", xn, D, D, hsT, "ffn0_y_all", [1, 1])
            squares("mix1", x, D, D, hsT, "residual", [3, 4])
            modulate("mix1", 16, 48 + A_SHM, hT)
            modulate("mix1", 24, A_KV, hsT)

            W3 = KVLORA + 2 * ROPE
            squares("kvl", ckv, KVLORA, W3, xn, "ckv", [1, 2])
            for k in range(2):
                act.wait_ge(S("ckv_turned"), 1)
                act.activation(cols(ckvT, k * T, T), bank(2, k * T, T), ACT.Copy, scale=cols(vec, V_KVLORA + k)
                               ).then_inc(S("ckvT"), 1)
            squares("ql", cq, QLORA, QLORA, xn, "cq", [1, 2])
            for k in range(3):
                act.wait_ge(S("cq_turned"), 1)
                act.activation(cols(cqT, k * T, T), psum[:, 3 * BANK + k * T:3 * BANK + (k + 1) * T], ACT.Copy,
                               scale=cols(vec, V_QNORM + k)).then_inc(S("cqT"), 1)
            for i in range(8):
                act.wait_ge(S("kq"), i + 1)
                dst = kT if i < 4 else qT
                act.activation(cols(dst, (i % 4) * 2 * T, 2 * T), bank(i % 2), ACT.Copy).then_inc(S("kq_out"), 1)
            for i in range(TB * HEADS):
                act.wait_ge(S("score_max"), i + 1)
                nk = P * (i // HEADS + 1)
                act.activation(cols(sc_, (i % 2) * T, nk), cols(sc_, (i % 2) * T, nk), ACT.Exp, scale=SCALE,
                               bias=cols(smx, 16 + i), accum_out=cols(smx, 32 + i)).then_inc(S("score_exp"), 1)
                act.wait_ge(S("p_turned"), i + 1)
                act.activation(cols(pT, (i % 2) * T, nk), bank(2 + i % 2, 0, nk), ACT.Copy).then_inc(S("pT"), 1)
            act.wait_ge(S("tile_used"), AT["wo", 1] + 1)
            act.activation(cols(xn, 0, D), psum[:, 4 * BANK:6 * BANK], ACT.Copy).then_inc(S("mix1_y"), 1)
            squares("mix1p", xn, D, D, hsT, "mix1_y_all", [1, 1])
            squares("ffn1", x, D, D, hsT, "residual", [5, 6])
            modulate("ffn1", 32, 48 + A_SHF, hT)
            for b in range(TB):
                act.wait_ge(S("top_gap"), b + 1)
                act.activation(cols(gg, b), cols(gg, b), ACT.Exp).then_inc(S("gap_exp"), 1)

            act.wait_ge(S("items_ready"), 1)
            n_items = act.value_load(reg_i[0:1, 0:1], min_val=EXPERTS, max_val=ITEMS)
            with act.Fori(0, ITEMS) as j:
                with act.If(j < n_items):
                    act.wait_ge(S("dispatched"), 2 * j + 1)
                    for k in range(KD // 2):
                        act.activation(cols(xeT, k * P, P), psum[:, 6 * BANK + k * P:6 * BANK + (k + 1) * P],
                                       ACT.Identity, scale=cols(mcol, 32 + k), bias=cols(adaC, 48 + A_SHF + k)
                                       ).then_inc(S("xe_act"), 1)
                    swiglu("e", 1, E_GROUPS, e_hT, e_sg, N0, j)
                    act.wait_ge(S("tile_used"), N0 + E_TILES * (j + 1))
                    act.activation(cols(ye, 0, BANK), bank(4), ACT.Copy).then_inc(S("ye_act"), 1)
                with act.Else():
                    act.nop()
            squares("ffn1p", acc, D, D, hsT, "experts_done", [1, 1])

        @block.gpsimd
        def _(pool):
            for k in range(KD):
                cos, sin = tabs[k % 2]
                pool.wait_ge(S("scanned"), k + 1)
                if k >= 1:
                    pool.wait_ge(S("y_ssm"), k)
                shape = [P, PAIRS_KT, 2, CHUNK]
                for dst, tab, g in ((prods[2], cos, g_im), (prods[3], sin, g_re)):
                    pool.tensor_tensor(four(dst), wide(tab, shape), four(g), ALU.mult
                                       ).then_inc(S("rotated_pool"), 1)

        @block.vector
        def _(dve):
            chained = [0]

            def link(ins):
                chained[0] += 1
                ins.then_inc(S("dve_chain"), 1)
                dve.wait_ge(S("dve_chain"), chained[0])

            def mean_root(tag, width):
                k = NORMS[tag]
                dve.wait_ge(S("squares"), k // 2 + 2)
                dve.tensor_scalar(cols(stat, k + 2, 2), cols(stat, k, 2), 1.0 / width, EPS, ALU.mult, ALU.add
                                  ).then_inc(S("mean"), 1)
                dve.wait_ge(S("root"), k // 4 + 1)
                link(dve.reciprocal(cols(stat, k + 2, 2), cols(stat, k, 2)))

            def normed(tag, src, width, step, dst, dstep):
                mean_root(tag, width)
                k = NORMS[tag] + 2
                for b in range(TB):
                    dve.tensor_scalar(cols(dst, b * dstep, width), cols(src, b * step, width),
                                      cols(stat, k + b), None, ALU.mult).then_inc(S("normed"), 1)

            def modulate(turned, scale, shift, dst):
                for k in DVE_SLICES:
                    dve.wait_ge(S("turned"), 4 * TURNED.index(turned) + k // 2 + 1)
                    dve.tensor_scalar(cols(dst, k * T, T), bank(k // 2, (k % 2) * T, T), cols(mcol, scale + k),
                                      cols(adaC, shift + k), ALU.mult, ALU.add).then_inc(S("mod_dve"), 1)

            def ada_cols(t, n):
                dve.wait_ge(S("ada_turned"), n)
                link(dve.tensor_tensor(cols(adaC, 4 * t, 4 * (n - t)), bank(5, t * 4, 4 * (n - t)),
                                       cols(vec, V_ADAB + 4 * t, 4 * (n - t)), ALU.add))

            def gains(dst, scale, gain):
                return dve.scalar_tensor_tensor(cols(mcol, dst, KD), cols(adaC, scale, KD), 1.0, cols(vec, gain, KD),
                                                ALU.add, ALU.mult)

            def residual(tag, gate, src):
                mean_root(tag, D)
                k = NORMS[tag] + 2
                dve.wait_ge(S("gates"), RESIDUALS.index(tag) + 1)
                for b in range(TB):
                    link(dve.scalar_tensor_tensor(cols(src, b * D, D), cols(src, b * D, D), cols(stat, k + b),
                                                  psum[:, gate * BANK:(gate + 2) * BANK], ALU.mult, ALU.mult))
                    dve.tensor_tensor(cols(x, b * D, D), cols(x, b * D, D), cols(src, b * D, D), ALU.add
                                      ).then_inc(S("residual"), 1)

            def whole_turns(dst, src, scale):
                link(dve.tensor_scalar(dst, src, scale, MAGIC, ALU.mult, ALU.add))
                link(dve.tensor_scalar(dst, dst, MAGIC, None, ALU.subtract))

            def reduced(ang, whole):
                whole_turns(whole, ang, INV_2PI)
                for part in (PI_1, PI_2, PI_3):
                    link(dve.scalar_tensor_tensor(ang, whole, -part, ang, ALU.mult, ALU.add))

            def cos_phase(dst, turn):
                link(dve.tensor_scalar(dst, turn, 0.25, None, ALU.is_gt))
                return dve.scalar_tensor_tensor(dst, turn, 0.25, dst, ALU.add, ALU.subtract)

            def exact_exp(src, t1, t2, power, rq):
                whole_turns(t1, src, 1.4426950408889634)
                link(dve.scalar_tensor_tensor(t2, t1, -LN2_1, src, ALU.mult, ALU.add))
                link(dve.scalar_tensor_tensor(t2, t1, -LN2_2, t2, ALU.mult, ALU.add))
                link(dve.tensor_scalar(rq, t2, 1.0 / 40320, 1.0 / 5040, ALU.mult, ALU.add))
                for c in (720, 120, 24, 6, 2, 1):
                    link(dve.tensor_tensor(rq, rq, t2, ALU.mult))
                    link(dve.tensor_scalar(rq, rq, 1.0 / c, None, ALU.add))
                link(dve.tensor_tensor(rq, rq, t2, ALU.mult))
                link(dve.tensor_scalar(t1, t1, 127.0, 0.0, ALU.add, ALU.max))
                link(dve.tensor_scalar(t1, t1, 255.0, 8388608.0, ALU.min, ALU.mult))
                link(dve.tensor_copy(pow_i[:, :], t1))
                link(dve.tensor_copy(power, pow_i[:, :].bitcast(FP32)))

            dve.wait_ge(S("cons_loaded"), 16)
            dve.wait_ge(S("vec_loaded"), 16)
            dve.wait_ge(S("x_loaded"), 16)
            normed("mix0", x, D, D, xn, D)
            step, are, aim = (cols(vec, V_STEP + i * PAIRS, PAIRS) for i in range(3))
            exact_exp(step, q[0], q[1], q[2], q[3])
            link(dve.scalar_tensor_tensor(q[0], q[3], 1.0, q[2], ALU.add, ALU.mult))
            link(dve.tensor_tensor(q[6], are, q[0], ALU.mult))
            link(dve.tensor_tensor(q[3], aim, q[0], ALU.mult))
            reduced(q[3], q[1])
            link(dve.tensor_scalar(turns, q[3], INV_2PI, None, ALU.mult))
            dve.tensor_scalar(q[3], q[3], SIN_MAX, -SIN_MAX, ALU.min, ALU.max).then_inc(S("theta"), 1)
            dve.wait_ge(S("theta"), 1)
            exact_exp(q[6], q[0], q[1], q[2], q[7])
            link(dve.tensor_tensor(q[7], q[7], q[2], ALU.mult))
            link(dve.tensor_tensor(mag, q[7], q[2], ALU.add))
            link(dve.scalar_tensor_tensor(q[7], q[2], -1.0, q[7], ALU.add, ALU.add))
            dve.wait_ge(S("theta_sin"), 2)
            link(dve.tensor_tensor(q[5], q[5], q[5], ALU.mult))
            link(dve.tensor_scalar(q[5], q[5], -2.0, None, ALU.mult))
            link(dve.scalar_tensor_tensor(q[6], q[5], 1.0, q[7], ALU.add, ALU.mult))
            link(dve.tensor_tensor(q[6], q[6], q[5], ALU.add))
            link(dve.tensor_tensor(q[7], mag, q[4], ALU.mult))
            link(dve.tensor_tensor(q[0], are, are, ALU.mult))
            link(dve.tensor_tensor(q[1], aim, aim, ALU.mult))
            link(dve.tensor_tensor(q[0], q[0], q[1], ALU.add))
            link(dve.reciprocal(q[0], q[0]))
            for dst, u1, u2, op in ((cf_re, q[6], q[7], ALU.add), (cf_im, q[7], q[6], ALU.subtract)):
                link(dve.tensor_tensor(q[1], u1, are, ALU.mult))
                link(dve.tensor_tensor(q[2], u2, aim, ALU.mult))
                link(dve.tensor_tensor(q[1], q[1], q[2], op))
                link(dve.tensor_tensor(dst, q[1], q[0], ALU.mult))
            dve.wait_ge(S("blocks_loaded"), 16)
            pair = lambda ap: ap.rearrange("p (q c) -> p q c", c=32)
            over_pair = lambda ap: ap.unsqueeze(2).broadcast_to([P, PAIRS, 32])
            for i, (dst, u1, u2, op) in enumerate(((bb[0], b_re, b_im, ALU.subtract), (bb[1], b_im, b_re, ALU.add))):
                link(dve.tensor_tensor(pair(pq3), pair(u1), over_pair(cf_re), ALU.mult))
                link(dve.tensor_tensor(pair(pq4), pair(u2), over_pair(cf_im), ALU.mult))
                dve.tensor_tensor(dst, pq3, pq4, op).then_inc(S("bb"), 1)
                dve.wait_ge(S("bb"), i + 1)
            ada_cols(0, 4)
            gains(0, A_SCM, V_MIXPRE).then_inc(S("mcol0"), 1)
            dve.wait_ge(S("mcol0"), 1)
            modulate("mix0", 0, A_SHM, hT)
            for i in range(2):
                dve.wait_ge(S("bb_turned"), 2 * i + 2)
                dve.tensor_copy(bbT[i], psum[:, (4 + 2 * i) * BANK:(6 + 2 * i) * BANK]).then_inc(S("bbT"), 1)

            dve.wait_ge(S("pos_loaded"), 16)
            link(dve.tensor_copy(ph_a[:, 0:TB], pos_i[:, :]))
            for b in range(TB):
                link(dve.tensor_scalar(cols(rp[0], b * HALF, HALF), cons[:, C_FREQ:C_FREQ + HALF],
                                       cols(ph_a, b), None, ALU.mult))
            reduced(rp[0], rp[2])
            link(dve.tensor_scalar(rp[0], rp[0], INV_2PI, None, ALU.mult))
            link(dve.tensor_scalar(rp[0], rp[0], 0.5, -0.5, ALU.min, ALU.max))
            cos_phase(rp[1], rp[0]).then_inc(S("rope_turns"), 1)

            def phases(k):
                if k >= 1:
                    dve.wait_ge(S("table"), 2 * k)
                step_ = cols(ph_c1, 0, CHUNK)
                link(dve.tensor_tensor(ph_a.rearrange("p (q t) -> p q t", t=CHUNK),
                                       turns[:, PAIRS_KT * k:PAIRS_KT * (k + 1)].unsqueeze(2)
                                       .broadcast_to([P, PAIRS_KT, CHUNK]),
                                       step_.unsqueeze(1).broadcast_to([P, PAIRS_KT, CHUNK]), ALU.mult))
                link(dve.tensor_scalar(ph_b, ph_a, MAGIC, MAGIC, ALU.add, ALU.subtract))
                link(dve.tensor_tensor(ph_a, ph_a, ph_b, ALU.subtract))
                cos_phase(ph_b, ph_a).then_inc(S("phase"), 1)

            ph_c1 = cons[:, C_STEP:C_STEP + CHUNK]
            phases(0)
            dve.wait_ge(S("tile_used"), AT["w_in", 1] + 1)
            for k in DVE_SLICES:
                dve.tensor_copy(cols(hT, k * T, T), bank(k // 2, (k % 2) * T, T)).then_inc(S("u_dve"), 1)
            dve.wait_ge(S("rope_tab"), 2)
            shape = [P, PAIRS_KT, 2, CHUNK]

            def skip(k):
                dve.wait_ge(S("y_ssm"), k + 1)
                dve.scalar_tensor_tensor(cols(hT, k * T, T), cols(hT, k * T, T), cols(vec, V_SSMD + k),
                                         bank(4 + 3 * (k % 2), 0, T), ALU.mult, ALU.add).then_inc(S("y_skip"), 1)

            for k in range(KD):
                cos, sin = tabs[k % 2]
                v_re, v_im = (psum[:, 0:4 * BANK].rearrange("p (q i c t) -> p q i c t", q=PAIRS_KT, i=2, c=2)[:, :, i]
                              for i in range(2))
                dve.wait_ge(S("v"), k + 1)
                dve.wait_ge(S("table"), 2 * (k + 1))
                for dst, tab, v in ((rot[0], cos, v_re), (rot[1], sin, v_im), (rot[2], cos, v_im),
                                    (rot[3], sin, v_re)):
                    dve.tensor_tensor(four(dst), wide(tab, shape), v, ALU.mult).then_inc(S("v_read"), 1)
                dve.wait_ge(S("v_read"), 4 * k + 4)
                link(dve.tensor_tensor(rot[0], rot[0], rot[1], ALU.add))
                link(dve.tensor_tensor(rot[2], rot[2], rot[3], ALU.subtract))
                if k + 1 < KD:
                    phases(k + 1)
                if k >= 1:
                    dve.wait_ge(S("rotated_pool"), 2 * k)

                def scan(g, r, j, ch, first):
                    o = j * T + ch * CHUNK
                    i = PAIRS_KT * k + j
                    return dve.tensor_tensor_scan(cols(g, o, CHUNK), cols(mag, i).broadcast_to([P, CHUNK]),
                                                  cols(r, o, CHUNK), first, ALU.mult, ALU.add)
                for j in range(PAIRS_KT):
                    for g, r in ((g_re, rot[0]), (g_im, rot[2])):
                        last = scan(g, r, j, 0, 0.0)
                        last.then_inc(S("dve_chain"), 1)
                        chained[0] += 1
                dve.wait_ge(S("dve_chain"), chained[0])
                ends = [four(g)[:, :, 0, CHUNK - 1] for g in (g_re, g_im)]
                last_t = [t_.rearrange("p (q t) -> p q t", t=CHUNK)[:, :, CHUNK - 1] for t_ in (cos, sin)]
                cc = [cols(carry, i * PAIRS_KT, PAIRS_KT) for i in range(6)]
                for dst, t_, g in ((cc[0], 0, 0), (cc[1], 1, 1), (cc[2], 0, 1), (cc[3], 1, 0)):
                    chained[0] += 1
                    dve.tensor_tensor(dst, last_t[t_], ends[g], ALU.mult).then_inc(S("dve_chain"), 1)
                dve.wait_ge(S("dve_chain"), chained[0])
                link(dve.tensor_tensor(cc[0], cc[0], cc[1], ALU.subtract))
                link(dve.tensor_tensor(cc[2], cc[2], cc[3], ALU.add))
                for j in range(PAIRS_KT):
                    for g, r, c in ((g_re, rot[0], cc[0]), (g_im, rot[2], cc[2])):
                        scan(g, r, j, 1, cols(c, j)).then_inc(S("scan"), 1)
                dve.wait_ge(S("scan"), 8 * (k + 1))
                dve.nop().then_inc(S("scanned"), 1)
                if k >= 1:
                    dve.wait_ge(S("y_ssm"), k)
                dve.tensor_tensor(four(prods[0]), wide(cos, shape), four(g_re), ALU.mult).then_inc(S("rotated"), 1)
                for ch in range(2):
                    dve.scalar_tensor_tensor(four(prods[1])[:, :, ch, :], sin.rearrange("p (q t) -> p q t", t=CHUNK),
                                             -1.0, four(g_im)[:, :, ch, :], ALU.mult, ALU.mult
                                             ).then_inc(S("rotated"), 1)
                if k >= 1:
                    skip(k - 1)
            skip(KD - 1)
            ada_cols(4, ADA_TILES)
            for dst, scale, gain in ((8, A_SCF, V_FFNPRE), (16, 48 + A_SCM, V_MIXPRE + 8), (24, A_KV + 8, V_KVNORM),
                                     (32, 48 + A_SCF, V_FFNPRE + 8)):
                gains(dst, scale, gain).then_inc(S("mcols"), 1)
            for i, (g, gain) in enumerate(((A_GM, V_MIXPOST), (A_GF, V_FFNPOST), (48 + A_GM, V_MIXPOST + 8),
                                           (48 + A_GF, V_FFNPOST + 8))):
                dve.tensor_tensor(cols(gcol, i * KD, KD), cols(adaC, g, KD), cols(vec, gain, KD), ALU.mult
                                  ).then_inc(S("mcols"), 1)
            dve.wait_ge(S("mcols"), 8)
            for i in range(4):
                for b in range(TB):
                    dve.wait_ge(S("z_sigmoid"), TB * i + b + 1)
                    dve.tensor_tensor(cols(xn, b * D + i * FG, FG), bank(4 + b, 0, FG), cols(f_sg, b * FG, FG),
                                      ALU.mult).then_inc(S("z_gated"), 1)
            residual("mix0p", 6, xn)
            dve.wait_ge(S("residual"), 2)
            normed("ffn0", x, D, D, xn, D)
            modulate("ffn0", 8, A_SHF, hT)

            def swiglu(tag, blocks_, groups, h_, sg, j):
                for g in range(groups):
                    for b in range(blocks_):
                        dve.wait_ge(S(tag + "_silu"), blocks_ * g + b + 1 + j * groups * blocks_)
                        if g >= 2 and b == 0:
                            dve.wait_ge(S(tag + "_turned"), g - 1 + j * groups)
                        bk = b if blocks_ == 2 else g % 2
                        s = b if blocks_ == 2 else g % 2
                        dve.tensor_tensor(cols(h_, ((g % 2) * blocks_ + b) * FG, FG), bank(bk, FG, FG),
                                          cols(sg, s * FG, FG), ALU.mult).then_inc(S(tag + "_h"), 1)

            swiglu("f", TB, F_GROUPS, f_h, f_sg, 0)
            dve.wait_ge(S("tile_used"), AT["ffn_dn", 5] + 1)
            link(dve.tensor_copy(cols(xn, D, D), psum[:, 6 * BANK:8 * BANK]))
            dve.wait_ge(S("ffn0_y"), 1)
            dve.nop().then_inc(S("ffn0_y_all"), 1)
            residual("ffn0p", 0, xn)
            dve.wait_ge(S("residual"), 4)
            normed("mix1", x, D, D, xn, D)
            modulate("mix1", 16, 48 + A_SHM, hT)
            modulate("mix1", 24, A_KV, hsT)

            W3 = KVLORA + 2 * ROPE
            R = KVLORA + ROPE

            def turn(dst1, dst2, x1, x2, b, lead, t1, t2):
                c_, s_ = cols(rope, b * HALF, HALF), cols(rope, 64 + b * HALF, HALF)
                if lead:
                    c_, s_ = (v_.unsqueeze(1).broadcast_to([P, lead, HALF]) for v_ in (c_, s_))
                for dst, u1, u2, f1, f2, op in ((dst1, x1, x2, c_, s_, ALU.subtract), (dst2, x1, x2, s_, c_, ALU.add)):
                    link(dve.tensor_tensor(t1, u1, f1, ALU.mult))
                    link(dve.tensor_tensor(t2, u2, f2, ALU.mult))
                    link(dve.tensor_tensor(dst, t1, t2, op))

            for b in range(TB):
                dve.wait_ge(S("ckr"), b + 1)
                o = b * W3
                link(dve.tensor_copy(cols(ckv, o, KVLORA), bank(b, 0, KVLORA)))
                k1, k2 = o + KVLORA, o + KVLORA + HALF
                turn(cols(ckv, k1, HALF), cols(ckv, k2, HALF), bank(b, KVLORA, HALF), bank(b, KVLORA + HALF, HALF),
                     b, 0, cols(ratmp, 0, HALF), cols(ratmp, HALF, HALF))
                dve.tensor_copy(cols(ckv, o + R, ROPE), cols(ckv, k1, ROPE)).then_inc(S("ckv"), 1)
            normed("kvl", ckv, KVLORA, W3, ckv, W3)
            for b in range(TB):
                dve.wait_ge(S("cq_"), b + 1)
                dve.tensor_copy(cols(cq, b * QLORA, QLORA), bank(b, 0, QLORA)).then_inc(S("cq"), 1)
            dve.wait_ge(S("ckv_turned"), 1)
            dve.tensor_copy(krT, bank(3, 0, T)).then_inc(S("krT"), 1)
            normed("ql", cq, QLORA, QLORA, cq, QLORA)
            for i in range(TB * 2):
                dve.wait_ge(S("v_kv"), i + 1)
                dve.tensor_copy(cols(vv, i * BANK, BANK), bank(4 + i)).then_inc(S("vv"), 1)
            heads = lambda ap, o: ap.rearrange("p (h d) -> p h d", h=HEADS)[:, :, o:o + HALF]
            rt = [cols(xn, i * 256, 256).rearrange("p (h d) -> p h d", h=HEADS) for i in range(2)]
            for b in range(TB):
                dve.wait_ge(S("qr_"), b + 1)
                dst = cols(qr, b * 512, 512)
                turn(heads(dst, 0), heads(dst, HALF), heads(bank(4 + b), 0), heads(bank(4 + b), HALF), b, HEADS,
                     rt[0], rt[1])
                dve.nop().then_inc(S("qr"), 1)
            for b in range(TB):
                dve.wait_ge(S("qr_turned"), b + 1)
                dve.tensor_copy(cols(qrT, b * 512, 512), bank(6 + b)).then_inc(S("qrT"), 1)

            def out_head(i):
                blk, h = divmod(i, HEADS)
                dve.wait_ge(S("o"), i + 1)
                dve.tensor_copy(cols(oT, h * T + blk * P, P), bank(4 + i % 2, 0, P)).then_inc(S("oT"), 1)

            for i in range(TB * HEADS):
                blk = i // HEADS
                nk = P * (blk + 1)
                dve.wait_ge(S("score"), i + 1)
                s_ = cols(sc_, (i % 2) * T, nk)
                if i >= 2:
                    dve.wait_ge(S("p_turned"), i - 1)
                dg = cols(sc_, (i % 2) * T + blk * P, P)
                link(dve.tensor_tensor(dg, bank(i % 2, blk * P, P), cols(cons, C_MASK, P), ALU.add))
                if blk:
                    link(dve.tensor_copy(cols(sc_, (i % 2) * T, P), bank(i % 2, 0, P)))
                link(dve.reduce_max(cols(smx, i), s_, AX.X))
                dve.tensor_scalar(cols(smx, 16 + i), cols(smx, i), -SCALE, None, ALU.mult
                                  ).then_inc(S("score_max"), 1)
                dve.wait_ge(S("score_exp"), i + 1)
                link(dve.reciprocal(cols(smx, 48 + i), cols(smx, 32 + i)))
                dve.tensor_scalar(s_, s_, cols(smx, 48 + i), None, ALU.mult).then_inc(S("probs"), 1)
                if i >= 1:
                    out_head(i - 1)
            out_head(TB * HEADS - 1)
            dve.wait_ge(S("tile_used"), AT["wo", 1] + 1)
            link(dve.tensor_copy(cols(xn, D, D), psum[:, 6 * BANK:8 * BANK]))
            dve.wait_ge(S("mix1_y"), 1)
            dve.nop().then_inc(S("mix1_y_all"), 1)
            residual("mix1p", 0, xn)
            dve.wait_ge(S("residual"), 6)
            normed("ffn1", x, D, D, xn, D)
            modulate("ffn1", 32, 48 + A_SHF, hT)

            dve.wait_ge(S("logits"), 2)
            link(dve.memset(acc[:, :], 0.0))
            link(dve.memset(ones8, 1.0))
            link(dve.tensor_copy(lg, bank(4, 0, TB * 8)))
            iota8 = cols(iota, 0, 8)
            for b in range(TB):
                o = b * 8
                link(dve.max(cols(mx, o, 8), cols(lg, o, 8)))
                link(dve.max_index(cols(idx8, o, 8), cols(mx, o, 8), cols(lg, o, 8)))
                link(dve.tensor_copy(cols(ixf, o, 8), cols(idx8, o, 8)))
                link(dve.tensor_scalar(cols(oh1, o, 8), iota8, cols(ixf, o), None, ALU.is_equal))
                link(dve.tensor_scalar(cols(oh2, o, 8), iota8, cols(ixf, o + 1), None, ALU.is_equal))
                link(dve.tensor_tensor(cols(msel, o, 8), cols(oh1, o, 8), cols(oh2, o, 8), ALU.add))
                dve.tensor_tensor(cols(gg, b), cols(mx, o + 1), cols(mx, o), ALU.subtract).then_inc(S("top_gap"), 1)
            dve.wait_ge(S("top_gap"), 2)
            dve.nop().then_inc(S("chosen"), 1)
            for b in range(TB):
                o = b * 8
                dve.wait_ge(S("gap_exp"), b + 1)
                link(dve.tensor_scalar(cols(gg, TB + b), cols(gg, b), 1.0, None, ALU.add))
                link(dve.reciprocal(cols(gg, TB + b), cols(gg, TB + b)))
                link(dve.tensor_tensor(cols(gg, 2 * TB + b), cols(gg, TB + b), cols(gg, b), ALU.mult))
                link(dve.tensor_scalar(cols(gsel, o, 8), cols(oh1, o, 8), cols(gg, TB + b), None, ALU.mult))
                link(dve.scalar_tensor_tensor(cols(gsel, o, 8), cols(oh2, o, 8), cols(gg, 2 * TB + b),
                                              cols(gsel, o, 8), ALU.mult, ALU.add))
            dve.wait_ge(S("places"), 1)
            link(dve.tensor_copy(cnt, bank(5, 2 * 8, 8)))
            link(dve.scalar_tensor_tensor(posn, bank(5, 0, TB * 8), 1.0, msel, ALU.add, ALU.mult))
            link(dve.tensor_scalar(over, cnt, float(P), None, ALU.is_gt))
            link(dve.tensor_tensor_scan(incl, ones8, over, 0.0, ALU.mult, ALU.add))
            link(dve.tensor_tensor(rank, incl, over, ALU.subtract))
            link(dve.memset(eid, 0.0))
            link(dve.tensor_scalar(cols(eid, 0), cols(incl, 7), float(EXPERTS), None, ALU.add))
            for r in range(3):
                link(dve.tensor_scalar(cols(sel, r * 8, 8), rank, float(r), None, ALU.is_equal))
                link(dve.tensor_tensor(cols(sel, r * 8, 8), cols(sel, r * 8, 8), over, ALU.mult))
                link(dve.tensor_tensor(tmp8, cols(sel, r * 8, 8), iota8, ALU.mult))
                link(dve.reduce_sum(cols(eid, 1 + r), tmp8, AX.X))
            for b in range(TB):
                o = b * ITEMS
                link(dve.tensor_scalar(cols(posj, o, 8), cols(posn, b * 8, 8), -1.0, None, ALU.add))
                link(dve.tensor_copy(cols(gj, o, 8), cols(gsel, b * 8, 8)))
                for r in range(3):
                    link(dve.tensor_tensor(tmp8, cols(sel, r * 8, 8), cols(posn, b * 8, 8), ALU.mult))
                    link(dve.reduce_sum(cols(posj, o + 8 + r), tmp8, AX.X))
                    link(dve.tensor_scalar(cols(posj, o + 8 + r), cols(posj, o + 8 + r), -1.0 - P, None, ALU.add))
                    link(dve.tensor_tensor(tmp8, cols(sel, r * 8, 8), cols(gsel, b * 8, 8), ALU.mult))
                    link(dve.reduce_sum(cols(gj, o + 8 + r), tmp8, AX.X))
            link(dve.tensor_copy(reg_i[:, 0:1], cols(eid, 0)))
            link(dve.tensor_copy(reg_i[:, 8:11], cols(eid, 1, 3)))
            dve.nop().then_inc(S("items_ready"), 1)
            n_items = dve.value_load(reg_i[0:1, 0:1], min_val=EXPERTS, max_val=ITEMS)
            with dve.Fori(0, ITEMS) as j:
                with dve.If(j < n_items):
                    for b in range(TB):
                        at = posj[:, bass.ds(b * ITEMS + j, 1)]
                        gate = gj[:, bass.ds(b * ITEMS + j, 1)]
                        dve.tensor_scalar(cols(pm, b * P, P), iota, at, None, ALU.is_equal
                                          ).then_inc(S("places_of_item"), 1)
                        dve.tensor_scalar(cols(pg, b * P, P), iota, at, gate, ALU.is_equal, ALU.mult
                                          ).then_inc(S("places_of_item"), 1)
                    dve.wait_ge(S("dispatched"), 2 * j + 2)
                    for k in range(KD // 2, KD):
                        dve.tensor_scalar(cols(xeT, k * P, P), psum[:, 6 * BANK + k * P:6 * BANK + (k + 1) * P],
                                          cols(mcol, 32 + k), cols(adaC, 48 + A_SHF + k), ALU.mult, ALU.add
                                          ).then_inc(S("xe_dve"), 1)
                    dve.wait_ge(S("gates_turned"), j + 1)
                    dve.tensor_copy(pgT, bank(2, 0, T)).then_inc(S("pgT"), 1)
                    swiglu("e", 1, E_GROUPS, e_h, e_sg, j)
                    dve.wait_ge(S("tile_used"), N0 + E_TILES * (j + 1))
                    dve.tensor_copy(cols(ye, BANK, BANK), bank(5)).then_inc(S("ye_dve"), 1)
                    for i in range(4):
                        dve.wait_ge(S("combined"), 4 * j + i + 1)
                        dve.tensor_tensor(cols(acc, i * BANK, BANK), cols(acc, i * BANK, BANK), bank(COMB[i]),
                                          ALU.add).then_inc(S("added"), 1)
                    dve.wait_ge(S("added"), 4 * (j + 1))
                    dve.memset(tmp8, 0.0)
                with dve.Else():
                    dve.nop()
            dve.nop().then_inc(S("experts_done"), 1)
            mean_root("ffn1p", D)
            dve.wait_ge(S("gates"), 4)
            for b in range(TB):
                k = NORMS["ffn1p"] + 2
                link(dve.scalar_tensor_tensor(cols(acc, b * D, D), cols(acc, b * D, D), cols(stat, k + b),
                                              psum[:, 0:2 * BANK], ALU.mult, ALU.mult))
                dve.tensor_tensor(cols(x, b * D, D), cols(x, b * D, D), cols(acc, b * D, D), ALU.add
                                  ).then_inc(S("result"), 1)

        @block.tensor
        def _(pe):
            def turned(tag, src):
                for k in range(KD):
                    for b in range(TB):
                        if k == 0:
                            pe.wait_ge(S("normed"), 2 * NORMED.index(tag) + b + 1)
                        mm = pe.transpose(bank(k // 2, (k % 2) * T + b * P, P), cols(src, b * D + k * P, P), ident)
                    if k % 2:
                        mm.then_inc(S("turned"), 1)

            def ada(t):
                n = AT["ada", t]
                if t >= 1:
                    pe.wait_ge(S("ada_row"), t)
                tile_wait(pe, n)
                for k in range(KD):
                    mm = pe.matmul(bank(6, 0, BANK, 0, 1), cols(cact, k), tile(n, k * BANK, BANK),
                                   start=(k == 0), stop=(k == KD - 1))
                mm.then_inc(S("tile_used"), 1)

            def ada_turn(t):
                pe.wait_ge(S("ada_row"), t + 1)
                for i in range(4):
                    mm = pe.matmul(bank(5, t * 4 + i, 1), rowbuf[0:1, i * P:(i + 1) * P], ones[0:1, 0:1],
                                   start=True, stop=True)
                mm.then_inc(S("ada_turned"), 1)

            def modulated(tag):
                pe.wait_ge(S("mod_act"), 4 * MODULATED.index(tag) + 4)
                pe.wait_ge(S("mod_dve"), 4 * MODULATED.index(tag) + 4)

            def gates(i, b0):
                for k in range(KD):
                    mm = pe.matmul(bank(b0 + k // 4, (k % 4) * P, P), cols(gcol, i * KD + k).broadcast_to([P, P]),
                                   ident, start=True, stop=True)
                mm.then_inc(S("gates"), 1)

            pe.wait_ge(S("cons_loaded"), 16)
            turned("mix0", xn)
            pe.wait_ge(S("cact"), 1)
            for t in range(4):
                ada(t)
                ada_turn(t)
            pe.wait_ge(S("ada_row"), 4)
            pe.wait_ge(S("mcol0"), 1)
            for i in range(2):
                pe.wait_ge(S("bb"), i + 1)
                for k in range(KD):
                    mm = pe.transpose(bank(4 + 2 * i + k // 4, (k % 4) * P, P), cols(bb[i], k * P, P), ident)
                    if k % 4 == 3:
                        mm.then_inc(S("bb_turned"), 1)
            modulated("mix0")
            n = AT["w_in", 0]
            tile_wait(pe, n)
            tile_wait(pe, n + 1)
            for c in range(KD):
                for k in range(KD):
                    mm = pe.matmul(bank(c // 2, (c % 2) * T, T), tile(n + k // 4, (k % 4) * D + c * P, P),
                                   cols(hT, k * T, T), start=(k == 0), stop=(k == KD - 1))
                    if c == KD - 1 and k in (3, 7):
                        mm.then_inc(S("tile_used"), 1)

            def v(k):
                if k >= 1:
                    pe.wait_ge(S("v_read"), 4 * k)
                for i in range(2):
                    for j in range(PAIRS_KT):
                        r = slice(32 * j, 32 * j + 32)
                        mm = pe.matmul(bank(j, i * T, T),
                                       bbT[i][r, k * P:(k + 1) * P], hT[r, k * T:(k + 1) * T],
                                       start=True, stop=True)
                mm.then_inc(S("v"), 1)

            def y(k):
                pe.wait_ge(S("c_negated"), 1)
                if k >= 2:
                    pe.wait_ge(S("y_skip"), k - 1)
                for j in range(PAIRS_KT):
                    o = (PAIRS_KT * k + j) * 32
                    for i, c in enumerate((c_re, c_re, c_im, c_im)):
                        if j == 0 and i == 0:
                            pe.wait_ge(S("rotated"), 3 * k + 3)
                            pe.wait_ge(S("rotated_pool"), 2 * k + 2)
                        mm = pe.matmul(bank(4 + 3 * (k % 2), 0, T, 32 * j, 32 * j + 32), cols(c, o, 32),
                                       cols(prods[i], j * T, T), start=(i == 0), stop=(i == 3))
                mm.then_inc(S("y_ssm"), 1)

            pe.wait_ge(S("bbT"), 2)
            pe.wait_ge(S("u_act"), 4)
            pe.wait_ge(S("u_dve"), 4)
            v(0)
            for k in range(KD):
                for t in range(4 + 3 * k, 7 + 3 * k):
                    ada(t)
                    ada_turn(t)
                if k + 1 < KD:
                    v(k + 1)
                y(k)
            pe.wait_ge(S("y_gelu"), KD)
            pe.wait_ge(S("mcols"), 8)
            for i in range(4):
                n = AT["w_out", i]
                tile_wait(pe, n)
                for b in range(TB):
                    if i >= 1:
                        pe.wait_ge(S("z_gated"), TB * (i - 1) + b + 1)
                    for k in range(KD):
                        mm = pe.matmul(bank(4 + b), cols(hT, k * T + b * P, P), tile(n, k * BANK, BANK),
                                       start=(k == 0), stop=(k == KD - 1))
                        if b == 1 and k == KD - 1:
                            mm.then_inc(S("tile_used"), 1)
                        elif k == KD - 1:
                            mm.then_inc(S("z0"), 1)
            gates(0, 6)
            turned("ffn0", xn)
            modulated("ffn0")

            def swiglu(tag, blocks_, groups, src, width, h_, h_T, n0, j):
                wide_ = blocks_ * P

                def up(g):
                    n = n0 + place(groups, 'gu', g)
                    pe.wait_ge(S(f"tile_loaded{n % SLOTS}"), 16 * (n // SLOTS + 1) + j * 16 * (E_TILES // SLOTS))
                    for b in range(blocks_):
                        if blocks_ == 2 and g >= 1:
                            pe.wait_ge(S(tag + "_h"), 2 * (g - 1) + b + 1)
                        elif blocks_ == 1 and g >= 2:
                            pe.wait_ge(S(tag + "_h"), g - 1 + j * groups)
                        dst = bank(b if blocks_ == 2 else g % 2)
                        for k in range(KD):
                            mm = pe.matmul(dst, cols(src, k * width + b * P, P), tile(n, k * BANK, BANK),
                                           start=(k == 0), stop=(k == KD - 1))
                        if b == blocks_ - 1:
                            mm.then_inc(S("tile_used"), 1)
                        else:
                            mm.then_inc(S(tag + "_gu"), 1)

                def turn(g):
                    pe.wait_ge(S(tag + "_h"), blocks_ * (g + 1 + j * groups))
                    if g >= 2:
                        pe.wait_ge(S(tag + "_hT"), g - 1 + j * groups)
                    if tag == "e" and g == 0:
                        pe.wait_ge(S("pgT"), j + 1)
                    for i in range(2):
                        for b in range(blocks_):
                            mm = pe.transpose(bank(2 + g % 2, i * wide_ + b * P, P),
                                              cols(h_, ((g % 2) * blocks_ + b) * FG + i * P, P), ident)
                    mm.then_inc(S(tag + "_turned"), 1)

                def down(g):
                    n = n0 + place(groups, 'dn', g // 2)
                    pe.wait_ge(S(f"tile_loaded{n % SLOTS}"), 16 * (n // SLOTS + 1) + j * 16 * (E_TILES // SLOTS))
                    pe.wait_ge(S(tag + "_hT"), g + 1 + j * groups)
                    for b in range(blocks_):
                        for i in range(2):
                            for c in range(2):
                                mm = pe.matmul(bank(4 + 2 * b + c),
                                               cols(h_T, (g % 2) * 2 * wide_ + i * wide_ + b * P, P),
                                               tile(n, ((g % 2) * 2 + i) * D + c * BANK, BANK),
                                               start=(g == 0 and i == 0), stop=(g == groups - 1 and i == 1))
                    if g % 2 or g == groups - 1:
                        mm.then_inc(S("tile_used"), 1)
                    else:
                        mm.then_inc(S(tag + "_down"), 1)

                up(0)
                up(1)
                turn(0)
                for p_ in range((groups + 1) // 2):
                    g = 2 * p_
                    if g + 2 < groups:
                        up(g + 2)
                    if g + 1 < groups:
                        turn(g + 1)
                    down(g)
                    if g + 1 < groups:
                        down(g + 1)
                    if g + 3 < groups:
                        up(g + 3)
                    if g + 2 < groups:
                        turn(g + 2)

            swiglu("f", TB, F_GROUPS, hT, T, f_h, f_hT, AT["ffn_gu", 0], 0)
            gates(1, 0)
            turned("mix1", xn)

            for tag, name, done, width in (("kv", "dkv", "ckr", KVLORA + ROPE), ("mix1", "dq", "cq_", QLORA)):
                src = hsT if tag == "kv" else hT
                n = AT[name, 0]
                modulated("kv")
                if tag == "mix1":
                    pe.wait_ge(S("ckv"), 2)
                tile_wait(pe, n)
                for b in range(TB):
                    for k in range(KD):
                        mm = pe.matmul(bank(b, 0, width), cols(src, k * T + b * P, P), tile(n, k * width, width),
                                       start=(k == 0), stop=(k == KD - 1))
                    mm.then_inc(S(done), 1)
            pe.wait_ge(S("cq"), 2)
            for _ in range(2):
                pe.nop().then_inc(S("tile_used"), 1)
            W3 = KVLORA + 2 * ROPE
            pe.wait_ge(S("normed"), 8)
            for b in range(TB):
                for k in range(2):
                    pe.transpose(bank(2, k * T + b * P, P), cols(ckv, b * W3 + k * P, P), ident)
                mm = pe.transpose(bank(3, b * P, P), cols(ckv, b * W3 + KVLORA, P), ident)
            mm.then_inc(S("ckv_turned"), 1)
            pe.wait_ge(S("normed"), 10)
            pe.wait_ge(S("krT"), 1)
            for b in range(TB):
                for k in range(3):
                    mm = pe.transpose(psum[:, 3 * BANK + k * T + b * P:3 * BANK + k * T + (b + 1) * P],
                                      cols(cq, b * QLORA + k * P, P), ident)
            mm.then_inc(S("cq_turned"), 1)
            for i in range(8):
                key = i < 4
                n = AT["ukv" if key else "uqn", 0]
                width, kk = (2 * D, 2) if key else (D, 3)
                src = ckvT if key else cqT
                if i == 0:
                    tile_wait(pe, n)
                    pe.wait_ge(S("ckvT"), 2)
                if i == 4:
                    nv = AT["ukv", 0]
                    pe.wait_ge(S("cqT"), 3)
                    for b in range(TB):
                        for c in range(2):
                            for k in range(2):
                                mm = pe.matmul(bank(4 + 2 * b + c), cols(ckvT, k * T + b * P, P),
                                               tile(nv, k * 2 * D + D + c * BANK, BANK), start=(k == 0),
                                               stop=(k == 1))
                            mm.then_inc(S("v_kv"), 1)
                    pe.wait_ge(S("vv"), 4)
                    pe.nop().then_inc(S("tile_used"), 1)
                    tile_wait(pe, n)
                if i >= 2:
                    pe.wait_ge(S("kq_out"), i - 1)
                for h in range(2):
                    for k in range(kk):
                        mm = pe.matmul(bank(i % 2, h * T, T), tile(n, k * width + (2 * (i % 4) + h) * P, P),
                                       cols(src, k * T, T), start=(k == 0), stop=(k == kk - 1))
                mm.then_inc(S("kq"), 1)
            pe.wait_ge(S("kq_out"), 8)
            pe.nop().then_inc(S("tile_used"), 1)
            n = AT["uqr", 0]
            tile_wait(pe, n)
            for b in range(TB):
                for k in range(3):
                    mm = pe.matmul(bank(4 + b), cols(cqT, k * T + b * P, P), tile(n, k * 512, 512), start=(k == 0),
                                   stop=(k == 2))
                mm.then_inc(S("qr_"), 1)
            pe.wait_ge(S("qr"), 2)
            pe.nop().then_inc(S("tile_used"), 1)
            for b in range(TB):
                for k in range(4):
                    mm = pe.transpose(bank(6 + b, k * P, P), cols(qr, b * 512 + k * P, P), ident)
                mm.then_inc(S("qr_turned"), 1)
            pe.wait_ge(S("qrT"), 2)

            def scores(i):
                blk, h = divmod(i, HEADS)
                nk = P * (blk + 1)
                if i >= 2:
                    pe.wait_ge(S("score_max"), i - 1)
                pe.matmul(bank(i % 2, 0, nk), cols(qT, h * T + blk * P, P), cols(kT, h * T, nk),
                          start=True, stop=False)
                r = slice(64 * (h % 2), 64 * (h % 2) + 64)
                pe.matmul(bank(i % 2, 0, nk), qrT[r, blk * 512 + (h // 2) * P:blk * 512 + (h // 2 + 1) * P],
                          krT[r, 0:nk], start=False, stop=True).then_inc(S("score"), 1)

            def attend(i):
                blk, h = divmod(i, HEADS)
                pe.wait_ge(S("probs"), i + 1)
                if i >= 2:
                    pe.wait_ge(S("pT"), i - 1)
                for kb in range(blk + 1):
                    mm = pe.transpose(bank(2 + i % 2, kb * P, P), cols(sc_, (i % 2) * T + kb * P, P), ident)
                mm.then_inc(S("p_turned"), 1)
                pe.wait_ge(S("pT"), i + 1)
                if i >= 2:
                    pe.wait_ge(S("oT"), i - 1)
                for kb in range(blk + 1):
                    mm = pe.matmul(bank(4 + i % 2, 0, P), cols(vv, kb * D + h * VD, VD),
                                   cols(pT, (i % 2) * T + kb * P, P), start=(kb == 0), stop=(kb == blk))
                mm.then_inc(S("o"), 1)

            scores(0)
            for i in range(TB * HEADS):
                if i + 1 < TB * HEADS:
                    scores(i + 1)
                attend(i)
            pe.wait_ge(S("oT"), TB * HEADS)
            n = AT["wo", 0]
            tile_wait(pe, n)
            tile_wait(pe, n + 1)
            for b in range(TB):
                for c in range(2):
                    for k in range(KD):
                        mm = pe.matmul(bank(4 + 2 * b + c), cols(oT, k * T + b * P, P),
                                       tile(n + k // 4, (k % 4) * D + c * BANK, BANK),
                                       start=(k == 0), stop=(k == KD - 1))
                        if b == TB - 1 and c == 1 and k in (3, 7):
                            mm.then_inc(S("tile_used"), 1)
            gates(2, 0)
            turned("ffn1", xn)
            modulated("ffn1")
            pe.wait_ge(S("router_loaded"), 16)
            for b in range(TB):
                for k in range(KD):
                    mm = pe.matmul(bank(4, b * 8, 8), cols(hT, k * T + b * P, P), cols(routerW, k * 8, 8),
                                   start=(k == 0), stop=(k == KD - 1))
                mm.then_inc(S("logits"), 1)
            pe.wait_ge(S("chosen"), 1)
            tri = cols(cons, C_TRI, P)
            m0, m1 = cols(msel, 0, 8), cols(msel, 8, 8)
            for dst, parts in ((0, ((tri, m0),)), (8, ((tri, m1), (ones, m0))), (16, ((ones, m0), (ones, m1)))):
                for i, (l, r) in enumerate(parts):
                    mm = pe.matmul(bank(5, dst, 8), l, r, start=(i == 0), stop=(i == len(parts) - 1))
            mm.then_inc(S("places"), 1)

            pe.wait_ge(S("items_ready"), 1)
            n_items = pe.value_load(reg_i[0:1, 0:1], min_val=EXPERTS, max_val=ITEMS)
            with pe.Fori(0, ITEMS) as j:
                with pe.If(j < n_items):
                    pe.wait_ge(S("places_of_item"), 4 * (j + 1))
                    for k in range(KD):
                        for b in range(TB):
                            mm = pe.matmul(psum[:, 6 * BANK + k * P:6 * BANK + (k + 1) * P],
                                           cols(xn, b * D + k * P, P), cols(pm, b * P, P),
                                           start=(b == 0), stop=(b == TB - 1))
                        if k % 4 == 3:
                            mm.then_inc(S("dispatched"), 1)
                    for b in range(TB):
                        mm = pe.transpose(bank(2, b * P, P), cols(pg, b * P, P), ident)
                    mm.then_inc(S("gates_turned"), 1)
                    pe.wait_ge(S("xe_act"), 4 * (j + 1))
                    pe.wait_ge(S("xe_dve"), 4 * (j + 1))
                    swiglu("e", 1, E_GROUPS, xeT, P, e_h, e_hT, N0, j)
                    pe.wait_ge(S("ye_act"), j + 1)
                    pe.wait_ge(S("ye_dve"), j + 1)
                    for i in range(4):
                        b, c = divmod(i, 2)
                        pe.matmul(bank(COMB[i]), cols(pgT, b * P, P), cols(ye, c * BANK, BANK), start=True,
                                  stop=True).then_inc(S("combined"), 1)
                    pe.wait_ge(S("added"), 4 * (j + 1))
                with pe.Else():
                    pe.nop()
            gates(3, 0)


def by_partition(v):
    return np.asarray(v).reshape(-1, P).T


def column_tiles(w, width):
    k, n = w.shape
    return np.ascontiguousarray(w.reshape(k // P, P, n // width, width).transpose(2, 1, 0, 3)).reshape(
        n // width, P, -1)


def row_tiles(w, rows):
    k, n = w.shape
    return np.ascontiguousarray(w.reshape(k // rows, rows // P, P, n).transpose(0, 2, 1, 3)).reshape(k // rows, P, -1)


def paired(w, half):
    k = w.shape[0]
    return np.ascontiguousarray(w.reshape(k, 2, half // FG, FG).transpose(0, 2, 1, 3)).reshape(k, 2 * half)


def lay_out(i):
    i = {k: np.asarray(v) for k, v in i.items()}
    c = np.zeros((P, C_N), np.float32)
    r = np.arange(P)
    c[:, C_ID:C_ID + P] = np.eye(P)
    c[:, C_MASK:C_MASK + P] = np.where(r[None, :] <= r[:, None], 0.0, -1e30)
    c[:, C_TRI:C_TRI + P] = r[:, None] < r[None, :]
    c[:, C_ONES:C_ONES + P] = 1.0
    c[:, C_IOTA:C_IOTA + P] = r[None, :]
    c[:, C_FREQ:C_FREQ + HALF] = (10000.0 ** (-np.arange(0, ROPE, 2, dtype=np.float64) / ROPE)).astype(np.float32)
    c[:, C_STEP:C_STEP + CHUNK] = r[None, :] + 1

    def states(v):
        return v.reshape(PAIRS, P).T

    parts = [by_partition(i[n].reshape(-1)) for n in ("norm_mix_pre", "norm_mix_post", "norm_ffn_pre",
                                                      "norm_ffn_post", "kv_norm", "mla_kv_norm")]
    parts += [by_partition(i["mla_q_norm"][0]), by_partition(i["ssm_d"][0]), by_partition(i["ada_b"].reshape(-1)),
              by_partition(i["kv_ada_b"]), by_partition(i["c"][0]),
              states(np.repeat(i["ssm_log_step"][0][:, None], STATES, 1)), states(i["ssm_a_re"][0]),
              states(i["ssm_a_im"][0])]

    def block_diagonal(v):
        d = np.zeros((2, STATES, PAIRS, 2, GC), np.float32)
        v = v.reshape(PAIRS, 2, STATES, GC)
        for g in range(2):
            d[g, :, :, g, :] = v[:, g].transpose(1, 0, 2)
        return d.reshape(P, PAIRS * 32)

    blocks = [block_diagonal(i["ssm_b_re"][0]), block_diagonal(i["ssm_b_im"][0]),
              block_diagonal(i["ssm_c_re"][0].transpose(0, 2, 1)), block_diagonal(i["ssm_c_im"][0].transpose(0, 2, 1))]
    ukv = i["mla_w_ukv"].reshape(KVLORA, HEADS, 2, P).transpose(0, 2, 1, 3).reshape(KVLORA, 2 * D)
    uq = i["mla_w_uq"][0].reshape(QLORA, HEADS, NOPE + ROPE)
    return {
        "x": i["x"][0],
        "vec": np.ascontiguousarray(np.concatenate(parts, 1)),
        "cons": c,
        "blocks": np.ascontiguousarray(np.concatenate(blocks, 1)),
        "router": row_tiles(i["moe_router"][0], D)[0],
        "pos": np.ascontiguousarray(i["positions"].astype(np.int32).reshape(TB, P).T),
        "ada": column_tiles(np.concatenate([i["ada_w"][0], i["ada_w"][1], i["kv_ada_w"]], 1), BANK),
        "w_in": row_tiles(i["ssm_w_in"][0], 512),
        "w_out": column_tiles(paired(i["ssm_w_out"][0], D), BANK),
        "ffn_gu": column_tiles(paired(i["ffn_w_gu"][0], DFF), BANK),
        "ffn_dn": row_tiles(np.concatenate([i["ffn_w_down"][0], np.zeros((FG, D), np.float32)], 0), 512),
        "dkv": row_tiles(i["mla_w_dkv"], D),
        "dq": row_tiles(i["mla_w_dq"][0], D),
        "ukv": row_tiles(ukv, KVLORA),
        "uqn": row_tiles(np.ascontiguousarray(uq[:, :, :NOPE].reshape(QLORA, D)), QLORA),
        "uqr": row_tiles(np.ascontiguousarray(uq[:, :, NOPE:].reshape(QLORA, 512)), QLORA),
        "wo": row_tiles(i["mla_w_o"][0], 512),
        "e_gu": np.stack([column_tiles(paired(w, EFF), BANK) for w in i["moe_w_gu"][0]]),
        "e_dn": np.stack([row_tiles(w, 512) for w in i["moe_w_down"][0]]),
    }


def kernel(**inputs):
    import concourse.bacc as bacc
    from concourse.bass_utils import run_bass_kernel_spmd

    nc = bacc.Bacc("TRN2", target_bir_lowering=False, num_devices=1)
    arrays = lay_out(inputs)
    aps = {n: nc.dram_tensor("in_" + n, v.shape, mybir.dt.from_np(v.dtype), kind="ExternalInput").ap()
           for n, v in arrays.items()}
    out = nc.dram_tensor("out_x", (T, D), FP32, kind="ExternalOutput").ap()
    build(nc, aps, out)
    r = run_bass_kernel_spmd(nc, [{"in_" + n: v for n, v in arrays.items()}], core_ids=[0])
    return r.results[0]["out_x"].reshape(1, T, D)
```

```python
import concourse.bass as bass
from concourse import mybir
from contextlib import ExitStack
import numpy as np

FP32 = mybir.dt.float32
FP32R = mybir.dt.float32r
I32 = mybir.dt.int32
U32 = mybir.dt.uint32
ALU = mybir.AluOpType
ACT = mybir.ActivationFunctionType
AX = mybir.AxisListType

P = 128
D = 1024
T = 256
TB = T // P
KD = D // P
BANK = 512
WCOLS = 4096
SLOTS = 7
EPS = 1e-6
GROUPS, STATES, GC = 64, 64, 16
PAIRS = GROUPS // 2
PAIRS_KT = PAIRS // KD
CHUNK = 128
WORK = 14000
HEADS, NOPE, ROPE, VD = 8, 128, 64, 128
QLORA, KVLORA = 384, 256
SCALE = float((NOPE + ROPE) ** -0.5)
HALF = ROPE // 2
DFF, EXPERTS, EFF = 2816, 8, 3584
FG = 256
F_GROUPS = DFF // FG
E_GROUPS = EFF // FG
SLOTS_E = P
ITEMS = EXPERTS + 3
E_TILES = E_GROUPS + E_GROUPS // 2
QUARTER = WCOLS // 4
Q_OUT = 0
Q_FFN = 4 * 4
Q_EXP = Q_FFN + 4 * 16 + 2
E_QUARTERS = 4 * E_TILES
SPLIT0 = WORK - 8 * QUARTER

C_ID, C_MASK, C_TRI, C_ONES, C_IOTA, C_FREQ = 0, 128, 256, 384, 512, 640
C_STEP = 672
C_N = 800
V_MIXPRE, V_MIXPOST, V_FFNPRE, V_FFNPOST = 0, 16, 32, 48
V_KVNORM, V_KVLORA, V_QNORM, V_SSMD, V_ADAB, V_C = 64, 72, 74, 77, 85, 197
V_STEP, V_ARE, V_AIM = 205, 237, 269
V_N = 301
A_SHM, A_SCM, A_GM, A_SHF, A_SCF, A_GF, A_KV = 0, 8, 16, 24, 32, 40, 96

ADA_TILES = 28
PE_ADA = [[8], [11], [13], [16], [18], [20, 23], [25], [27]]
DVE_ADA_SLICE = [[9, 10], [12], [14, 15], [17], [19], [21, 22], [24], [26]]
DVE_ADA = [3, 4, 5, 6, 7] + [t for ts in DVE_ADA_SLICE for t in ts]
EARLY_ADA = 3
PE_ROWS = [0, 1, 2] + [t for ts in PE_ADA for t in ts]
MAGIC = 12582912.0
TWO_PI = 6.283185
INV_2PI = 0.15915494309189535
PI_1, PI_2, PI_3 = 6.28125, 0.0019340515136718750, 1.2556659146e-06
LN2_1, LN2_2 = 0.693359375, -2.12194440e-4
SIN_MAX = 3.1415925


TURN_BANK = {2: (0, 2), 1: (2, 3)}
Z_BANKS = ((0, 1), (4, 5))
COMB = (6, 7, 4, 5)


def tile_order(groups):
    order = [("gu", 0), ("gu", 1), ("gu", 2)]
    for p in range((groups + 1) // 2):
        order += [("gu", 2 * p + 3)] * (2 * p + 3 < groups) + [("dn", p)] + [("gu", 2 * p + 4)] * (2 * p + 4 < groups)
    return order


def place(groups, kind, i):
    return tile_order(groups).index((kind, i))


def quarters_before(groups, kind, g):
    return 4 * g + 2 * max(g - 2, 0) if kind == "gu" else 4 * min(g + 3, groups) + 2 * g


def four(ap):
    return ap.rearrange("p (q c t) -> p q c t", q=PAIRS_KT, c=2)


def wide(table, shape):
    return table.rearrange("p (q t) -> p q t", q=PAIRS_KT).unsqueeze(2).broadcast_to(shape)


def tile_list():
    tiles = [("ada", i, WCOLS) for i in range(4)]
    tiles += [("w_in", i, WCOLS) for i in range(2)]
    tiles += [("ada", i, WCOLS) for i in range(4, ADA_TILES)]
    tiles += [("w_out", i, WCOLS) for i in range(4)]
    tiles += [("ffn_" + kind, g, WCOLS // (1 + (kind == "dn" and 2 * g + 2 > F_GROUPS)))
              for kind, g in tile_order(F_GROUPS)]
    tiles.append(("dkv", 0, KD * (KVLORA + ROPE)))
    tiles.append(("dq", 0, KD * QLORA))
    tiles.append(("ukv", 0, WCOLS))
    tiles.append(("uqn", 0, 3 * D))
    tiles.append(("uqr", 0, 3 * 512))
    tiles += [("wo", i, WCOLS) for i in range(2)]
    return tiles



def build(nc, a, out):
    ctx = ExitStack()
    sems = {}

    def S(name):
        if name not in sems:
            sems[name] = ctx.enter_context(nc.semaphore(name))
        return sems[name]

    at_byte = {}

    def sb(name, cols, dt=FP32, rows=P):
        at_byte[name] = -(-nc.sbuf_base // 32) * 32
        return ctx.enter_context(nc.sbuf_tensor(name, [rows, cols], dt))

    TILES = tile_list()
    N0 = len(TILES)
    AT = {(w, i): n for n, (w, i, _) in enumerate(TILES)}
    SUMMED = [AT["ada", t] for t in DVE_ADA]

    def tile_done(n):
        if n in SUMMED:
            return S("ada_summed"), SUMMED.index(n) + 1
        return S("tile_used"), n + 1 - sum(m < n for m in SUMMED)

    with ctx:
        ring = sb("ring", SLOTS * WCOLS)
        cons = sb("cons", C_N)
        vec = sb("vec", V_N)
        x = sb("x", TB * D)
        xn = sb("xn", TB * D)
        hT = sb("hT", KD * T)
        hsT = sb("hsT", KD * T)
        adaC = sb("adaC", 112)
        cact = sb("cact", KD)
        rowbuf = sb("rowbuf", BANK, rows=1)
        mcol = sb("mcol", 5 * KD)
        gcol = sb("gcol", 4 * KD)
        stat = sb("stat", 64)
        routerW = sb("routerW", KD * EXPERTS)
        pos_i = sb("pos_i", TB, I32)
        rope = sb("rope", 2 * TB * HALF)
        idx8 = sb("idx8", TB * 8, U32)
        reg_i = sb("reg_i", 16, I32)
        pow_i = sb("pow_i", PAIRS, I32)
        work = sb("work", WORK)

        def rounded(name, over, o, n):
            return nc.alloc_sbuf_tensor_at(name, [P, n], FP32R, offset=at_byte[over] + 4 * o)

        w_hi = [rounded(f"w_hi{i}", "work", SPLIT0 + i * QUARTER, QUARTER) for i in range(4)]
        w_lo = [rounded(f"w_lo{i}", "work", SPLIT0 + (4 + i) * QUARTER, QUARTER) for i in range(4)]
        s_hi, s_lo = rounded("s_hi", "xn", 0, KD * T), rounded("s_lo", "hsT", 0, KD * T)
        psum = ctx.enter_context(nc.psum_tensor("psum", [P, 8 * BANK], FP32))

        ident = cons[:, C_ID:C_ID + P]
        ones = cons[:, C_ONES:C_ONES + P]
        iota = cons[:, C_IOTA:C_IOTA + P]

        def bank(b, o=0, n=BANK, p0=0, p1=P):
            return psum[p0:p1, b * BANK + o:b * BANK + o + n]

        class Area:

            def __init__(self):
                self.at = 0

            def take(self, n):
                self.at += n
                assert self.at <= WORK, self.at
                return work[:, self.at - n:self.at]

            def skip(self, n):
                self.at += n
                return self.at - n

        def cols(ap, o, n=1):
            return ap[:, o:o + n]

        m = Area()
        b_re, b_im, c_re, c_im = (m.take(1024) for _ in range(4))
        blocks = work[:, 0:4096]
        pq3, pq4 = m.take(1024), m.take(1024)
        prods = [b_re, b_im, pq3, pq4]
        bbT = [m.take(1024), m.take(1024)]
        g_re, g_im = m.take(1024), m.take(1024)
        ph_a, ph_b = m.take(512), m.take(512)
        tabs = [(m.take(512), m.take(512)) for _ in range(2)]
        turns, mag, cf_re, cf_im = (m.take(PAIRS) for _ in range(4))
        part_sum = m.take(BANK)
        q = [cols(part_sum, i * PAIRS, PAIRS) for i in range(8)]
        half_pi = m.take(1)
        carry = m.take(6 * PAIRS_KT)
        sums = [cols(g_im, 0, BANK), cols(g_im, BANK, BANK), tabs[1][0], tabs[1][1], cols(g_im, 0, BANK)]
        rot = [cols(xn, 0, 1024), cols(xn, 1024, 1024), cols(hsT, 0, 1024)]
        cn_re = cols(hsT, 1024, 1024)
        bb = [cols(hsT, 0, 1024), cols(hsT, 1024, 1024)]
        rp = [cols(g_re, 0, 64), cols(g_re, 64, 64), cols(g_re, 128, 64), cols(g_re, 192, TB)]

        m = Area()
        f_sg = m.take(TB * FG)
        f_h = m.take(2 * TB * FG)
        f_hi, f_lo = (rounded(f"f_{n}", "work", m.skip(4 * T), 4 * T) for n in ("hi", "lo"))
        zz = m.take(TB * D)
        assert m.at <= SPLIT0

        m = Area()
        ckv = m.take(TB * (KVLORA + 2 * ROPE))
        cq = m.take(TB * QLORA)
        ckvT = m.take(2 * T)
        krT = m.take(T)
        cqT = m.take(3 * T)
        kT = m.take(HEADS * T)
        vv = m.take(TB * HEADS * VD)
        qT = m.take(HEADS * T)
        qr = m.take(TB * HEADS * ROPE)
        qrT = m.take(4 * T)
        sc_ = m.take(2 * T)
        probT = m.take(2 * T)
        ratmp = m.take(256)
        smx = m.take(64)
        oT = hsT

        m = Area()
        e_sg = m.take(2 * FG)
        e_h = m.take(2 * FG)
        e_hi, e_lo = (rounded(f"e_{n}", "work", m.skip(4 * P), 4 * P) for n in ("hi", "lo"))
        xe_hi, xe_lo = (rounded(f"xe_{n}", "work", m.skip(KD * P), KD * P) for n in ("hi", "lo"))
        pm = m.take(TB * P)
        pT = rounded("pT_e", "work", m.skip(T), T)
        gate_t, gate_s = m.take(TB), m.take(1)
        ye_hi, ye_lo = rounded("ye_hi", "hsT", 0, D), rounded("ye_lo", "hsT", D, D)
        xeT = cols(hsT, 0, D)
        acc = hT
        lg = m.take(TB * 8)
        mx = m.take(TB * 8)
        ixf = m.take(TB * 8)
        oh1, oh2, msel, gsel, posn = (m.take(TB * 8) for _ in range(5))
        gg = m.take(3 * TB)
        cnt, over, incl, rank, ones8 = (m.take(8) for _ in range(5))
        sel = m.take(3 * 8)
        tmp8 = m.take(8)
        posj = m.take(TB * (ITEMS + 1))
        gj = m.take(TB * (ITEMS + 1))
        eid = m.take(8)
        silu_tab = m.take(1)
        assert m.at <= SPLIT0

        block = ctx.enter_context(nc.Block())

        def tile_wait(eng, n):
            eng.wait_ge(S(f"tile_loaded{n % SLOTS}"), 16 * (n // SLOTS + 1))

        def tile(n, o=0, w=WCOLS):
            return ring[:, (n % SLOTS) * WCOLS + o:(n % SLOTS) * WCOLS + o + w]

        NORMS = {"mix0": 0, "mix0p": 4, "ffn0": 8, "ffn0p": 12, "mix1": 16, "kvl": 20, "ql": 24,
                 "mix1p": 28, "ffn1": 32, "ffn1p": 36}
        NORMED = ["mix0", "ffn0", "mix1", "kvl", "ql", "ffn1"]
        TURNED = ["mix0", "ffn0", "mix1", "ffn1"]
        MODULATED = ["mix0", "ffn0", "mix1", "kv", "ffn1"]
        RESIDUALS = ["mix0p", "ffn0p", "mix1p", "ffn1p"]

        ACT_SLICES, DVE_SLICES = (0, 1, 4, 5), (2, 3, 6, 7)

        @block.sync
        def _(sp):
            sp.dma_start(vec[:, :], a["vec"]).then_inc(S("vec_loaded"), 16)
            sp.dma_start(cons[:, :], a["cons"]).then_inc(S("cons_loaded"), 16)
            sp.dma_start(x[:, :].rearrange("p (b d) -> p b d", b=TB),
                         a["x"].rearrange("(b p) d -> p b d", p=P)).then_inc(S("x_loaded"), 16)
            for n, (w, i, c) in enumerate(TILES):
                if n >= SLOTS:
                    sp.wait_ge(*tile_done(n - SLOTS))
                sp.dma_start(tile(n, 0, c), a[w][i, :, 0:c]).then_inc(S(f"tile_loaded{n % SLOTS}"), 16)
                if n == AT["w_in", 1]:
                    sp.dma_start(blocks, a["blocks"]).then_inc(S("blocks_loaded"), 16)
                    sp.dma_start(routerW[:, :], a["router"]).then_inc(S("router_loaded"), 16)
                    sp.dma_start(pos_i[:, :], a["pos"]).then_inc(S("pos_loaded"), 16)

            def expert_tiles(j, e):
                for t in range(E_TILES):
                    kind, g = tile_order(E_GROUPS)[t]
                    n = N0 + t
                    sp.wait_ge(S("tile_used"), tile_done(n - SLOTS)[1] + E_TILES * j)
                    src = a["e_gu"][e, g, :, :] if kind == "gu" else a["e_dn"][e, g, :, :]
                    sp.dma_start(tile(n), src).then_inc(S(f"tile_loaded{n % SLOTS}"), 16)

            with sp.Fori(0, EXPERTS) as j:
                expert_tiles(j, j)
            sp.wait_ge(S("items_ready"), 1)
            n_items = sp.value_load(reg_i[0:1, 0:1], min_val=EXPERTS, max_val=ITEMS)
            with sp.Fori(EXPERTS, ITEMS) as j:
                with sp.If(j < n_items):
                    e = sp.value_load(reg_i[0:1, bass.ds(j, 1)], min_val=0, max_val=EXPERTS - 1)
                    expert_tiles(j, e)
                with sp.Else():
                    sp.nop()
            for b in range(TB):
                sp.wait_ge(S("result"), b + 1)
                sp.dma_start(out[b * P:(b + 1) * P, :], x[:, b * D:(b + 1) * D]).then_inc(S("stored"), 16)
            sp.wait_ge(S("stored"), 16 * TB)

        @block.scalar
        def _(act):
            def squares(tag, src, width, step, junk, wait, each):
                k = NORMS[tag]
                for b in range(TB):
                    act.wait_ge(S(wait), each[b])
                    act.activation(cols(junk, b * width, width), cols(src, b * step, width), ACT.Square,
                                   accum_out=stat[:, k + b:k + b + 1]).then_inc(S("squares"), 1)
                act.wait_ge(S("mean"), k // 4 + 1)
                act.activation(cols(stat, k, 2), cols(stat, k + 2, 2), ACT.Sqrt).then_inc(S("root"), 1)

            def modulate(turned, scale, shift, dst):
                for k in ACT_SLICES:
                    act.wait_ge(S("turned"), 4 * TURNED.index(turned) + k // 2 + 1)
                    act.activation(cols(dst, k * T, T), bank(k // 2, (k % 2) * T, T), ACT.Identity,
                                   scale=cols(mcol, scale + k), bias=cols(adaC, shift + k)
                                   ).then_inc(S("mod_act"), 1)

            def ada_row(i, t):
                act.wait_ge(*tile_done(AT["ada", t]))
                if i >= 1:
                    act.wait_ge(S("ada_turned"), i)
                act.activation(rowbuf[0:1, :], bank(6 + i % 2, 0, BANK, 0, 1), ACT.Copy).then_inc(S("ada_row"), 1)

            act.wait_ge(S("vec_loaded"), 16)
            act.activation(cact[:, :], cols(vec, V_C, KD), ACT.Silu).then_inc(S("cact"), 1)
            squares("mix0", x, D, D, xn, "x_loaded", [16, 16])
            act.wait_ge(S("theta"), 1)
            act.activation(q[4], q[3], ACT.Sin).then_inc(S("theta_sin"), 1)
            act.activation(q[5], q[3], ACT.Sin, scale=0.5).then_inc(S("theta_sin"), 1)
            for t in range(EARLY_ADA):
                ada_row(t, t)
            act.wait_ge(S("mcol0"), 1)
            modulate("mix0", 0, A_SHM, hT)
            act.wait_ge(S("rope_turns"), 1)
            act.activation(cols(rope, 64, 64), rp[0], ACT.Sin, scale=TWO_PI).then_inc(S("rope_tab"), 1)
            act.activation(cols(rope, 0, 64), rp[1], ACT.Sin, scale=TWO_PI).then_inc(S("rope_tab"), 1)

            def tables(k):
                cos, sin = tabs[k % 2]
                act.wait_ge(S("phase"), k + 1)
                if k == 1:
                    act.wait_ge(S("sum_turned"), len(sums))
                if k >= 2:
                    act.wait_ge(S("v_read"), 4 * (k - 1))
                    act.wait_ge(S("rotated"), 4 * (k - 1))
                act.activation(sin, ph_a, ACT.Sin, scale=TWO_PI).then_inc(S("table"), 1)
                act.activation(ph_b, ph_a, ACT.Abs).then_inc(S("phase_abs"), 1)
                act.wait_ge(S("phase_abs"), k + 1)
                act.activation(cos, ph_b, ACT.Sin, scale=-TWO_PI, bias=half_pi).then_inc(S("table"), 1)

            tables(0)
            act.wait_ge(S("blocks_loaded"), 16)
            act.activation(c_im, c_im, ACT.Copy, scale=-1.0).then_inc(S("c_negated"), 1)
            act.wait_ge(*tile_done(AT["w_in", 1]))
            for k in ACT_SLICES:
                act.activation(cols(hT, k * T, T), bank(k // 2, (k % 2) * T, T), ACT.Copy).then_inc(S("u_act"), 1)
            act.wait_ge(S("bb_turned"), 4)
            act.activation(bbT[1], psum[:, 6 * BANK:8 * BANK], ACT.Copy).then_inc(S("bbT_im"), 1)
            act.activation(cn_re, c_re, ACT.Copy, scale=-1.0).then_inc(S("c_negated"), 1)
            i = EARLY_ADA
            for k in range(KD):
                if k + 1 < KD:
                    tables(k + 1)
                for t in PE_ADA[k]:
                    ada_row(i, t)
                    i += 1
            for k in range(KD):
                act.wait_ge(S("y_skip"), k + 1)
                act.activation(cols(hT, k * T, T), cols(hT, k * T, T), ACT.Gelu_apprx_tanh
                               ).then_inc(S("y_gelu"), 1)
                if k == KD - 2:
                    act.wait_ge(S("scan"), 8 * KD)
                for k_ in range(KD - 1) if k == KD - 2 else [k] if k == KD - 1 else []:
                    act.wait_ge(S("y_gelu"), k_ + 1)
                    act.activation(s_hi[:, k_ * T:(k_ + 1) * T], cols(hT, k_ * T, T), ACT.Copy
                                   ).then_inc(S("s_hi"), 1)

            def split(q0, n, o, quarters, j=0, first=0):
                for i in range(first, quarters):
                    qn = q0 + i
                    if i == first:
                        act.wait_ge(S(f"tile_loaded{n % SLOTS}"), 16 * (n // SLOTS + 1) + j * 16 * (E_TILES // SLOTS))
                    if qn >= 4:
                        act.wait_ge(S("quarter_used"), qn - 3 + j * E_QUARTERS)
                    act.activation(w_hi[qn % 4][:, :], tile(n, i * QUARTER, QUARTER), ACT.Copy
                                   ).then_inc(S("w_hi"), 1)

            split(Q_OUT, AT["w_out", 0], 0, 4)
            for i in range(4):
                if i < 3:
                    split(Q_OUT + 4 * (i + 1), AT["w_out", i + 1], 0, 4)
                act.wait_ge(S("quarter_used"), Q_OUT + 4 * (i + 1))
                for b in range(TB):
                    if i >= 1:
                        act.wait_ge(S("z_gated"), TB * (i - 1) + b + 1)
                    act.activation(cols(f_sg, b * FG, FG), bank(Z_BANKS[i % 2][b], FG, FG), ACT.Sigmoid
                                   ).then_inc(S("z_sigmoid"), 1)
            squares("mix0p", zz, D, D, hsT, "z_gated", [2 * 3 + 1, 2 * 4])
            squares("ffn0", x, D, D, hsT, "residual", [1, 2])
            modulate("ffn0", 8, A_SHF, hT)
            for k in range(KD):
                act.wait_ge(S("mod_act"), 8)
                act.wait_ge(S("mod_dve"), 8)
                act.activation(s_hi[:, k * T:(k + 1) * T], cols(hT, k * T, T), ACT.Copy).then_inc(S("s_hi"), 1)

            def swiglu(tag, blocks_, groups, h_hi, sg, n0, q0, j):
                wide = blocks_ * P

                def used(kind, g):
                    return q0 + quarters_before(groups, kind, g) + (4 if kind == "gu" else 2) + j * E_QUARTERS

                def part(kind, g, i0=0, i1=4):
                    q1 = q0 + quarters_before(groups, kind, g)
                    if kind == "gu":
                        split(q1, n0 + place(groups, kind, g), 0, i1, j, i0)
                    else:
                        h = 2 * (g % 2)
                        split(q1 - h, n0 + place(groups, kind, g // 2), 0, h + 2, j, h)

                def silu(g):
                    act.wait_ge(S("quarter_used"), used("gu", g))
                    for b in range(blocks_):
                        if blocks_ == 2:
                            if g >= 1:
                                act.wait_ge(S(tag + "_h"), 2 * g - 1 + b)
                            src, dst = bank(2 * (g % 2) + b, 0, FG), cols(sg, b * FG, FG)
                        else:
                            if g >= 2:
                                act.wait_ge(S(tag + "_h"), g - 1 + j * groups)
                            src, dst = bank(g % 2, 0, FG), cols(sg, (g % 2) * FG, FG)
                        act.activation(dst, src, ACT.Silu).then_inc(S(tag + "_silu"), 1)

                def turned(g):
                    act.wait_ge(S(tag + "_turned"), g + 1 + j * groups)
                    if g >= 2:
                        act.wait_ge(S("quarter_used"), used("dn", g - 2))
                    act.activation(h_hi[:, (g % 2) * 2 * wide:(g % 2 + 1) * 2 * wide],
                                   bank(TURN_BANK[blocks_][g % 2], 0, 2 * wide),
                                   ACT.Copy).then_inc(S(tag + "_hi"), 1)

                part("gu", 0)
                if blocks_ == 1:
                    gated_result(j)
                part("gu", 1)
                silu(0)
                part("gu", 2, 0, 2)
                silu(1)
                turned(0)
                part("gu", 2, 2, 4)
                for g in range(groups):
                    if 3 <= g + 2 < groups:
                        part("gu", g + 2)
                    if g + 1 < groups:
                        part("dn", g)
                    if g + 2 < groups:
                        silu(g + 2)
                    elif g + 2 == groups:
                        part("dn", g + 1)
                    if g + 1 < groups:
                        turned(g + 1)
                    if g + 2 == groups and blocks_ == 1:
                        item_tokens(j + 1)

            swiglu("f", TB, F_GROUPS, f_hi, f_sg, AT["ffn_gu", 0], Q_FFN, 0)
            act.wait_ge(S("quarter_used"), Q_EXP)
            act.activation(cols(xn, 0, D), psum[:, 4 * BANK:6 * BANK], ACT.Copy).then_inc(S("ffn0_y"), 1)
            squares("ffn0p", xn, D, D, hsT, "ffn0_y_all", [1, 1])
            squares("mix1", x, D, D, hsT, "residual", [3, 4])
            modulate("mix1", 16, 48 + A_SHM, hT)
            modulate("mix1", 24, A_KV, hsT)

            W3 = KVLORA + 2 * ROPE
            squares("kvl", ckv, KVLORA, W3, xn, "ckv", [1, 2])
            for k in range(2):
                act.wait_ge(S("ckv_turned"), 1)
                act.activation(cols(ckvT, k * T, T), bank(2, k * T, T), ACT.Copy, scale=cols(vec, V_KVLORA + k)
                               ).then_inc(S("ckvT"), 1)
            squares("ql", cq, QLORA, QLORA, xn, "cq", [1, 2])
            for k in range(3):
                act.wait_ge(S("cq_turned"), 1)
                act.activation(cols(cqT, k * T, T), psum[:, 3 * BANK + k * T:3 * BANK + (k + 1) * T], ACT.Copy,
                               scale=cols(vec, V_QNORM + k)).then_inc(S("cqT"), 1)
            for i in range(8):
                act.wait_ge(S("kq"), i + 1)
                dst = kT if i < 4 else qT
                act.activation(cols(dst, (i % 4) * 2 * T, 2 * T), bank(i % 2), ACT.Copy).then_inc(S("kq_out"), 1)
            for i in range(TB * HEADS):
                act.wait_ge(S("score_max"), i + 1)
                nk = P * (i // HEADS + 1)
                act.activation(cols(sc_, (i % 2) * T, nk), cols(sc_, (i % 2) * T, nk), ACT.Exp, scale=SCALE,
                               bias=cols(smx, 16 + i), accum_out=cols(smx, 32 + i)).then_inc(S("score_exp"), 1)
                act.wait_ge(S("p_turned"), i + 1)
                act.activation(cols(probT, (i % 2) * T, nk), bank(2 + i % 2, 0, nk), ACT.Copy).then_inc(S("pT"), 1)
            act.wait_ge(*tile_done(AT["wo", 1]))
            act.activation(cols(xn, 0, D), psum[:, 4 * BANK:6 * BANK], ACT.Copy).then_inc(S("mix1_y"), 1)
            squares("mix1p", xn, D, D, hsT, "mix1_y_all", [1, 1])
            squares("ffn1", x, D, D, hsT, "residual", [5, 6])
            modulate("ffn1", 32, 48 + A_SHF, hT)
            for b in range(TB):
                act.wait_ge(S("top_gap"), b + 1)
                act.activation(cols(gg, b), cols(gg, b), ACT.Exp).then_inc(S("gap_exp"), 1)

            act.wait_ge(S("items_ready"), 1)
            n_items = act.value_load(reg_i[0:1, 0:1], min_val=EXPERTS, max_val=ITEMS)
            def item_tokens(j):
                act.wait_ge(S("dispatched"), 2 * j + 1)
                for k in range(KD // 2):
                    act.activation(cols(xeT, k * P, P), psum[:, 6 * BANK + k * P:6 * BANK + (k + 1) * P],
                                   ACT.Identity, scale=cols(mcol, 32 + k), bias=cols(adaC, 48 + A_SHF + k)
                                   ).then_inc(S("xe_act"), 1)
                act.wait_ge(S("xe_act"), 4 * j + 4)
                act.activation(xe_hi[:, 0:BANK], cols(xeT, 0, BANK), ACT.Copy).then_inc(S("xe_hi"), 1)
                act.wait_ge(S("xe_dve"), 4 * j + 4)
                act.activation(xe_hi[:, BANK:D], cols(xeT, BANK, BANK), ACT.Copy).then_inc(S("xe_hi"), 1)

            def gated_result(j):
                act.wait_ge(S("quarter_used"), Q_EXP + E_QUARTERS * j)
                act.wait_ge(S("gate_s"), j + 1)
                act.wait_ge(S("xe_lo"), 2 * (j + 1))
                act.activation(ye_hi[:, 0:BANK], bank(4), ACT.Copy, scale=gate_s).then_inc(S("ye_hi"), 1)

            item_tokens(0)
            with act.Fori(0, ITEMS) as j:
                with act.If(j < n_items):
                    act.activation(silu_tab, cols(cact, 0), ACT.Silu)
                    swiglu("e", 1, E_GROUPS, e_hi, e_sg, N0, Q_EXP, j)
                with act.Else():
                    act.nop()
            gated_result(n_items)
            squares("ffn1p", acc, D, D, hsT, "experts_done", [1, 1])

        @block.gpsimd
        def _(pool):
            def phases(k):
                if k >= 1:
                    pool.wait_ge(S("table"), 2 * k)
                step_ = cols(cons, C_STEP, CHUNK).unsqueeze(1).broadcast_to([P, PAIRS_KT, CHUNK])
                pool.tensor_tensor(ph_a.rearrange("p (q t) -> p q t", t=CHUNK),
                                   turns[:, PAIRS_KT * k:PAIRS_KT * (k + 1)].unsqueeze(2)
                                   .broadcast_to([P, PAIRS_KT, CHUNK]), step_, ALU.mult
                                   ).then_inc(S("phase_step"), 1)
                pool.wait_ge(S("phase_step"), 2 * k + 1)
                pool.tensor_scalar(ph_b, ph_a, MAGIC, MAGIC, ALU.add, ALU.subtract).then_inc(S("phase_step"), 1)
                pool.wait_ge(S("phase_step"), 2 * k + 2)
                pool.tensor_tensor(ph_a, ph_a, ph_b, ALU.subtract).then_inc(S("phase"), 1)

            pool.wait_ge(S("theta"), 1)
            phases(0)
            for k in range(KD):
                if k + 1 < KD:
                    phases(k + 1)
                cos, sin = tabs[k % 2]
                pool.wait_ge(S("scan"), 8 * (k + 1))
                if k >= 1:
                    pool.wait_ge(S("y_ssm"), k)
                shape = [P, PAIRS_KT, 2, CHUNK]
                products = ((prods[0], cos, g_re), (prods[1], sin, g_im), (prods[2], cos, g_im),
                            (prods[3], sin, g_re))
                for dst, tab, g in products[2:] if k == KD - 1 else products:
                    pool.tensor_tensor(four(dst), wide(tab, shape), four(g), ALU.mult
                                       ).then_inc(S("rotated"), 1)

            pool.wait_ge(S("items_ready"), 1)
            n_items = pool.value_load(reg_i[0:1, 0:1], min_val=EXPERTS, max_val=ITEMS)

            def item_tokens(j):
                for c in range(2):
                    pool.wait_ge(S("xe_hi"), 2 * j + c + 1)
                    pool.tensor_tensor(xe_lo[:, c * BANK:(c + 1) * BANK], cols(xeT, c * BANK, BANK),
                                       xe_hi[:, c * BANK:(c + 1) * BANK], ALU.subtract).then_inc(S("xe_lo"), 1)

            item_tokens(0)
            with pool.Fori(0, ITEMS) as j:
                with pool.If(j < n_items):
                    item_tokens(j + 1)
                with pool.Else():
                    pool.nop()

        @block.vector
        def _(dve):
            chained = [0]

            def link(ins):
                chained[0] += 1
                ins.then_inc(S("dve_chain"), 1)
                dve.wait_ge(S("dve_chain"), chained[0])

            def mean_root(tag, width):
                k = NORMS[tag]
                dve.wait_ge(S("squares"), k // 2 + 2)
                dve.tensor_scalar(cols(stat, k + 2, 2), cols(stat, k, 2), 1.0 / width, EPS, ALU.mult, ALU.add
                                  ).then_inc(S("mean"), 1)
                dve.wait_ge(S("root"), k // 4 + 1)
                link(dve.reciprocal(cols(stat, k + 2, 2), cols(stat, k, 2)))

            def normed(tag, src, width, step, dst, dstep):
                mean_root(tag, width)
                k = NORMS[tag] + 2
                for b in range(TB):
                    dve.tensor_scalar(cols(dst, b * dstep, width), cols(src, b * step, width),
                                      cols(stat, k + b), None, ALU.mult).then_inc(S("normed"), 1)

            def modulate(turned, scale, shift, dst):
                for k in DVE_SLICES:
                    dve.wait_ge(S("turned"), 4 * TURNED.index(turned) + k // 2 + 1)
                    dve.tensor_scalar(cols(dst, k * T, T), bank(k // 2, (k % 2) * T, T), cols(mcol, scale + k),
                                      cols(adaC, shift + k), ALU.mult, ALU.add).then_inc(S("mod_dve"), 1)

            def ada_cols(t, n, rows, sums_):
                dve.wait_ge(S("ada_turned"), rows)
                dve.wait_ge(S("sum_turned"), sums_)
                link(dve.tensor_tensor(cols(adaC, 4 * t, 4 * (n - t)), bank(5, t * 4, 4 * (n - t)),
                                       cols(vec, V_ADAB + 4 * t, 4 * (n - t)), ALU.add))

            def gains(dst, scale, gain):
                return dve.scalar_tensor_tensor(cols(mcol, dst, KD), cols(adaC, scale, KD), 1.0, cols(vec, gain, KD),
                                                ALU.add, ALU.mult)

            def residual(tag, gate, src):
                mean_root(tag, D)
                k = NORMS[tag] + 2
                dve.wait_ge(S("gates"), RESIDUALS.index(tag) + 1)
                for b in range(TB):
                    link(dve.scalar_tensor_tensor(cols(src, b * D, D), cols(src, b * D, D), cols(stat, k + b),
                                                  psum[:, gate * BANK:(gate + 2) * BANK], ALU.mult, ALU.mult))
                    dve.tensor_tensor(cols(x, b * D, D), cols(x, b * D, D), cols(src, b * D, D), ALU.add
                                      ).then_inc(S("residual"), 1)

            def whole_turns(dst, src, scale):
                link(dve.tensor_scalar(dst, src, scale, MAGIC, ALU.mult, ALU.add))
                link(dve.tensor_scalar(dst, dst, MAGIC, None, ALU.subtract))

            def reduced(ang, whole):
                whole_turns(whole, ang, INV_2PI)
                for part in (PI_1, PI_2, PI_3):
                    link(dve.scalar_tensor_tensor(ang, whole, -part, ang, ALU.mult, ALU.add))

            def cos_phase(dst, turn):
                link(dve.tensor_scalar(dst, turn, 0.25, None, ALU.is_gt))
                return dve.scalar_tensor_tensor(dst, turn, 0.25, dst, ALU.add, ALU.subtract)

            def exact_exp(src, t1, t2, power, rq):
                whole_turns(t1, src, 1.4426950408889634)
                link(dve.scalar_tensor_tensor(t2, t1, -LN2_1, src, ALU.mult, ALU.add))
                link(dve.scalar_tensor_tensor(t2, t1, -LN2_2, t2, ALU.mult, ALU.add))
                link(dve.tensor_scalar(rq, t2, 1.0 / 40320, 1.0 / 5040, ALU.mult, ALU.add))
                for c in (720, 120, 24, 6, 2, 1):
                    link(dve.tensor_tensor(rq, rq, t2, ALU.mult))
                    link(dve.tensor_scalar(rq, rq, 1.0 / c, None, ALU.add))
                link(dve.tensor_tensor(rq, rq, t2, ALU.mult))
                link(dve.tensor_scalar(t1, t1, 127.0, 0.0, ALU.add, ALU.max))
                link(dve.tensor_scalar(t1, t1, 255.0, 8388608.0, ALU.min, ALU.mult))
                link(dve.tensor_copy(pow_i[:, :], t1))
                link(dve.tensor_copy(power, pow_i[:, :].bitcast(FP32)))

            dve.wait_ge(S("cons_loaded"), 16)
            dve.wait_ge(S("vec_loaded"), 16)
            dve.memset(half_pi, float(np.pi / 2)).then_inc(S("half_pi"), 1)
            step, are, aim = (cols(vec, V_STEP + i * PAIRS, PAIRS) for i in range(3))
            exact_exp(step, q[0], q[1], q[2], q[3])
            link(dve.scalar_tensor_tensor(q[0], q[3], 1.0, q[2], ALU.add, ALU.mult))
            link(dve.tensor_tensor(q[6], are, q[0], ALU.mult))
            link(dve.tensor_tensor(q[3], aim, q[0], ALU.mult))
            reduced(q[3], q[1])
            link(dve.tensor_scalar(turns, q[3], INV_2PI, None, ALU.mult))
            dve.tensor_scalar(q[3], q[3], SIN_MAX, -SIN_MAX, ALU.min, ALU.max).then_inc(S("theta"), 1)
            dve.wait_ge(S("theta"), 1)
            dve.wait_ge(S("x_loaded"), 16)
            normed("mix0", x, D, D, xn, D)
            exact_exp(q[6], q[0], q[1], q[2], q[7])
            link(dve.tensor_tensor(q[7], q[7], q[2], ALU.mult))
            link(dve.tensor_tensor(mag, q[7], q[2], ALU.add))
            link(dve.scalar_tensor_tensor(q[7], q[2], -1.0, q[7], ALU.add, ALU.add))
            dve.wait_ge(S("theta_sin"), 2)
            link(dve.tensor_tensor(q[5], q[5], q[5], ALU.mult))
            link(dve.tensor_scalar(q[5], q[5], -2.0, None, ALU.mult))
            link(dve.scalar_tensor_tensor(q[6], q[5], 1.0, q[7], ALU.add, ALU.mult))
            link(dve.tensor_tensor(q[6], q[6], q[5], ALU.add))
            link(dve.tensor_tensor(q[7], mag, q[4], ALU.mult))
            link(dve.tensor_tensor(q[0], are, are, ALU.mult))
            link(dve.tensor_tensor(q[1], aim, aim, ALU.mult))
            link(dve.tensor_tensor(q[0], q[0], q[1], ALU.add))
            link(dve.reciprocal(q[0], q[0]))
            for dst, u1, u2, op in ((cf_re, q[6], q[7], ALU.add), (cf_im, q[7], q[6], ALU.subtract)):
                link(dve.tensor_tensor(q[1], u1, are, ALU.mult))
                link(dve.tensor_tensor(q[2], u2, aim, ALU.mult))
                link(dve.tensor_tensor(q[1], q[1], q[2], op))
                link(dve.tensor_tensor(dst, q[1], q[0], ALU.mult))
            def ada_sum(i, t, dst):
                n = AT["ada", t]
                tile_wait(dve, n)
                link(dve.tensor_scalar(dst, tile(n, 0, BANK), cols(cact, 0), None, ALU.mult))
                for k in range(1, KD):
                    ins = dve.scalar_tensor_tensor(dst, tile(n, k * BANK, BANK), cols(cact, k), dst, ALU.mult, ALU.add)
                    if k + 1 < KD:
                        link(ins)
                ins.then_inc(S("ada_summed"), 1)

            dve.wait_ge(S("cact"), 1)
            ada_sum(0, 3, sums[0])
            ada_cols(0, 4, EARLY_ADA, 1)
            gains(0, A_SCM, V_MIXPRE).then_inc(S("mcol0"), 1)
            dve.wait_ge(S("mcol0"), 1)
            modulate("mix0", 0, A_SHM, hT)

            dve.wait_ge(S("pos_loaded"), 16)
            link(dve.tensor_copy(rp[3], pos_i[:, :]))
            for b in range(TB):
                link(dve.tensor_scalar(cols(rp[0], b * HALF, HALF), cons[:, C_FREQ:C_FREQ + HALF],
                                       cols(rp[3], b), None, ALU.mult))
            reduced(rp[0], rp[2])
            link(dve.tensor_scalar(rp[0], rp[0], INV_2PI, None, ALU.mult))
            link(dve.tensor_scalar(rp[0], rp[0], 0.5, -0.5, ALU.min, ALU.max))
            cos_phase(rp[1], rp[0]).then_inc(S("rope_turns"), 1)
            dve.wait_ge(S("blocks_loaded"), 16)
            pair = lambda ap: ap.rearrange("p (q c) -> p q c", c=32)
            over_pair = lambda ap: ap.unsqueeze(2).broadcast_to([P, PAIRS, 32])
            dve.wait_ge(S("turned"), 4)
            for i, (dst, u1, u2, op) in enumerate(((bb[0], b_re, b_im, ALU.subtract), (bb[1], b_im, b_re, ALU.add))):
                link(dve.tensor_tensor(pair(pq3), pair(u1), over_pair(cf_re), ALU.mult))
                link(dve.tensor_tensor(pair(pq4), pair(u2), over_pair(cf_im), ALU.mult))
                dve.tensor_tensor(dst, pq3, pq4, op).then_inc(S("bb"), 1)
                dve.wait_ge(S("bb"), i + 1)
            for i in range(1, len(sums)):
                if i == len(sums) - 1:
                    dve.wait_ge(S("sum_turned"), 1)
                ada_sum(i, DVE_ADA[i], sums[i])

            dve.wait_ge(*tile_done(AT["w_in", 1]))
            for k in DVE_SLICES:
                dve.tensor_copy(cols(hT, k * T, T), bank(k // 2, (k % 2) * T, T)).then_inc(S("u_dve"), 1)
            dve.wait_ge(S("bb_turned"), 2)
            dve.tensor_copy(bbT[0], psum[:, 4 * BANK:6 * BANK]).then_inc(S("bbT_re"), 1)
            dve.wait_ge(S("rope_tab"), 2)
            shape = [P, PAIRS_KT, 2, CHUNK]

            def skip(k):
                dve.wait_ge(S("y_ssm"), k + 1)
                dve.scalar_tensor_tensor(cols(hT, k * T, T), cols(hT, k * T, T), cols(vec, V_SSMD + k),
                                         bank(4, 0, T), ALU.mult, ALU.add).then_inc(S("y_skip"), 1)

            def slice_sum(t):
                dve.wait_ge(S("sum_turned"), DVE_ADA.index(t))
                ada_sum(DVE_ADA.index(t), t, part_sum)

            for k in range(KD):
                cos, sin = tabs[k % 2]
                v_re, v_im = (psum[:, 0:4 * BANK].rearrange("p (q i c t) -> p q i c t", q=PAIRS_KT, i=2, c=2)[:, :, i]
                              for i in range(2))
                if k >= 1:
                    dve.wait_ge(S("scan"), 8 * k)
                dve.wait_ge(S("v"), k + 1)
                dve.wait_ge(S("table"), 2 * (k + 1))
                for i, (dst, v1, v2, op) in enumerate(((rot[0], v_re, v_im, ALU.add), (rot[2], v_im, v_re,
                                                                                       ALU.subtract))):
                    dve.tensor_tensor(four(dst), wide(cos, shape), v1, ALU.mult).then_inc(S("v_read"), 1)
                    dve.tensor_tensor(four(rot[1]), wide(sin, shape), v2, ALU.mult).then_inc(S("v_read"), 1)
                    dve.wait_ge(S("v_read"), 4 * k + 2 * i + 2)
                    link(dve.tensor_tensor(dst, dst, rot[1], op))
                slice_sum(DVE_ADA_SLICE[k][0])
                if k >= 1:
                    dve.wait_ge(S("rotated"), 4 * k)

                def scan(g, r, j, ch, first):
                    o = j * T + ch * CHUNK
                    i = PAIRS_KT * k + j
                    return dve.tensor_tensor_scan(cols(g, o, CHUNK), cols(mag, i).broadcast_to([P, CHUNK]),
                                                  cols(r, o, CHUNK), first, ALU.mult, ALU.add)
                for j in range(PAIRS_KT):
                    for g, r in ((g_re, rot[0]), (g_im, rot[2])):
                        last = scan(g, r, j, 0, 0.0)
                        last.then_inc(S("dve_chain"), 1)
                        chained[0] += 1
                dve.wait_ge(S("dve_chain"), chained[0])
                ends = [four(g)[:, :, 0, CHUNK - 1] for g in (g_re, g_im)]
                last_t = [t_.rearrange("p (q t) -> p q t", t=CHUNK)[:, :, CHUNK - 1] for t_ in (cos, sin)]
                cc = [cols(carry, i * PAIRS_KT, PAIRS_KT) for i in range(6)]
                for dst, t_, g in ((cc[0], 0, 0), (cc[1], 1, 1), (cc[2], 0, 1), (cc[3], 1, 0)):
                    chained[0] += 1
                    dve.tensor_tensor(dst, last_t[t_], ends[g], ALU.mult).then_inc(S("dve_chain"), 1)
                dve.wait_ge(S("dve_chain"), chained[0])
                link(dve.tensor_tensor(cc[0], cc[0], cc[1], ALU.subtract))
                link(dve.tensor_tensor(cc[2], cc[2], cc[3], ALU.add))
                for j in range(PAIRS_KT):
                    for g, r, c in ((g_re, rot[0], cc[0]), (g_im, rot[2], cc[2])):
                        scan(g, r, j, 1, cols(c, j)).then_inc(S("scan"), 1)
                if k == KD - 1:
                    for i, (tab, g) in enumerate(((cos, g_re), (sin, g_im))):
                        if i == 0:
                            dve.wait_ge(S("scan"), 8 * KD)
                            dve.wait_ge(S("y_ssm"), k)
                        dve.tensor_tensor(four(prods[i]), wide(tab, shape), four(g), ALU.mult
                                          ).then_inc(S("rotated_dve"), 1)
                for t in DVE_ADA_SLICE[k][1:]:
                    slice_sum(t)
                if k >= 1:
                    skip(k - 1)
            def split(q0, n, quarters, j=0, first=0, last=True):
                for i in range(first, quarters):
                    qn = q0 + i
                    dve.wait_ge(S("w_hi"), qn + 1 + j * E_QUARTERS)
                    ins = dve.tensor_tensor(w_lo[qn % 4][:, :], tile(n, i * QUARTER, QUARTER), w_hi[qn % 4][:, :],
                                            ALU.subtract)
                    ins.then_inc(S("w_lo"), 1)
                if last:
                    dve.wait_ge(S("w_lo"), q0 + quarters + j * E_QUARTERS)
                    dve.nop().then_inc(S("tile_used"), 1)

            for k in range(KD):
                if k == KD // 2:
                    skip(KD - 1)
                dve.wait_ge(S("s_hi"), k + 1)
                dve.tensor_tensor(s_lo[:, k * T:(k + 1) * T], cols(hT, k * T, T), s_hi[:, k * T:(k + 1) * T],
                                  ALU.subtract).then_inc(S("s_lo"), 1)
            split(Q_OUT, AT["w_out", 0], 4)
            ada_cols(4, ADA_TILES, ADA_TILES - len(DVE_ADA), len(DVE_ADA))
            for dst, scale, gain in ((8, A_SCF, V_FFNPRE), (16, 48 + A_SCM, V_MIXPRE + 8), (24, A_KV + 8, V_KVNORM),
                                     (32, 48 + A_SCF, V_FFNPRE + 8)):
                gains(dst, scale, gain).then_inc(S("mcols"), 1)
            for i, (g, gain) in enumerate(((A_GM, V_MIXPOST), (A_GF, V_FFNPOST), (48 + A_GM, V_MIXPOST + 8),
                                           (48 + A_GF, V_FFNPOST + 8))):
                dve.tensor_tensor(cols(gcol, i * KD, KD), cols(adaC, g, KD), cols(vec, gain, KD), ALU.mult
                                  ).then_inc(S("mcols"), 1)
            dve.wait_ge(S("mcols"), 8)
            for i in range(4):
                if i < 3:
                    split(Q_OUT + 4 * (i + 1), AT["w_out", i + 1], 4)
                for b in range(TB):
                    dve.wait_ge(S("z_sigmoid"), TB * i + b + 1)
                    dve.tensor_tensor(cols(zz, b * D + i * FG, FG), bank(Z_BANKS[i % 2][b], 0, FG),
                                      cols(f_sg, b * FG, FG), ALU.mult).then_inc(S("z_gated"), 1)
            residual("mix0p", 6, zz)
            dve.wait_ge(S("residual"), 2)
            normed("ffn0", x, D, D, xn, D)
            modulate("ffn0", 8, A_SHF, hT)

            for k in range(KD):
                dve.wait_ge(S("s_hi"), KD + k + 1)
                dve.tensor_tensor(s_lo[:, k * T:(k + 1) * T], cols(hT, k * T, T), s_hi[:, k * T:(k + 1) * T],
                                  ALU.subtract).then_inc(S("s_lo"), 1)

            def swiglu(tag, blocks_, groups, h_, h_hi, h_lo, sg, n0, q0, j):
                wide_ = blocks_ * P

                def part(kind, g, i0=0, i1=4):
                    q1 = q0 + quarters_before(groups, kind, g)
                    if kind == "gu":
                        split(q1, n0 + place(groups, kind, g), i1, j, i0, i1 == 4)
                    else:
                        h = 2 * (g % 2)
                        split(q1 - h, n0 + place(groups, kind, g // 2), h + 2, j, h, g % 2 == 1 or g == groups - 1)

                def product(g):
                    for b in range(blocks_):
                        dve.wait_ge(S(tag + "_silu"), blocks_ * g + b + 1 + j * groups * blocks_)
                        if g >= 2 and b == 0:
                            dve.wait_ge(S(tag + "_turned"), g - 1 + j * groups)
                        i, bk = (b, 2 * (g % 2) + b) if blocks_ == 2 else (g % 2, g % 2)
                        dve.tensor_tensor(cols(h_, ((g % 2) * blocks_ + b) * FG, FG), bank(bk, FG, FG),
                                          cols(sg, i * FG, FG), ALU.mult).then_inc(S(tag + "_h"), 1)

                def turned(g):
                    dve.wait_ge(S(tag + "_hi"), g + 1 + j * groups)
                    o = (g % 2) * 2 * wide_
                    dve.tensor_tensor(h_lo[:, o:o + 2 * wide_], bank(TURN_BANK[blocks_][g % 2], 0, 2 * wide_),
                                      h_hi[:, o:o + 2 * wide_], ALU.subtract).then_inc(S(tag + "_lo"), 1)

                part("gu", 0)
                if blocks_ == 1:
                    gated_result(j)
                    part("gu", 1)
                    add_result(j)
                    turned_places(j)
                    product(0)
                    item_places(j + 1)
                else:
                    part("gu", 1)
                    product(0)
                part("gu", 2, 0, 2)
                product(1)
                turned(0)
                part("gu", 2, 2, 4)
                for g in range(groups):
                    if 3 <= g + 2 < groups:
                        part("gu", g + 2)
                    if g + 1 < groups:
                        part("dn", g)
                    if g + 2 < groups:
                        product(g + 2)
                    elif g + 2 == groups:
                        part("dn", g + 1)
                    if g + 1 < groups:
                        turned(g + 1)
                    if g + 2 == groups and blocks_ == 1:
                        item_tokens(j + 1)

            swiglu("f", TB, F_GROUPS, f_h, f_hi, f_lo, f_sg, AT["ffn_gu", 0], Q_FFN, 0)
            dve.wait_ge(S("quarter_used"), Q_EXP)
            link(dve.tensor_copy(cols(xn, D, D), psum[:, 6 * BANK:8 * BANK]))
            dve.wait_ge(S("ffn0_y"), 1)
            dve.nop().then_inc(S("ffn0_y_all"), 1)
            residual("ffn0p", 0, xn)
            dve.wait_ge(S("residual"), 4)
            normed("mix1", x, D, D, xn, D)
            modulate("mix1", 16, 48 + A_SHM, hT)
            modulate("mix1", 24, A_KV, hsT)

            W3 = KVLORA + 2 * ROPE
            R = KVLORA + ROPE

            def turn(dst1, dst2, x1, x2, b, lead, t1, t2):
                c_, s_ = cols(rope, b * HALF, HALF), cols(rope, 64 + b * HALF, HALF)
                if lead:
                    c_, s_ = (v_.unsqueeze(1).broadcast_to([P, lead, HALF]) for v_ in (c_, s_))
                for dst, u1, u2, f1, f2, op in ((dst1, x1, x2, c_, s_, ALU.subtract), (dst2, x1, x2, s_, c_, ALU.add)):
                    link(dve.tensor_tensor(t1, u1, f1, ALU.mult))
                    link(dve.tensor_tensor(t2, u2, f2, ALU.mult))
                    link(dve.tensor_tensor(dst, t1, t2, op))

            for b in range(TB):
                dve.wait_ge(S("ckr"), b + 1)
                o = b * W3
                link(dve.tensor_copy(cols(ckv, o, KVLORA), bank(b, 0, KVLORA)))
                k1, k2 = o + KVLORA, o + KVLORA + HALF
                turn(cols(ckv, k1, HALF), cols(ckv, k2, HALF), bank(b, KVLORA, HALF), bank(b, KVLORA + HALF, HALF),
                     b, 0, cols(ratmp, 0, HALF), cols(ratmp, HALF, HALF))
                dve.tensor_copy(cols(ckv, o + R, ROPE), cols(ckv, k1, ROPE)).then_inc(S("ckv"), 1)
            normed("kvl", ckv, KVLORA, W3, ckv, W3)
            for b in range(TB):
                dve.wait_ge(S("cq_"), b + 1)
                dve.tensor_copy(cols(cq, b * QLORA, QLORA), bank(b, 0, QLORA)).then_inc(S("cq"), 1)
            dve.wait_ge(S("ckv_turned"), 1)
            dve.tensor_copy(krT, bank(3, 0, T)).then_inc(S("krT"), 1)
            normed("ql", cq, QLORA, QLORA, cq, QLORA)
            for i in range(TB * 2):
                dve.wait_ge(S("v_kv"), i + 1)
                dve.tensor_copy(cols(vv, i * BANK, BANK), bank(4 + i)).then_inc(S("vv"), 1)
            heads = lambda ap, o: ap.rearrange("p (h d) -> p h d", h=HEADS)[:, :, o:o + HALF]
            rt = [cols(xn, i * 256, 256).rearrange("p (h d) -> p h d", h=HEADS) for i in range(2)]
            for b in range(TB):
                dve.wait_ge(S("qr_"), b + 1)
                dst = cols(qr, b * 512, 512)
                turn(heads(dst, 0), heads(dst, HALF), heads(bank(4 + b), 0), heads(bank(4 + b), HALF), b, HEADS,
                     rt[0], rt[1])
                dve.nop().then_inc(S("qr"), 1)
            for b in range(TB):
                dve.wait_ge(S("qr_turned"), b + 1)
                dve.tensor_copy(cols(qrT, b * 512, 512), bank(6 + b)).then_inc(S("qrT"), 1)

            def out_head(i):
                blk, h = divmod(i, HEADS)
                dve.wait_ge(S("o"), i + 1)
                dve.tensor_copy(cols(oT, h * T + blk * P, P), bank(4 + i % 2, 0, P)).then_inc(S("oT"), 1)

            for i in range(TB * HEADS):
                blk = i // HEADS
                nk = P * (blk + 1)
                dve.wait_ge(S("score"), i + 1)
                s_ = cols(sc_, (i % 2) * T, nk)
                if i >= 2:
                    dve.wait_ge(S("p_turned"), i - 1)
                dg = cols(sc_, (i % 2) * T + blk * P, P)
                link(dve.tensor_tensor(dg, bank(i % 2, blk * P, P), cols(cons, C_MASK, P), ALU.add))
                if blk:
                    link(dve.tensor_copy(cols(sc_, (i % 2) * T, P), bank(i % 2, 0, P)))
                link(dve.reduce_max(cols(smx, i), s_, AX.X))
                dve.tensor_scalar(cols(smx, 16 + i), cols(smx, i), -SCALE, None, ALU.mult
                                  ).then_inc(S("score_max"), 1)
                dve.wait_ge(S("score_exp"), i + 1)
                link(dve.reciprocal(cols(smx, 48 + i), cols(smx, 32 + i)))
                dve.tensor_scalar(s_, s_, cols(smx, 48 + i), None, ALU.mult).then_inc(S("probs"), 1)
                if i >= 1:
                    out_head(i - 1)
            out_head(TB * HEADS - 1)
            dve.wait_ge(*tile_done(AT["wo", 1]))
            link(dve.tensor_copy(cols(xn, D, D), psum[:, 6 * BANK:8 * BANK]))
            dve.wait_ge(S("mix1_y"), 1)
            dve.nop().then_inc(S("mix1_y_all"), 1)
            residual("mix1p", 0, xn)
            dve.wait_ge(S("residual"), 6)
            normed("ffn1", x, D, D, xn, D)
            modulate("ffn1", 32, 48 + A_SHF, hT)

            dve.wait_ge(S("logits"), 2)
            link(dve.memset(acc[:, :], 0.0))
            link(dve.memset(ones8, 1.0))
            link(dve.tensor_copy(lg, bank(4, 0, TB * 8)))
            iota8 = cols(iota, 0, 8)
            for b in range(TB):
                o = b * 8
                link(dve.max(cols(mx, o, 8), cols(lg, o, 8)))
                link(dve.max_index(cols(idx8, o, 8), cols(mx, o, 8), cols(lg, o, 8)))
                link(dve.tensor_copy(cols(ixf, o, 8), cols(idx8, o, 8)))
                link(dve.tensor_scalar(cols(oh1, o, 8), iota8, cols(ixf, o), None, ALU.is_equal))
                link(dve.tensor_scalar(cols(oh2, o, 8), iota8, cols(ixf, o + 1), None, ALU.is_equal))
                link(dve.tensor_tensor(cols(msel, o, 8), cols(oh1, o, 8), cols(oh2, o, 8), ALU.add))
                dve.tensor_tensor(cols(gg, b), cols(mx, o + 1), cols(mx, o), ALU.subtract).then_inc(S("top_gap"), 1)
            dve.wait_ge(S("top_gap"), 2)
            dve.nop().then_inc(S("chosen"), 1)
            for b in range(TB):
                o = b * 8
                dve.wait_ge(S("gap_exp"), b + 1)
                link(dve.tensor_scalar(cols(gg, TB + b), cols(gg, b), 1.0, None, ALU.add))
                link(dve.reciprocal(cols(gg, TB + b), cols(gg, TB + b)))
                link(dve.tensor_tensor(cols(gg, 2 * TB + b), cols(gg, TB + b), cols(gg, b), ALU.mult))
                link(dve.tensor_scalar(cols(gsel, o, 8), cols(oh1, o, 8), cols(gg, TB + b), None, ALU.mult))
                link(dve.scalar_tensor_tensor(cols(gsel, o, 8), cols(oh2, o, 8), cols(gg, 2 * TB + b),
                                              cols(gsel, o, 8), ALU.mult, ALU.add))
            dve.wait_ge(S("places"), 1)
            link(dve.tensor_copy(cnt, bank(5, 2 * 8, 8)))
            link(dve.scalar_tensor_tensor(posn, bank(5, 0, TB * 8), 1.0, msel, ALU.add, ALU.mult))
            link(dve.tensor_scalar(over, cnt, float(P), None, ALU.is_gt))
            link(dve.tensor_tensor_scan(incl, ones8, over, 0.0, ALU.mult, ALU.add))
            link(dve.tensor_tensor(rank, incl, over, ALU.subtract))
            link(dve.memset(eid, 0.0))
            link(dve.tensor_scalar(cols(eid, 0), cols(incl, 7), float(EXPERTS), None, ALU.add))
            for r in range(3):
                link(dve.tensor_scalar(cols(sel, r * 8, 8), rank, float(r), None, ALU.is_equal))
                link(dve.tensor_tensor(cols(sel, r * 8, 8), cols(sel, r * 8, 8), over, ALU.mult))
                link(dve.tensor_tensor(tmp8, cols(sel, r * 8, 8), iota8, ALU.mult))
                link(dve.reduce_sum(cols(eid, 1 + r), tmp8, AX.X))
            link(dve.memset(posj, -1.0))
            link(dve.memset(gj, 0.0))
            for b in range(TB):
                o = b * (ITEMS + 1)
                link(dve.tensor_scalar(cols(posj, o, 8), cols(posn, b * 8, 8), -1.0, None, ALU.add))
                link(dve.tensor_copy(cols(gj, o, 8), cols(gsel, b * 8, 8)))
                for r in range(3):
                    link(dve.tensor_tensor(tmp8, cols(sel, r * 8, 8), cols(posn, b * 8, 8), ALU.mult))
                    link(dve.reduce_sum(cols(posj, o + 8 + r), tmp8, AX.X))
                    link(dve.tensor_scalar(cols(posj, o + 8 + r), cols(posj, o + 8 + r), -1.0 - P, None, ALU.add))
                    link(dve.tensor_tensor(tmp8, cols(sel, r * 8, 8), cols(gsel, b * 8, 8), ALU.mult))
                    link(dve.reduce_sum(cols(gj, o + 8 + r), tmp8, AX.X))
            link(dve.tensor_copy(reg_i[:, 0:1], cols(eid, 0)))
            link(dve.tensor_copy(reg_i[:, 8:11], cols(eid, 1, 3)))
            dve.nop().then_inc(S("items_ready"), 1)
            n_items = dve.value_load(reg_i[0:1, 0:1], min_val=EXPERTS, max_val=ITEMS)
            def item_tokens(j):
                dve.wait_ge(S("dispatched"), 2 * j + 2)
                for k in range(KD // 2, KD):
                    dve.tensor_scalar(cols(xeT, k * P, P), psum[:, 6 * BANK + k * P:6 * BANK + (k + 1) * P],
                                      cols(mcol, 32 + k), cols(adaC, 48 + A_SHF + k), ALU.mult, ALU.add
                                      ).then_inc(S("xe_dve"), 1)

            def item_places(j):
                for b in range(TB):
                    col = b * (ITEMS + 1) + j
                    col = slice(col, col + 1) if isinstance(j, int) else bass.ds(col, 1)
                    dve.tensor_scalar(cols(pm, b * P, P), iota, posj[:, col], None, ALU.is_equal
                                      ).then_inc(S("places_of_item"), 1)
                    dve.tensor_copy(cols(gate_t, b), gj[:, col]).then_inc(S("places_of_item"), 1)

            def turned_places(j):
                dve.wait_ge(S("places_turned"), j + 1)
                dve.tensor_copy(pT[:, :], bank(2, 0, T)).then_inc(S("pT_e"), 1)
                dve.tensor_copy(gate_s, bank(3, 0, 1)).then_inc(S("gate_s"), 1)

            def gated_result(j):
                dve.wait_ge(S("quarter_used"), Q_EXP + E_QUARTERS * j)
                dve.wait_ge(S("gate_s"), j + 1)
                dve.wait_ge(S("xe_lo"), 2 * (j + 1))
                dve.tensor_scalar(ye_hi[:, BANK:D], bank(5), gate_s, None, ALU.mult).then_inc(S("ye_hi_dve"), 1)
                dve.wait_ge(S("ye_hi_dve"), j + 1)
                dve.scalar_tensor_tensor(ye_lo[:, BANK:D], bank(5), gate_s, ye_hi[:, BANK:D], ALU.mult,
                                         ALU.subtract).then_inc(S("ye_lo"), 1)
                dve.wait_ge(S("ye_hi"), j + 1)
                dve.scalar_tensor_tensor(ye_lo[:, 0:BANK], bank(4), gate_s, ye_hi[:, 0:BANK], ALU.mult,
                                         ALU.subtract).then_inc(S("ye_lo"), 1)

            def add_result(j):
                for i in range(4):
                    dve.wait_ge(S("combined"), 4 * j + i + 1)
                    dve.tensor_tensor(cols(acc, i * BANK, BANK), cols(acc, i * BANK, BANK), bank(COMB[i]),
                                      ALU.add).then_inc(S("added"), 1)
                dve.wait_ge(S("added"), 4 * (j + 1))

            item_places(0)
            dve.tensor_scalar(pT[:, :], cols(cons, 0, T), 0.0, None, ALU.mult).then_inc(S("pT_e"), 1)
            dve.memset(gate_s, 0.0).then_inc(S("gate_s"), 1)
            item_tokens(0)
            with dve.Fori(0, ITEMS) as j:
                with dve.If(j < n_items):
                    swiglu("e", 1, E_GROUPS, e_h, e_hi, e_lo, e_sg, N0, Q_EXP, j)
                    dve.memset(tmp8, 0.0)
                with dve.Else():
                    dve.nop()
            gated_result(n_items)
            add_result(n_items)
            dve.nop().then_inc(S("experts_done"), 1)
            mean_root("ffn1p", D)
            dve.wait_ge(S("gates"), 4)
            for b in range(TB):
                k = NORMS["ffn1p"] + 2
                link(dve.scalar_tensor_tensor(cols(acc, b * D, D), cols(acc, b * D, D), cols(stat, k + b),
                                              psum[:, 0:2 * BANK], ALU.mult, ALU.mult))
                dve.tensor_tensor(cols(x, b * D, D), cols(x, b * D, D), cols(acc, b * D, D), ALU.add
                                  ).then_inc(S("result"), 1)

        @block.tensor
        def _(pe):
            def turned(tag, src):
                for k in range(KD):
                    for b in range(TB):
                        if k == 0:
                            pe.wait_ge(S("normed"), 2 * NORMED.index(tag) + b + 1)
                        mm = pe.transpose(bank(k // 2, (k % 2) * T + b * P, P), cols(src, b * D + k * P, P), ident)
                    if k % 2:
                        mm.then_inc(S("turned"), 1)

            def ada(i, t):
                n = AT["ada", t]
                if i >= 2:
                    pe.wait_ge(S("ada_row"), i - 1)
                tile_wait(pe, n)
                for k in range(KD):
                    mm = pe.matmul(bank(6 + i % 2, 0, BANK, 0, 1), cols(cact, k), tile(n, k * BANK, BANK),
                                   start=(k == 0), stop=(k == KD - 1))
                mm.then_inc(S("tile_used"), 1)
                if i >= 1 and i != EARLY_ADA:
                    ada_turn(i - 1)

            def ada_turn(i):
                pe.wait_ge(S("ada_row"), i + 1)
                for c in range(4):
                    mm = pe.matmul(bank(5, PE_ROWS[i] * 4 + c, 1), rowbuf[0:1, c * P:(c + 1) * P], ones[0:1, 0:1],
                                   start=True, stop=True)
                mm.then_inc(S("ada_turned"), 1)

            def sum_turn(i, src):
                pe.wait_ge(S("ada_summed"), i + 1)
                for c in range(4):
                    mm = pe.matmul(bank(5, DVE_ADA[i] * 4 + c, 1), cols(src, c * P, P), cols(ones, 0),
                                   start=True, stop=True)
                mm.then_inc(S("sum_turned"), 1)

            def modulated(tag):
                pe.wait_ge(S("mod_act"), 4 * MODULATED.index(tag) + 4)
                pe.wait_ge(S("mod_dve"), 4 * MODULATED.index(tag) + 4)

            def gates(i, b0):
                for k in range(KD):
                    mm = pe.matmul(bank(b0 + k // 4, (k % 4) * P, P), cols(gcol, i * KD + k).broadcast_to([P, P]),
                                   ident, start=True, stop=True)
                mm.then_inc(S("gates"), 1)

            def split_product(dst, hi, lo, qn, o, first, last):
                pe.matmul(dst, hi, w_hi[qn % 4][:, o:o + BANK], start=first, stop=False)
                pe.matmul(dst, lo, w_hi[qn % 4][:, o:o + BANK], start=False, stop=False)
                return pe.matmul(dst, hi, w_lo[qn % 4][:, o:o + BANK], start=False, stop=last)

            def up_product(q0, banks, hi, lo, width, j, parts=None):
                for i in range(4):
                    if parts is not None:
                        pe.wait_ge(S("s_lo"), parts + 2 * i + 2)
                    pe.wait_ge(S("w_lo"), q0 + i + 1 + j * E_QUARTERS)
                    for b, bk in enumerate(banks):
                        for c in range(2):
                            k = 2 * i + c
                            x0 = k * width + b * P
                            mm = split_product(bank(bk), hi[:, x0:x0 + P], lo[:, x0:x0 + P], q0 + i, c * BANK,
                                               k == 0, k == KD - 1)
                    mm.then_inc(S("quarter_used"), 1)

            pe.wait_ge(S("cons_loaded"), 16)
            turned("mix0", xn)
            pe.wait_ge(S("cact"), 1)
            for t in range(EARLY_ADA):
                ada(t, t)
            ada_turn(EARLY_ADA - 1)
            sum_turn(0, sums[0])
            modulated("mix0")
            n = AT["w_in", 0]
            tile_wait(pe, n)
            tile_wait(pe, n + 1)
            for c in range(KD):
                for k in range(KD):
                    mm = pe.matmul(bank(c // 2, (c % 2) * T, T), tile(n + k // 4, (k % 4) * D + c * P, P),
                                   cols(hT, k * T, T), start=(k == 0), stop=(k == KD - 1))
                    if c == KD - 1 and k in (3, 7):
                        mm.then_inc(S("tile_used"), 1)

            pe.wait_ge(S("mcol0"), 1)
            for i in range(2):
                pe.wait_ge(S("bb"), i + 1)
                for k in range(KD):
                    mm = pe.transpose(bank(4 + 2 * i + k // 4, (k % 4) * P, P), cols(bb[i], k * P, P), ident)
                    if k % 4 == 3:
                        mm.then_inc(S("bb_turned"), 1)

            def v(k):
                if k >= 1:
                    pe.wait_ge(S("v_read"), 4 * k)
                for i in range(2):
                    for j in range(PAIRS_KT):
                        r = slice(32 * j, 32 * j + 32)
                        mm = pe.matmul(bank(j, i * T, T),
                                       bbT[i][r, k * P:(k + 1) * P], hT[r, k * T:(k + 1) * T],
                                       start=True, stop=True)
                mm.then_inc(S("v"), 1)

            def y(k):
                pe.wait_ge(S("c_negated"), 2)
                if k >= 1:
                    pe.wait_ge(S("y_skip"), k)
                for j in range(PAIRS_KT):
                    o = (PAIRS_KT * k + j) * 32
                    for i, c in enumerate((c_re, cn_re, c_im, c_im)):
                        if j == 0 and k < KD - 1:
                            pe.wait_ge(S("rotated"), 4 * k + i + 1)
                        elif j == 0:
                            pe.wait_ge(S("rotated_dve" if i < 2 else "rotated"), i + 1 if i < 2 else 4 * k + i - 1)
                        mm = pe.matmul(bank(4, 0, T, 32 * j, 32 * j + 32), cols(c, o, 32),
                                       cols(prods[i], j * T, T), start=(i == 0), stop=(i == 3))
                mm.then_inc(S("y_ssm"), 1)

            pe.wait_ge(S("bbT_re"), 1)
            pe.wait_ge(S("bbT_im"), 1)
            pe.wait_ge(S("u_act"), 4)
            pe.wait_ge(S("u_dve"), 4)
            v(0)
            for i in range(1, len(sums)):
                sum_turn(i, sums[i])
            i = EARLY_ADA
            for k in range(KD):
                if k + 1 < KD:
                    v(k + 1)
                sum_turn(DVE_ADA.index(DVE_ADA_SLICE[k][0]), part_sum)
                for n_, t in enumerate(PE_ADA[k]):
                    ada(i, t)
                    i += 1
                    if n_ == 0:
                        for t in DVE_ADA_SLICE[k][1:]:
                            sum_turn(DVE_ADA.index(t), part_sum)
                y(k)
            ada_turn(i - 1)
            for i in range(4):
                if i == 1:
                    pe.wait_ge(S("mcols"), 8)
                if i >= 2:
                    pe.wait_ge(S("z_gated"), TB * (i - 1))
                up_product(Q_OUT + 4 * i, Z_BANKS[i % 2], s_hi, s_lo, T, 0, 0 if i == 0 else None)
            gates(0, 6)
            turned("ffn0", xn)

            def swiglu(tag, blocks_, groups, x_hi, x_lo, width, h_, h_hi, h_lo, q0, j):
                wide_ = blocks_ * P

                def up(g):
                    if blocks_ == 2 and g >= 2:
                        pe.wait_ge(S(tag + "_lo"), g - 1)
                    elif blocks_ == 1 and g >= 2:
                        pe.wait_ge(S(tag + "_h"), g - 1 + j * groups)
                    up_product(q0 + quarters_before(groups, "gu", g),
                               (2 * (g % 2), 2 * (g % 2) + 1) if blocks_ == 2 else (g % 2,), x_hi, x_lo, width, j,
                               KD if blocks_ == 2 and g == 0 else None)

                def turn(g):
                    pe.wait_ge(S(tag + "_h"), blocks_ * (g + 1 + j * groups))
                    if g >= 2:
                        pe.wait_ge(S(tag + "_lo"), g - 1 + j * groups)
                    if blocks_ == 1 and g == 0:
                        pe.wait_ge(S("gate_s"), j + 2)
                    for i in range(2):
                        for b in range(blocks_):
                            mm = pe.transpose(bank(TURN_BANK[blocks_][g % 2], i * wide_ + b * P, P),
                                              cols(h_, ((g % 2) * blocks_ + b) * FG + i * P, P), ident)
                    mm.then_inc(S(tag + "_turned"), 1)

                def down(g):
                    pe.wait_ge(S(tag + "_lo"), g + 1 + j * groups)
                    for i in range(2):
                        qn = q0 + quarters_before(groups, "dn", g) + i
                        pe.wait_ge(S("w_lo"), qn + 1 + j * E_QUARTERS)
                        for b in range(blocks_):
                            x0 = (g % 2) * 2 * wide_ + i * wide_ + b * P
                            for c in range(2):
                                mm = split_product(bank(4 + 2 * b + c), h_hi[:, x0:x0 + P], h_lo[:, x0:x0 + P], qn,
                                                   c * BANK, g == 0 and i == 0, g == groups - 1 and i == 1)
                        mm.then_inc(S("quarter_used"), 1)

                up(0)
                if blocks_ == 1:
                    combine(j)
                    turn_places(j)
                up(1)
                turn(0)
                if blocks_ == 1:
                    pe.wait_ge(S("added"), 4 * (j + 1))
                for g in range(groups):
                    if g + 2 < groups:
                        up(g + 2)
                    elif g + 2 == groups and blocks_ == 1:
                        dispatch(j + 1)
                    if g + 1 < groups:
                        turn(g + 1)
                    down(g)

            swiglu("f", TB, F_GROUPS, s_hi, s_lo, T, f_h, f_hi, f_lo, Q_FFN, 0)
            gates(1, 0)
            turned("mix1", xn)

            for tag, name, done, width in (("kv", "dkv", "ckr", KVLORA + ROPE), ("mix1", "dq", "cq_", QLORA)):
                src = hsT if tag == "kv" else hT
                n = AT[name, 0]
                modulated("kv")
                if tag == "mix1":
                    pe.wait_ge(S("ckv"), 2)
                tile_wait(pe, n)
                for b in range(TB):
                    for k in range(KD):
                        mm = pe.matmul(bank(b, 0, width), cols(src, k * T + b * P, P), tile(n, k * width, width),
                                       start=(k == 0), stop=(k == KD - 1))
                    mm.then_inc(S(done), 1)
            pe.wait_ge(S("cq"), 2)
            for _ in range(2):
                pe.nop().then_inc(S("tile_used"), 1)
            W3 = KVLORA + 2 * ROPE
            pe.wait_ge(S("normed"), 8)
            for b in range(TB):
                for k in range(2):
                    pe.transpose(bank(2, k * T + b * P, P), cols(ckv, b * W3 + k * P, P), ident)
                mm = pe.transpose(bank(3, b * P, P), cols(ckv, b * W3 + KVLORA, P), ident)
            mm.then_inc(S("ckv_turned"), 1)
            pe.wait_ge(S("normed"), 10)
            pe.wait_ge(S("krT"), 1)
            for b in range(TB):
                for k in range(3):
                    mm = pe.transpose(psum[:, 3 * BANK + k * T + b * P:3 * BANK + k * T + (b + 1) * P],
                                      cols(cq, b * QLORA + k * P, P), ident)
            mm.then_inc(S("cq_turned"), 1)
            for i in range(8):
                key = i < 4
                n = AT["ukv" if key else "uqn", 0]
                width, kk = (2 * D, 2) if key else (D, 3)
                src = ckvT if key else cqT
                if i == 0:
                    tile_wait(pe, n)
                    pe.wait_ge(S("ckvT"), 2)
                if i == 4:
                    nv = AT["ukv", 0]
                    pe.wait_ge(S("cqT"), 3)
                    for b in range(TB):
                        for c in range(2):
                            for k in range(2):
                                mm = pe.matmul(bank(4 + 2 * b + c), cols(ckvT, k * T + b * P, P),
                                               tile(nv, k * 2 * D + D + c * BANK, BANK), start=(k == 0),
                                               stop=(k == 1))
                            mm.then_inc(S("v_kv"), 1)
                    pe.wait_ge(S("vv"), 4)
                    pe.nop().then_inc(S("tile_used"), 1)
                    tile_wait(pe, n)
                if i >= 2:
                    pe.wait_ge(S("kq_out"), i - 1)
                for h in range(2):
                    for k in range(kk):
                        mm = pe.matmul(bank(i % 2, h * T, T), tile(n, k * width + (2 * (i % 4) + h) * P, P),
                                       cols(src, k * T, T), start=(k == 0), stop=(k == kk - 1))
                mm.then_inc(S("kq"), 1)
            pe.wait_ge(S("kq_out"), 8)
            pe.nop().then_inc(S("tile_used"), 1)
            n = AT["uqr", 0]
            tile_wait(pe, n)
            for b in range(TB):
                for k in range(3):
                    mm = pe.matmul(bank(4 + b), cols(cqT, k * T + b * P, P), tile(n, k * 512, 512), start=(k == 0),
                                   stop=(k == 2))
                mm.then_inc(S("qr_"), 1)
            pe.wait_ge(S("qr"), 2)
            pe.nop().then_inc(S("tile_used"), 1)
            for b in range(TB):
                for k in range(4):
                    mm = pe.transpose(bank(6 + b, k * P, P), cols(qr, b * 512 + k * P, P), ident)
                mm.then_inc(S("qr_turned"), 1)
            pe.wait_ge(S("qrT"), 2)

            def scores(i):
                blk, h = divmod(i, HEADS)
                nk = P * (blk + 1)
                if i >= 2:
                    pe.wait_ge(S("score_max"), i - 1)
                pe.matmul(bank(i % 2, 0, nk), cols(qT, h * T + blk * P, P), cols(kT, h * T, nk),
                          start=True, stop=False)
                r = slice(64 * (h % 2), 64 * (h % 2) + 64)
                pe.matmul(bank(i % 2, 0, nk), qrT[r, blk * 512 + (h // 2) * P:blk * 512 + (h // 2 + 1) * P],
                          krT[r, 0:nk], start=False, stop=True).then_inc(S("score"), 1)

            def attend(i):
                blk, h = divmod(i, HEADS)
                pe.wait_ge(S("probs"), i + 1)
                if i >= 2:
                    pe.wait_ge(S("pT"), i - 1)
                for kb in range(blk + 1):
                    mm = pe.transpose(bank(2 + i % 2, kb * P, P), cols(sc_, (i % 2) * T + kb * P, P), ident)
                mm.then_inc(S("p_turned"), 1)
                pe.wait_ge(S("pT"), i + 1)
                if i >= 2:
                    pe.wait_ge(S("oT"), i - 1)
                for kb in range(blk + 1):
                    mm = pe.matmul(bank(4 + i % 2, 0, P), cols(vv, kb * D + h * VD, VD),
                                   cols(probT, (i % 2) * T + kb * P, P), start=(kb == 0), stop=(kb == blk))
                mm.then_inc(S("o"), 1)

            scores(0)
            for i in range(TB * HEADS):
                if i + 1 < TB * HEADS:
                    scores(i + 1)
                attend(i)
            pe.wait_ge(S("oT"), TB * HEADS)
            n = AT["wo", 0]
            tile_wait(pe, n)
            tile_wait(pe, n + 1)
            for b in range(TB):
                for c in range(2):
                    for k in range(KD):
                        mm = pe.matmul(bank(4 + 2 * b + c), cols(oT, k * T + b * P, P),
                                       tile(n + k // 4, (k % 4) * D + c * BANK, BANK),
                                       start=(k == 0), stop=(k == KD - 1))
                        if b == TB - 1 and c == 1 and k in (3, 7):
                            mm.then_inc(S("tile_used"), 1)
            gates(2, 0)
            turned("ffn1", xn)
            modulated("ffn1")
            pe.wait_ge(S("router_loaded"), 16)
            for b in range(TB):
                for k in range(KD):
                    mm = pe.matmul(bank(4, b * 8, 8), cols(hT, k * T + b * P, P), cols(routerW, k * 8, 8),
                                   start=(k == 0), stop=(k == KD - 1))
                mm.then_inc(S("logits"), 1)
            pe.wait_ge(S("chosen"), 1)
            tri = cols(cons, C_TRI, P)
            m0, m1 = cols(msel, 0, 8), cols(msel, 8, 8)
            for dst, parts in ((0, ((tri, m0),)), (8, ((tri, m1), (ones, m0))), (16, ((ones, m0), (ones, m1)))):
                for i, (l, r) in enumerate(parts):
                    mm = pe.matmul(bank(5, dst, 8), l, r, start=(i == 0), stop=(i == len(parts) - 1))
            mm.then_inc(S("places"), 1)

            pe.wait_ge(S("items_ready"), 1)
            n_items = pe.value_load(reg_i[0:1, 0:1], min_val=EXPERTS, max_val=ITEMS)
            def dispatch(j):
                pe.wait_ge(S("places_of_item"), 4 * (j + 1))
                for k in range(KD):
                    for b in range(TB):
                        mm = pe.matmul(psum[:, 6 * BANK + k * P:6 * BANK + (k + 1) * P],
                                       cols(xn, b * D + k * P, P), cols(pm, b * P, P),
                                       start=(b == 0), stop=(b == TB - 1))
                    if k % 4 == 3:
                        mm.then_inc(S("dispatched"), 1)

            def turn_places(j):
                for b in range(TB):
                    pe.transpose(bank(2, b * P, P), cols(pm, b * P, P), ident)
                for b in range(TB):
                    mm = pe.matmul(bank(3, 0, 1), cols(pm, b * P, P), cols(gate_t, b), start=(b == 0),
                                   stop=(b == TB - 1))
                mm.then_inc(S("places_turned"), 1)

            def combine(j):
                pe.wait_ge(S("ye_lo"), 2 * (j + 1))
                pe.wait_ge(S("pT_e"), j + 1)
                for i in range(4):
                    b, c = divmod(i, 2)
                    for part in (ye_hi, ye_lo):
                        mm = pe.matmul(bank(COMB[i]), pT[:, b * P:(b + 1) * P], part[:, c * BANK:(c + 1) * BANK],
                                       start=(part is ye_hi), stop=(part is ye_lo))
                    mm.then_inc(S("combined"), 1)

            dispatch(0)
            with pe.Fori(0, ITEMS) as j:
                with pe.If(j < n_items):
                    pe.wait_ge(S("xe_lo"), 2 * (j + 1))
                    swiglu("e", 1, E_GROUPS, xe_hi, xe_lo, P, e_h, e_hi, e_lo, Q_EXP, j)
                with pe.Else():
                    pe.nop()
            combine(n_items)
            gates(3, 0)


def by_partition(v):
    return np.asarray(v).reshape(-1, P).T


def column_tiles(w, width):
    k, n = w.shape
    return np.ascontiguousarray(w.reshape(k // P, P, n // width, width).transpose(2, 1, 0, 3)).reshape(
        n // width, P, -1)


def row_tiles(w, rows):
    k, n = w.shape
    return np.ascontiguousarray(w.reshape(k // rows, rows // P, P, n).transpose(0, 2, 1, 3)).reshape(k // rows, P, -1)


def paired(w, half):
    k = w.shape[0]
    return np.ascontiguousarray(w.reshape(k, 2, half // FG, FG).transpose(0, 2, 1, 3)).reshape(k, 2 * half)


def lay_out(i):
    i = {k: np.asarray(v) for k, v in i.items()}
    c = np.zeros((P, C_N), np.float32)
    r = np.arange(P)
    c[:, C_ID:C_ID + P] = np.eye(P)
    c[:, C_MASK:C_MASK + P] = np.where(r[None, :] <= r[:, None], 0.0, -1e30)
    c[:, C_TRI:C_TRI + P] = r[:, None] < r[None, :]
    c[:, C_ONES:C_ONES + P] = 1.0
    c[:, C_IOTA:C_IOTA + P] = r[None, :]
    c[:, C_FREQ:C_FREQ + HALF] = (10000.0 ** (-np.arange(0, ROPE, 2, dtype=np.float64) / ROPE)).astype(np.float32)
    c[:, C_STEP:C_STEP + CHUNK] = r[None, :] + 1

    def states(v):
        return v.reshape(PAIRS, P).T

    parts = [by_partition(i[n].reshape(-1)) for n in ("norm_mix_pre", "norm_mix_post", "norm_ffn_pre",
                                                      "norm_ffn_post", "kv_norm", "mla_kv_norm")]
    parts += [by_partition(i["mla_q_norm"][0]), by_partition(i["ssm_d"][0]), by_partition(i["ada_b"].reshape(-1)),
              by_partition(i["kv_ada_b"]), by_partition(i["c"][0]),
              states(np.repeat(i["ssm_log_step"][0][:, None], STATES, 1)), states(i["ssm_a_re"][0]),
              states(i["ssm_a_im"][0])]

    def block_diagonal(v):
        d = np.zeros((2, STATES, PAIRS, 2, GC), np.float32)
        v = v.reshape(PAIRS, 2, STATES, GC)
        for g in range(2):
            d[g, :, :, g, :] = v[:, g].transpose(1, 0, 2)
        return d.reshape(P, PAIRS * 32)

    blocks = [block_diagonal(i["ssm_b_re"][0]), block_diagonal(i["ssm_b_im"][0]),
              block_diagonal(i["ssm_c_re"][0].transpose(0, 2, 1)), block_diagonal(i["ssm_c_im"][0].transpose(0, 2, 1))]
    ukv = i["mla_w_ukv"].reshape(KVLORA, HEADS, 2, P).transpose(0, 2, 1, 3).reshape(KVLORA, 2 * D)
    uq = i["mla_w_uq"][0].reshape(QLORA, HEADS, NOPE + ROPE)
    return {
        "x": i["x"][0],
        "vec": np.ascontiguousarray(np.concatenate(parts, 1)),
        "cons": c,
        "blocks": np.ascontiguousarray(np.concatenate(blocks, 1)),
        "router": row_tiles(i["moe_router"][0], D)[0],
        "pos": np.ascontiguousarray(i["positions"].astype(np.int32).reshape(TB, P).T),
        "ada": column_tiles(np.concatenate([i["ada_w"][0], i["ada_w"][1], i["kv_ada_w"]], 1), BANK),
        "w_in": row_tiles(i["ssm_w_in"][0], 512),
        "w_out": column_tiles(paired(i["ssm_w_out"][0], D), BANK),
        "ffn_gu": column_tiles(paired(i["ffn_w_gu"][0], DFF), BANK),
        "ffn_dn": row_tiles(np.concatenate([i["ffn_w_down"][0], np.zeros((FG, D), np.float32)], 0), 512),
        "dkv": row_tiles(i["mla_w_dkv"], D),
        "dq": row_tiles(i["mla_w_dq"][0], D),
        "ukv": row_tiles(ukv, KVLORA),
        "uqn": row_tiles(np.ascontiguousarray(uq[:, :, :NOPE].reshape(QLORA, D)), QLORA),
        "uqr": row_tiles(np.ascontiguousarray(uq[:, :, NOPE:].reshape(QLORA, 512)), QLORA),
        "wo": row_tiles(i["mla_w_o"][0], 512),
        "e_gu": np.stack([column_tiles(paired(w, EFF), BANK) for w in i["moe_w_gu"][0]]),
        "e_dn": np.stack([row_tiles(w, 512) for w in i["moe_w_down"][0]]),
    }


def kernel(**inputs):
    import concourse.bacc as bacc
    from concourse.bass_utils import run_bass_kernel_spmd

    nc = bacc.Bacc("TRN2", target_bir_lowering=False, num_devices=1)
    arrays = lay_out(inputs)
    aps = {n: nc.dram_tensor("in_" + n, v.shape, mybir.dt.from_np(v.dtype), kind="ExternalInput").ap()
           for n, v in arrays.items()}
    out = nc.dram_tensor("out_x", (T, D), FP32, kind="ExternalOutput").ap()
    build(nc, aps, out)
    r = run_bass_kernel_spmd(nc, [{"in_" + n: v for n, v in arrays.items()}], core_ids=[0])
    return r.results[0]["out_x"].reshape(1, T, D)
```

```python
import concourse.bass as bass
from concourse import mybir
from contextlib import ExitStack
import numpy as np

FP32 = mybir.dt.float32
FP32R = mybir.dt.float32r
I32 = mybir.dt.int32
U32 = mybir.dt.uint32
ALU = mybir.AluOpType
ACT = mybir.ActivationFunctionType
AX = mybir.AxisListType

P = 128
D = 1024
T = 256
TB = T // P
KD = D // P
BANK = 512
WCOLS = 4096
SLOTS = 7
EPS = 1e-6
GROUPS, STATES, GC = 64, 64, 16
PAIRS = GROUPS // 2
PAIRS_KT = PAIRS // KD
CHUNK = 128
WORK = 14000
HEADS, NOPE, ROPE, VD = 8, 128, 64, 128
QLORA, KVLORA = 384, 256
SCALE = float((NOPE + ROPE) ** -0.5)
HALF = ROPE // 2
STEPS = [(0, 0, 4, P), (0, 1, 4, P)] + [(1, h, 2, 2 * P) for h in (0, 1, 4, 5)]
STEP_AT = [sum(st[2] for st in STEPS[:s]) for s in range(len(STEPS) + 1)]
DFF, EXPERTS, EFF = 2816, 8, 3584
FG = 256
F_GROUPS = DFF // FG
E_GROUPS = EFF // FG
SLOTS_E = P
ITEMS = EXPERTS + 3
E_TILES = E_GROUPS + E_GROUPS // 2
QUARTER = WCOLS // 4
Q_OUT = 0
Q_FFN = 4 * 4
Q_EXP = Q_FFN + 4 * 16 + 2
E_QUARTERS = 4 * E_TILES
SPLIT0 = WORK - 8 * QUARTER

C_ID, C_MASK, C_TRI, C_ONES, C_IOTA, C_FREQ = 0, 128, 256, 384, 512, 640
C_STEP = 672
C_N = 800
V_MIXPRE, V_MIXPOST, V_FFNPRE, V_FFNPOST = 0, 16, 32, 48
V_KVNORM, V_KVLORA, V_QNORM, V_SSMD, V_ADAB, V_C = 64, 72, 74, 77, 85, 197
V_STEP, V_ARE, V_AIM = 205, 237, 269
V_N = 301
A_SHM, A_SCM, A_GM, A_SHF, A_SCF, A_GF, A_KV = 0, 8, 16, 24, 32, 40, 96

ADA_TILES = 28
PE_ADA = [[8], [11], [13], [16], [18], [20, 23], [25], [27]]
DVE_ADA_SLICE = [[9, 10], [12], [14, 15], [17], [19], [21, 22], [24], [26]]
DVE_ADA = [3, 4, 5, 6, 7] + [t for ts in DVE_ADA_SLICE for t in ts]
EARLY_ADA = 3
PE_ROWS = [0, 1, 2] + [t for ts in PE_ADA for t in ts]
MAGIC = 12582912.0
TWO_PI = 6.283185
INV_2PI = 0.15915494309189535
PI_1, PI_2, PI_3 = 6.28125, 0.0019340515136718750, 1.2556659146e-06
LN2_1, LN2_2 = 0.693359375, -2.12194440e-4
SIN_MAX = 3.1415925


TURN_BANK = {2: (0, 2), 1: (2, 3)}
Z_BANKS = ((0, 1), (4, 5))
COMB = (6, 7, 4, 5)


def tile_order(groups):
    order = [("gu", 0), ("gu", 1), ("gu", 2)]
    for p in range((groups + 1) // 2):
        order += [("gu", 2 * p + 3)] * (2 * p + 3 < groups) + [("dn", p)] + [("gu", 2 * p + 4)] * (2 * p + 4 < groups)
    return order


def place(groups, kind, i):
    return tile_order(groups).index((kind, i))


def quarters_before(groups, kind, g):
    return 4 * g + 2 * max(g - 2, 0) if kind == "gu" else 4 * min(g + 3, groups) + 2 * g


def four(ap):
    return ap.rearrange("p (q c t) -> p q c t", q=PAIRS_KT, c=2)


def wide(table, shape):
    return table.rearrange("p (q t) -> p q t", q=PAIRS_KT).unsqueeze(2).broadcast_to(shape)


def tile_list():
    tiles = [("ada", i, WCOLS) for i in range(4)]
    tiles += [("w_in", i, WCOLS) for i in range(2)]
    tiles += [("ada", i, WCOLS) for i in range(4, ADA_TILES)]
    tiles += [("w_out", i, WCOLS) for i in range(4)]
    tiles += [("ffn_" + kind, g, WCOLS // (1 + (kind == "dn" and 2 * g + 2 > F_GROUPS)))
              for kind, g in tile_order(F_GROUPS)]
    tiles.append(("dkv", 0, KD * (KVLORA + ROPE)))
    tiles.append(("dq", 0, KD * QLORA))
    tiles.append(("ukv", 0, WCOLS))
    tiles.append(("uqr", 0, 3 * 512))
    tiles.append(("uqn", 0, 3 * D))
    tiles += [("wo", i, WCOLS) for i in range(2)]
    return tiles



def build(nc, a, out):
    ctx = ExitStack()
    sems = {}

    def S(name):
        if name not in sems:
            sems[name] = ctx.enter_context(nc.semaphore(name))
        return sems[name]

    at_byte = {}

    def sb(name, cols, dt=FP32, rows=P):
        at_byte[name] = -(-nc.sbuf_base // 32) * 32
        return ctx.enter_context(nc.sbuf_tensor(name, [rows, cols], dt))

    TILES = tile_list()
    N0 = len(TILES)
    AT = {(w, i): n for n, (w, i, _) in enumerate(TILES)}
    SUMMED = [AT["ada", t] for t in DVE_ADA]

    def tile_done(n):
        if n in SUMMED:
            return S("ada_summed"), SUMMED.index(n) + 1
        return S("tile_used"), n + 1 - sum(m < n for m in SUMMED)

    with ctx:
        ring = sb("ring", SLOTS * WCOLS)
        cons = sb("cons", C_N)
        vec = sb("vec", V_N)
        x = sb("x", TB * D)
        xn = sb("xn", TB * D)
        hT = sb("hT", KD * T)
        hsT = sb("hsT", KD * T)
        adaC = sb("adaC", 112)
        cact = sb("cact", KD)
        rowbuf = sb("rowbuf", BANK, rows=1)
        mcol = sb("mcol", 5 * KD)
        gcol = sb("gcol", 4 * KD)
        stat = sb("stat", 40)
        z_squares = sb("z_squares", 8)
        tab_junk = sb("tab_junk", 16)
        routerW = sb("routerW", KD * EXPERTS)
        pos_i = sb("pos_i", TB, I32)
        rope = sb("rope", 2 * TB * HALF)
        idx8 = sb("idx8", TB * 8, U32)
        reg_i = sb("reg_i", 16, I32)
        pow_i = sb("pow_i", PAIRS, I32)
        work = sb("work", WORK)

        def rounded(name, over, o, n):
            return nc.alloc_sbuf_tensor_at(name, [P, n], FP32R, offset=at_byte[over] + 4 * o)

        w_hi = [rounded(f"w_hi{i}", "work", SPLIT0 + i * QUARTER, QUARTER) for i in range(4)]
        w_lo = [rounded(f"w_lo{i}", "work", SPLIT0 + (4 + i) * QUARTER, QUARTER) for i in range(4)]
        s_hi, s_lo = rounded("s_hi", "xn", 0, KD * T), rounded("s_lo", "hsT", 0, KD * T)
        psum = ctx.enter_context(nc.psum_tensor("psum", [P, 8 * BANK], FP32))

        ident = cons[:, C_ID:C_ID + P]
        ones = cons[:, C_ONES:C_ONES + P]
        iota = cons[:, C_IOTA:C_IOTA + P]

        def bank(b, o=0, n=BANK, p0=0, p1=P):
            return psum[p0:p1, b * BANK + o:b * BANK + o + n]

        class Area:

            def __init__(self):
                self.at = 0

            def take(self, n):
                self.at += n
                assert self.at <= WORK, self.at
                return work[:, self.at - n:self.at]

            def skip(self, n):
                self.at += n
                return self.at - n

        def cols(ap, o, n=1):
            return ap[:, o:o + n]

        m = Area()
        b_re, b_im, c_re, c_im = (m.take(1024) for _ in range(4))
        blocks = work[:, 0:4096]
        pq3, pq4 = m.take(1024), m.take(1024)
        prods = [b_re, b_im, pq3, pq4]
        bbT = [m.take(1024), m.take(1024)]
        g_re, g_im = m.take(1024), m.take(1024)
        ph_a, ph_b = m.take(512), m.take(512)
        tabs = [(m.take(512), m.take(512)) for _ in range(2)]
        turns, mag, cf_re, cf_im = (m.take(PAIRS) for _ in range(4))
        part_sum = m.take(BANK)
        q = [cols(part_sum, i * PAIRS, PAIRS) for i in range(8)]
        half_pi = m.take(1)
        carry = m.take(6 * PAIRS_KT)
        sums = [cols(g_im, 0, BANK), cols(g_im, BANK, BANK), tabs[1][0], tabs[1][1], cols(g_im, 0, BANK)]
        rot = [cols(xn, 0, 1024), cols(xn, 1024, 1024), cols(hsT, 0, 1024)]
        cn_re = cols(hsT, 1024, 1024)
        bb = [cols(hsT, 0, 1024), cols(hsT, 1024, 1024)]
        rp = [cols(g_re, 0, 64), cols(g_re, 64, 64), cols(g_re, 128, 64), cols(g_re, 192, TB)]

        m = Area()
        f_sg = m.take(TB * FG)
        f_h = m.take(2 * TB * FG)
        f_hi, f_lo = (rounded(f"f_{n}", "work", m.skip(4 * T), 4 * T) for n in ("hi", "lo"))
        zz = m.take(TB * D)
        assert m.at <= SPLIT0

        m = Area()
        ckv = m.take(TB * (KVLORA + 2 * ROPE))
        cq = m.take(TB * QLORA)
        ckvT = m.take(2 * T)
        krT = m.take(T)
        cqT = m.take(3 * T)
        kT = m.take(HEADS * T)
        vv = m.take(TB * HEADS * VD)
        qT = m.take(HEADS * T)
        qr = m.take(TB * HEADS * ROPE)
        qrT = m.take(4 * T)
        sc_ = m.take(2 * BANK)
        probT = m.take(2 * BANK)
        ratmp = m.take(256)
        smx = m.take(64)
        oT = hsT

        m = Area()
        e_sg = m.take(2 * FG)
        e_h = m.take(2 * FG)
        e_hi, e_lo = (rounded(f"e_{n}", "work", m.skip(4 * P), 4 * P) for n in ("hi", "lo"))
        xe_hi, xe_lo = (rounded(f"xe_{n}", "work", m.skip(KD * P), KD * P) for n in ("hi", "lo"))
        pm = m.take(TB * P)
        pT = rounded("pT_e", "work", m.skip(T), T)
        gate_t, gate_s = m.take(TB), m.take(1)
        ye_hi, ye_lo = rounded("ye_hi", "hsT", 0, D), rounded("ye_lo", "hsT", D, D)
        acc = hT
        lg = m.take(TB * 8)
        mx = m.take(TB * 8)
        ixf = m.take(TB * 8)
        oh1, oh2, msel, gsel, posn = (m.take(TB * 8) for _ in range(5))
        gg = m.take(3 * TB)
        cnt, over, incl, rank, ones8 = (m.take(8) for _ in range(5))
        sel, tmp24 = m.take(3 * 8), m.take(3 * 8)
        tmp8 = m.take(8)
        posj = m.take(TB * (ITEMS + 1))
        gj = m.take(TB * (ITEMS + 1))
        eid = m.take(8)
        silu_tab = m.take(1)
        assert m.at <= SPLIT0

        block = ctx.enter_context(nc.Block())

        def tile_wait(eng, n):
            eng.wait_ge(S(f"tile_loaded{n % SLOTS}"), 16 * (n // SLOTS + 1))

        def tile(n, o=0, w=WCOLS):
            return ring[:, (n % SLOTS) * WCOLS + o:(n % SLOTS) * WCOLS + o + w]

        NORMS = {"mix0": 0, "mix0p": 4, "ffn0": 8, "ffn0p": 12, "mix1": 16, "kvl": 20, "ql": 24,
                 "mix1p": 28, "ffn1": 32, "ffn1p": 36}
        SQUARED = {"mix0": 1, "ffn0": 2, "ffn0p": 4, "mix1": 5, "kvl": 6, "ql": 7, "mix1p": 9, "ffn1": 10, "ffn1p": 11}
        NORMED = {"mix0": 1, "ffn0": 2, "mix1": 3, "kvl": 5, "ql": 7, "ffn1": 8}
        TURNED = ["mix0", "ffn0", "mix1", "ffn1"]
        MODULATED = ["mix0", "ffn0", "kv", "mix1", "ffn1"]
        RESIDUALS = ["mix0p", "ffn0p", "mix1p", "ffn1p"]

        ACT_SLICES, DVE_SLICES = (0, 1, 4, 5), (2, 3, 6, 7)

        @block.sync
        def _(sp):
            sp.dma_start(vec[:, :], a["vec"]).then_inc(S("vec_loaded"), 16)
            sp.dma_start(cons[:, :], a["cons"]).then_inc(S("cons_loaded"), 16)
            sp.dma_start(x[:, :].rearrange("p (b d) -> p b d", b=TB),
                         a["x"].rearrange("(b p) d -> p b d", p=P)).then_inc(S("x_loaded"), 16)
            for n, (w, i, c) in enumerate(TILES):
                if n >= SLOTS:
                    sp.wait_ge(*tile_done(n - SLOTS))
                sp.dma_start(tile(n, 0, c), a[w][i, :, 0:c]).then_inc(S(f"tile_loaded{n % SLOTS}"), 16)
                if n == AT["w_in", 1]:
                    sp.dma_start(blocks, a["blocks"]).then_inc(S("blocks_loaded"), 16)
                    sp.dma_start(routerW[:, :], a["router"]).then_inc(S("router_loaded"), 16)
                    sp.dma_start(pos_i[:, :], a["pos"]).then_inc(S("pos_loaded"), 16)

            def expert_tiles(j, e):
                for t in range(E_TILES):
                    kind, g = tile_order(E_GROUPS)[t]
                    n = N0 + t
                    sp.wait_ge(S("tile_used"), tile_done(n - SLOTS)[1] + E_TILES * j)
                    src = a["e_gu"][e, g, :, :] if kind == "gu" else a["e_dn"][e, g, :, :]
                    sp.dma_start(tile(n), src).then_inc(S(f"tile_loaded{n % SLOTS}"), 16)

            with sp.Fori(0, EXPERTS) as j:
                expert_tiles(j, j)
            sp.wait_ge(S("items_ready"), 1)
            n_items = sp.value_load(reg_i[0:1, 0:1], min_val=EXPERTS, max_val=ITEMS)
            with sp.Fori(EXPERTS, ITEMS) as j:
                with sp.If(j < n_items):
                    e = sp.value_load(reg_i[0:1, bass.ds(j, 1)], min_val=0, max_val=EXPERTS - 1)
                    expert_tiles(j, e)
                with sp.Else():
                    sp.nop()
            for b in range(TB):
                sp.wait_ge(S("result"), b + 1)
                sp.dma_start(out[b * P:(b + 1) * P, :], x[:, b * D:(b + 1) * D]).then_inc(S("stored"), 16)
            sp.wait_ge(S("stored"), 16 * TB)

        @block.scalar
        def _(act):
            def root(tag):
                k = NORMS[tag]
                act.wait_ge(S("mean"), k // 4 + 1)
                act.activation(cols(stat, k, 2), cols(stat, k + 2, 2), ACT.Sqrt).then_inc(S("root"), 1)

            def squares(tag, src, junk, wait, n, src1=None):
                k = NORMS[tag]
                act.activation(cols(tab_junk, k // 4), cols(ones, 0), ACT.Sqrt)
                act.wait_ge(S(wait) if isinstance(wait, str) else wait, n)
                act.activation(junk, src, ACT.Square, accum_out=cols(stat, k)).then_inc(S("squares"), 1)
                if src1 is not None:
                    act.activation(cols(hsT, D, D), src1, ACT.Square, accum_out=cols(stat, k + 1)
                                   ).then_inc(S("squares"), 1)
                root(tag)

            def normed(tag):
                k = NORMS[tag] + 2
                act.wait_ge(S("rstd"), k // 4 + 1)
                act.activation(cols(xn, D, D), cols(x, D, D), ACT.Copy, scale=cols(stat, k + 1)
                               ).then_inc(S("normed_act"), 1)

            def modulate(turned, scale, shift, dst):
                for k in ACT_SLICES:
                    act.wait_ge(S("turned"), 4 * TURNED.index(turned) + k // 2 + 1)
                    act.activation(cols(dst, k * T, T), bank(k // 2, (k % 2) * T, T), ACT.Identity,
                                   scale=cols(mcol, scale + k), bias=cols(adaC, shift + k)
                                   ).then_inc(S("mod_act"), 1)

            def ada_row(i, t):
                act.wait_ge(*tile_done(AT["ada", t]))
                if i >= 1:
                    act.wait_ge(S("ada_turned"), i)
                act.activation(rowbuf[0:1, :], bank(6 + i % 2, 0, BANK, 0, 1), ACT.Copy).then_inc(S("ada_row"), 1)

            act.wait_ge(S("vec_loaded"), 16)
            act.activation(cact[:, :], cols(vec, V_C, KD), ACT.Silu).then_inc(S("cact"), 1)
            act.wait_ge(S("cons_loaded"), 16)
            squares("mix0", cols(x, 0, D), cols(xn, 0, D), "x_loaded", 16)
            normed("mix0")
            act.wait_ge(S("theta"), 1)
            act.activation(q[4], q[3], ACT.Sin).then_inc(S("theta_sin"), 1)
            act.activation(q[5], q[3], ACT.Sin, scale=0.5).then_inc(S("theta_sin"), 1)
            for t in range(EARLY_ADA):
                ada_row(t, t)
            act.wait_ge(S("mcol0"), 1)
            modulate("mix0", 0, A_SHM, hT)
            act.wait_ge(S("rope_turns"), 1)
            act.activation(cols(rope, 64, 64), rp[0], ACT.Sin, scale=TWO_PI).then_inc(S("rope_tab"), 1)
            act.activation(cols(rope, 0, 64), rp[1], ACT.Sin, scale=TWO_PI).then_inc(S("rope_tab"), 1)

            def tables(k):
                cos, sin = tabs[k % 2]
                act.wait_ge(S("phase"), k + 1)
                if k == 1:
                    act.wait_ge(S("sum_turned"), len(sums))
                if k >= 2:
                    act.wait_ge(S("v_read"), 4 * (k - 1))
                    act.wait_ge(S("rotated"), 4 * (k - 1))
                act.activation(sin, ph_a, ACT.Sin, scale=TWO_PI).then_inc(S("table"), 1)
                act.activation(ph_b, ph_a, ACT.Abs).then_inc(S("phase_abs"), 1)
                act.wait_ge(S("phase_abs"), k + 1)
                act.activation(cos, ph_b, ACT.Sin, scale=-TWO_PI, bias=half_pi).then_inc(S("table"), 1)

            tables(0)
            act.wait_ge(S("blocks_loaded"), 16)
            act.activation(c_im, c_im, ACT.Copy, scale=-1.0).then_inc(S("c_negated"), 1)
            act.wait_ge(*tile_done(AT["w_in", 1]))
            for k in ACT_SLICES:
                act.activation(cols(hT, k * T, T), bank(k // 2, (k % 2) * T, T), ACT.Copy).then_inc(S("u_act"), 1)
            act.wait_ge(S("bb_turned"), 4)
            act.activation(bbT[1], psum[:, 6 * BANK:8 * BANK], ACT.Copy).then_inc(S("bbT_im"), 1)
            act.activation(cn_re, c_re, ACT.Copy, scale=-1.0).then_inc(S("c_negated"), 1)
            i = EARLY_ADA
            for k in range(KD):
                if k + 1 < KD:
                    tables(k + 1)
                for t in PE_ADA[k]:
                    ada_row(i, t)
                    i += 1
            for k in range(KD):
                act.wait_ge(S("y_skip"), k + 1)
                act.activation(cols(hT, k * T, T), cols(hT, k * T, T), ACT.Gelu_apprx_tanh
                               ).then_inc(S("y_gelu"), 1)
                if k == KD - 2:
                    act.wait_ge(S("scan"), 8 * KD)
                for k_ in range(KD - 1) if k == KD - 2 else [k] if k == KD - 1 else []:
                    act.wait_ge(S("y_gelu"), k_ + 1)
                    act.activation(s_hi[:, k_ * T:(k_ + 1) * T], cols(hT, k_ * T, T), ACT.Copy
                                   ).then_inc(S("s_hi"), 1)

            def split(q0, n, quarters, j=0, first=0):
                for i in range(first, quarters):
                    qn = q0 + i
                    if i == first:
                        act.wait_ge(S(f"tile_loaded{n % SLOTS}"), 16 * (n // SLOTS + 1) + j * 16 * (E_TILES // SLOTS))
                    if qn >= 4:
                        act.wait_ge(S("quarter_used"), qn - 3 + j * E_QUARTERS)
                    act.activation(w_hi[qn % 4][:, :], tile(n, i * QUARTER, QUARTER), ACT.Copy
                                   ).then_inc(S("w_hi"), 1)

            split(Q_OUT, AT["w_out", 0], 4)
            for i in range(4):
                if i < 3:
                    split(Q_OUT + 4 * (i + 1), AT["w_out", i + 1], 4)
                act.wait_ge(S("quarter_used"), Q_OUT + 4 * (i + 1))
                for b in range(TB):
                    if i >= 1:
                        act.wait_ge(S("z_gated"), TB * (i - 1) + b + 1)
                    act.activation(cols(f_sg, b * FG, FG), bank(Z_BANKS[i % 2][b], FG, FG), ACT.Sigmoid
                                   ).then_inc(S("z_sigmoid"), 1)
                for b in range(TB if i >= 1 else 0):
                    act.wait_ge(S("z_gated"), TB * (i - 1) + b + 1)
                    if i >= 2:
                        act.wait_ge(S("z_squares"), TB * (i - 2) + b + 1)
                    act.activation(cols(f_h, b * FG, FG), cols(zz, b * D + (i - 1) * FG, FG), ACT.Square,
                                   accum_out=cols(z_squares, 4 * b + i - 1)).then_inc(S("z_squares"), 1)
            act.activation(cols(tab_junk, 10), cols(ones, 0), ACT.Sqrt)
            root("mix0p")
            split(Q_FFN, AT["ffn_gu", 0], 4)
            squares("ffn0", cols(x, 0, D), cols(hsT, 0, D), "residual_pool", 1)
            normed("ffn0")
            act.wait_ge(S("gates"), 2)
            act.activation(cols(zz, 0, D), psum[:, 4 * BANK:6 * BANK], ACT.Copy).then_inc(S("gate_row"), 1)
            modulate("ffn0", 8, A_SHF, hT)
            for k in range(KD):
                if k in ACT_SLICES:
                    act.wait_ge(S("mod_act"), 4 + ACT_SLICES.index(k) + 1)
                else:
                    act.wait_ge(S("mod_dve"), 4 + DVE_SLICES.index(k) + 1)
                act.wait_ge(S("turned"), 8)
                act.activation(s_hi[:, k * T:(k + 1) * T], cols(hT, k * T, T), ACT.Copy).then_inc(S("s_hi"), 1)

            def swiglu(tag, blocks_, groups, h_hi, sg, n0, q0, j):
                wide = blocks_ * P

                def used(kind, g):
                    return q0 + quarters_before(groups, kind, g) + (4 if kind == "gu" else 2) + j * E_QUARTERS

                def part(kind, g, i0=0, i1=4):
                    q1 = q0 + quarters_before(groups, kind, g)
                    if kind == "gu":
                        split(q1, n0 + place(groups, kind, g), i1, j, i0)
                    else:
                        h = 2 * (g % 2)
                        split(q1 - h, n0 + place(groups, kind, g // 2), h + 2, j, h)

                def silu(g):
                    act.wait_ge(S("quarter_used"), used("gu", g))
                    for b in range(blocks_):
                        if blocks_ == 2:
                            if g >= 1:
                                act.wait_ge(S(tag + "_h"), 2 * g - 1 + b)
                            src, dst = bank(2 * (g % 2) + b, 0, FG), cols(sg, b * FG, FG)
                        else:
                            if g >= 2:
                                act.wait_ge(S(tag + "_h"), g - 1 + j * groups)
                            src, dst = bank(g % 2, 0, FG), cols(sg, (g % 2) * FG, FG)
                        act.activation(dst, src, ACT.Silu).then_inc(S(tag + "_silu"), 1)

                def turned(g):
                    act.wait_ge(S(tag + "_turned"), g + 1 + j * groups)
                    if g >= 2:
                        act.wait_ge(S("quarter_used"), used("dn", g - 2))
                    act.activation(h_hi[:, (g % 2) * 2 * wide:(g % 2 + 1) * 2 * wide],
                                   bank(TURN_BANK[blocks_][g % 2], 0, 2 * wide),
                                   ACT.Copy).then_inc(S(tag + "_hi"), 1)

                if blocks_ == 1:
                    part("gu", 0)
                    gated_result(j)
                part("gu", 1)
                silu(0)
                part("gu", 2, 0, 2)
                silu(1)
                turned(0)
                part("gu", 2, 2, 4)
                for g in range(groups):
                    if 3 <= g + 2 < groups:
                        part("gu", g + 2)
                    if g + 1 < groups:
                        part("dn", g)
                    if g + 2 < groups:
                        silu(g + 2)
                    elif g + 2 == groups:
                        part("dn", g + 1)
                    if g + 1 < groups:
                        turned(g + 1)
                    if g + 2 == groups and blocks_ == 1:
                        item_tokens(j + 1)

            swiglu("f", TB, F_GROUPS, f_hi, f_sg, AT["ffn_gu", 0], Q_FFN, 0)
            squares("ffn0p", psum[:, 4 * BANK:6 * BANK], cols(hsT, 0, D), "quarter_used", Q_EXP,
                    psum[:, 6 * BANK:8 * BANK])
            squares("mix1", cols(x, 0, D), cols(xn, 0, D), "residual_pool", 2)
            normed("mix1")
            modulate("mix1", 24, A_KV, hsT)
            modulate("mix1", 16, 48 + A_SHM, hT)

            W3 = KVLORA + 2 * ROPE
            squares("kvl", cols(ckv, 0, KVLORA), cols(xn, 0, KVLORA), "ckv", 1)
            squares("ql", cols(cq, 0, QLORA), cols(xn, 0, QLORA), "cq", 1)
            for k in range(2):
                act.wait_ge(S("ckv_turned"), 1)
                act.activation(cols(ckvT, k * T, T), bank(2, k * T, T), ACT.Copy, scale=cols(vec, V_KVLORA + k)
                               ).then_inc(S("ckvT"), 1)

            def key_or_query(i):
                act.wait_ge(S("kq"), i + 1)
                dst = kT if i < 4 else qT
                act.activation(cols(dst, (i % 4) * 2 * T, 2 * T), bank(i % 2), ACT.Copy).then_inc(S("kq_out"), 1)

            for i in range(4):
                key_or_query(i)
            for k in range(3):
                act.wait_ge(S("cq_turned"), 1)
                act.activation(cols(cqT, k * T, T), psum[:, 2 * BANK + k * T:2 * BANK + (k + 1) * T], ACT.Copy,
                               scale=cols(vec, V_QNORM + k)).then_inc(S("cqT"), 1)
            for i in range(4, 8):
                key_or_query(i)
            def exps(s):
                blk, h0, n, nk = STEPS[s]
                act.wait_ge(S("score_max"), s + 1)
                for h in range(n):
                    sc = cols(sc_, (s % 2) * BANK + h * nk, nk)
                    i = STEP_AT[s] + h
                    act.activation(sc, sc, ACT.Exp, scale=SCALE, bias=cols(smx, 16 + i), accum_out=cols(smx, 32 + i)
                                   ).then_inc(S("score_exp"), 1)

            exps(0)
            act.wait_ge(S("gates"), 3)
            act.activation(cols(xn, D, D), psum[:, 6 * BANK:8 * BANK], ACT.Copy).then_inc(S("gate_row"), 1)
            for s in range(len(STEPS)):
                if s + 1 < len(STEPS):
                    exps(s + 1)
                act.wait_ge(S("p_turned"), s + 1)
                if s >= 2:
                    act.wait_ge(S("o"), s - 1)
                act.activation(cols(probT, (s % 2) * BANK, BANK), bank(2 + s % 2), ACT.Copy).then_inc(S("pT"), 1)
            squares("mix1p", psum[:, 4 * BANK:6 * BANK], cols(hsT, 0, D), *tile_done(AT["wo", 1]),
                    psum[:, 6 * BANK:8 * BANK])
            squares("ffn1", cols(x, 0, D), cols(xn, 0, D), "residual_pool", 3)
            normed("ffn1")
            modulate("ffn1", 32, 48 + A_SHF, hT)
            act.wait_ge(S("top_gap"), 1)
            act.activation(cols(gg, 0, TB), cols(gg, 0, TB), ACT.Exp).then_inc(S("gap_exp"), 1)

            def item_tokens(j):
                for c in range(2):
                    act.wait_ge(S("dispatched"), 2 * j + c + 1)
                    act.activation(xe_hi[:, c * BANK:(c + 1) * BANK], bank(6 + c), ACT.Copy).then_inc(S("xe_hi"), 1)

            def gated_result(j):
                act.wait_ge(S("quarter_used"), Q_EXP + E_QUARTERS * j)
                act.wait_ge(S("gate_s"), j + 1)
                act.activation(ye_hi[:, 0:BANK], bank(4), ACT.Copy, scale=gate_s).then_inc(S("ye_hi"), 1)

            item_tokens(0)
            act.wait_ge(S("items_ready"), 1)
            n_items = act.value_load(reg_i[0:1, 0:1], min_val=EXPERTS, max_val=ITEMS)
            with act.Fori(0, ITEMS) as j:
                with act.If(j < n_items):
                    act.activation(silu_tab, cols(cact, 0), ACT.Silu)
                    swiglu("e", 1, E_GROUPS, e_hi, e_sg, N0, Q_EXP, j)
                with act.Else():
                    act.nop()
            gated_result(n_items)
            squares("ffn1p", cols(acc, 0, D), cols(hsT, 0, D), "experts_done", 1)

        @block.gpsimd
        def _(pool):
            def phases(k):
                if k >= 1:
                    pool.wait_ge(S("table"), 2 * k)
                step_ = cols(cons, C_STEP, CHUNK).unsqueeze(1).broadcast_to([P, PAIRS_KT, CHUNK])
                pool.tensor_tensor(ph_a.rearrange("p (q t) -> p q t", t=CHUNK),
                                   turns[:, PAIRS_KT * k:PAIRS_KT * (k + 1)].unsqueeze(2)
                                   .broadcast_to([P, PAIRS_KT, CHUNK]), step_, ALU.mult
                                   ).then_inc(S("phase_step"), 1)
                pool.wait_ge(S("phase_step"), 2 * k + 1)
                pool.tensor_scalar(ph_b, ph_a, MAGIC, MAGIC, ALU.add, ALU.subtract).then_inc(S("phase_step"), 1)
                pool.wait_ge(S("phase_step"), 2 * k + 2)
                pool.tensor_tensor(ph_a, ph_a, ph_b, ALU.subtract).then_inc(S("phase"), 1)

            pool.wait_ge(S("theta"), 1)
            phases(0)
            for k in range(KD):
                if k + 1 < KD:
                    phases(k + 1)
                cos, sin = tabs[k % 2]
                pool.wait_ge(S("scan"), 8 * (k + 1))
                if k >= 1:
                    pool.wait_ge(S("y_ssm"), k)
                shape = [P, PAIRS_KT, 2, CHUNK]
                products = ((prods[0], cos, g_re), (prods[1], sin, g_im), (prods[2], cos, g_im),
                            (prods[3], sin, g_re))
                for dst, tab, g in products[2:] if k == KD - 1 else products:
                    pool.tensor_tensor(four(dst), wide(tab, shape), four(g), ALU.mult
                                       ).then_inc(S("rotated"), 1)

            for i in range(3):
                pool.wait_ge(S("scaled"), i + 1)
                src = (zz, hsT, hsT)[i]
                pool.tensor_tensor(cols(x, 0, D), cols(x, 0, D), cols(src, 0, D), ALU.add
                                   ).then_inc(S("residual_pool"), 1)
            pool.wait_ge(S("logits"), 2)
            pool.memset(acc[:, :], 0.0).then_inc(S("acc_zeroed"), 1)

            pool.wait_ge(S("items_ready"), 1)
            n_items = pool.value_load(reg_i[0:1, 0:1], min_val=EXPERTS, max_val=ITEMS)

            with pool.Fori(0, ITEMS) as j:
                with pool.If(j < n_items):
                    for i in range(2, 4):
                        qn = Q_EXP + 4 + i
                        pool.wait_ge(S("w_hi"), qn + 1 + j * E_QUARTERS)
                        pool.tensor_tensor(w_lo[qn % 4][:, :], tile(N0 + 1, i * QUARTER, QUARTER), w_hi[qn % 4][:, :],
                                           ALU.subtract).then_inc(S("w_lo_pool"), 1)
                with pool.Else():
                    pool.nop()

        @block.vector
        def _(dve):
            chained = [0]

            def link(ins):
                chained[0] += 1
                ins.then_inc(S("dve_chain"), 1)
                dve.wait_ge(S("dve_chain"), chained[0])

            def mean_root(tag, width, src=None, junk=None):
                k = NORMS[tag]
                if src is not None:
                    link(dve.scalar_tensor_tensor(junk, src, 1.0, src, ALU.mult, ALU.mult,
                                                  accum_out=cols(stat, k + 1)))
                if tag in SQUARED:
                    dve.wait_ge(S("squares"), SQUARED[tag])
                dve.tensor_scalar(cols(stat, k + 2, 2), cols(stat, k, 2), 1.0 / width, EPS, ALU.mult, ALU.add
                                  ).then_inc(S("mean"), 1)
                dve.wait_ge(S("root"), k // 4 + 1)
                dve.reciprocal(cols(stat, k + 2, 2), cols(stat, k, 2)).then_inc(S("rstd"), 1)
                dve.wait_ge(S("rstd"), k // 4 + 1)

            def normed(tag):
                mean_root(tag, D, cols(x, D, D), cols(xn, D, D))
                dve.tensor_scalar(cols(xn, 0, D), cols(x, 0, D), cols(stat, NORMS[tag] + 2), None, ALU.mult
                                  ).then_inc(S("normed"), 1)

            def latent_normed(tag, src, width, step):
                mean_root(tag, width, cols(src, step, width), cols(xn, 512, width))
                for b in range(TB):
                    dve.tensor_scalar(cols(src, b * step, width), cols(src, b * step, width),
                                      cols(stat, NORMS[tag] + 2 + b), None, ALU.mult).then_inc(S("normed"), 1)

            def modulate(turned, scale, shift, dst):
                for k in DVE_SLICES:
                    dve.wait_ge(S("turned"), 4 * TURNED.index(turned) + k // 2 + 1)
                    dve.tensor_scalar(cols(dst, k * T, T), bank(k // 2, (k % 2) * T, T), cols(mcol, scale + k),
                                      cols(adaC, shift + k), ALU.mult, ALU.add).then_inc(S("mod_dve"), 1)

            def ada_cols(t, n, rows, sums_):
                dve.wait_ge(S("ada_turned"), rows)
                dve.wait_ge(S("sum_turned"), sums_)
                link(dve.tensor_tensor(cols(adaC, 4 * t, 4 * (n - t)), bank(5, t * 4, 4 * (n - t)),
                                       cols(vec, V_ADAB + 4 * t, 4 * (n - t)), ALU.add))

            def gains(dst, scale, gain):
                return dve.scalar_tensor_tensor(cols(mcol, dst, KD), cols(adaC, scale, KD), 1.0, cols(vec, gain, KD),
                                                ALU.add, ALU.mult)

            def residual(tag, src, gate, dst):
                k = NORMS[tag] + 2
                for b in range(TB):
                    ins = dve.scalar_tensor_tensor(cols(dst, b * D, D), src[b], cols(stat, k + b), gate,
                                                   ALU.mult, ALU.mult)
                    ins.then_inc(S("scaled" if b == 0 else "scaled_1"), 1)
                dve.wait_ge(S("scaled_1"), RESIDUALS.index(tag) + 1)
                link(dve.tensor_tensor(cols(x, D, D), cols(x, D, D), cols(dst, D, D), ALU.add))

            def whole_turns(dst, src, scale):
                link(dve.tensor_scalar(dst, src, scale, MAGIC, ALU.mult, ALU.add))
                link(dve.tensor_scalar(dst, dst, MAGIC, None, ALU.subtract))

            def reduced(ang, whole):
                whole_turns(whole, ang, INV_2PI)
                for part in (PI_1, PI_2, PI_3):
                    link(dve.scalar_tensor_tensor(ang, whole, -part, ang, ALU.mult, ALU.add))

            def cos_phase(dst, turn):
                link(dve.tensor_scalar(dst, turn, 0.25, None, ALU.is_gt))
                return dve.scalar_tensor_tensor(dst, turn, 0.25, dst, ALU.add, ALU.subtract)

            def exact_exp(src, t1, t2, power, rq):
                whole_turns(t1, src, 1.4426950408889634)
                link(dve.scalar_tensor_tensor(t2, t1, -LN2_1, src, ALU.mult, ALU.add))
                link(dve.scalar_tensor_tensor(t2, t1, -LN2_2, t2, ALU.mult, ALU.add))
                link(dve.tensor_scalar(rq, t2, 1.0 / 40320, 1.0 / 5040, ALU.mult, ALU.add))
                for c in (720, 120, 24, 6, 2, 1):
                    link(dve.tensor_tensor(rq, rq, t2, ALU.mult))
                    link(dve.tensor_scalar(rq, rq, 1.0 / c, None, ALU.add))
                link(dve.tensor_tensor(rq, rq, t2, ALU.mult))
                link(dve.tensor_scalar(t1, t1, 127.0, 0.0, ALU.add, ALU.max))
                link(dve.tensor_scalar(t1, t1, 255.0, 8388608.0, ALU.min, ALU.mult))
                link(dve.tensor_copy(pow_i[:, :], t1))
                link(dve.tensor_copy(power, pow_i[:, :].bitcast(FP32)))

            dve.wait_ge(S("cons_loaded"), 16)
            dve.wait_ge(S("vec_loaded"), 16)
            dve.memset(half_pi, float(np.pi / 2)).then_inc(S("half_pi"), 1)
            step, are, aim = (cols(vec, V_STEP + i * PAIRS, PAIRS) for i in range(3))
            exact_exp(step, q[0], q[1], q[2], q[3])
            link(dve.scalar_tensor_tensor(q[0], q[3], 1.0, q[2], ALU.add, ALU.mult))
            link(dve.tensor_tensor(q[6], are, q[0], ALU.mult))
            link(dve.tensor_tensor(q[3], aim, q[0], ALU.mult))
            reduced(q[3], q[1])
            link(dve.tensor_scalar(turns, q[3], INV_2PI, None, ALU.mult))
            dve.tensor_scalar(q[3], q[3], SIN_MAX, -SIN_MAX, ALU.min, ALU.max).then_inc(S("theta"), 1)
            dve.wait_ge(S("theta"), 1)
            dve.wait_ge(S("x_loaded"), 16)
            normed("mix0")
            exact_exp(q[6], q[0], q[1], q[2], q[7])
            link(dve.tensor_tensor(q[7], q[7], q[2], ALU.mult))
            link(dve.tensor_tensor(mag, q[7], q[2], ALU.add))
            link(dve.scalar_tensor_tensor(q[7], q[2], -1.0, q[7], ALU.add, ALU.add))
            dve.wait_ge(S("theta_sin"), 2)
            link(dve.tensor_tensor(q[5], q[5], q[5], ALU.mult))
            link(dve.tensor_scalar(q[5], q[5], -2.0, None, ALU.mult))
            link(dve.scalar_tensor_tensor(q[6], q[5], 1.0, q[7], ALU.add, ALU.mult))
            link(dve.tensor_tensor(q[6], q[6], q[5], ALU.add))
            link(dve.tensor_tensor(q[7], mag, q[4], ALU.mult))
            link(dve.tensor_tensor(q[0], are, are, ALU.mult))
            link(dve.tensor_tensor(q[1], aim, aim, ALU.mult))
            link(dve.tensor_tensor(q[0], q[0], q[1], ALU.add))
            link(dve.reciprocal(q[0], q[0]))
            for dst, u1, u2, op in ((cf_re, q[6], q[7], ALU.add), (cf_im, q[7], q[6], ALU.subtract)):
                link(dve.tensor_tensor(q[1], u1, are, ALU.mult))
                link(dve.tensor_tensor(q[2], u2, aim, ALU.mult))
                link(dve.tensor_tensor(q[1], q[1], q[2], op))
                link(dve.tensor_tensor(dst, q[1], q[0], ALU.mult))
            def ada_sum(i, t, dst):
                n = AT["ada", t]
                tile_wait(dve, n)
                link(dve.tensor_scalar(dst, tile(n, 0, BANK), cols(cact, 0), None, ALU.mult))
                for k in range(1, KD):
                    ins = dve.scalar_tensor_tensor(dst, tile(n, k * BANK, BANK), cols(cact, k), dst, ALU.mult, ALU.add)
                    if k + 1 < KD:
                        link(ins)
                ins.then_inc(S("ada_summed"), 1)

            dve.wait_ge(S("cact"), 1)
            ada_sum(0, 3, sums[0])
            ada_cols(0, 4, EARLY_ADA, 1)
            gains(0, A_SCM, V_MIXPRE).then_inc(S("mcol0"), 1)
            dve.wait_ge(S("mcol0"), 1)
            modulate("mix0", 0, A_SHM, hT)

            dve.wait_ge(S("pos_loaded"), 16)
            link(dve.tensor_copy(rp[3], pos_i[:, :]))
            for b in range(TB):
                link(dve.tensor_scalar(cols(rp[0], b * HALF, HALF), cons[:, C_FREQ:C_FREQ + HALF],
                                       cols(rp[3], b), None, ALU.mult))
            reduced(rp[0], rp[2])
            link(dve.tensor_scalar(rp[0], rp[0], INV_2PI, None, ALU.mult))
            link(dve.tensor_scalar(rp[0], rp[0], 0.5, -0.5, ALU.min, ALU.max))
            cos_phase(rp[1], rp[0]).then_inc(S("rope_turns"), 1)
            dve.wait_ge(S("blocks_loaded"), 16)
            pair = lambda ap: ap.rearrange("p (q c) -> p q c", c=32)
            over_pair = lambda ap: ap.unsqueeze(2).broadcast_to([P, PAIRS, 32])
            dve.wait_ge(S("turned"), 4)
            for i, (dst, u1, u2, op) in enumerate(((bb[0], b_re, b_im, ALU.subtract), (bb[1], b_im, b_re, ALU.add))):
                link(dve.tensor_tensor(pair(pq3), pair(u1), over_pair(cf_re), ALU.mult))
                link(dve.tensor_tensor(pair(pq4), pair(u2), over_pair(cf_im), ALU.mult))
                dve.tensor_tensor(dst, pq3, pq4, op).then_inc(S("bb"), 1)
                dve.wait_ge(S("bb"), i + 1)
            for i in range(1, len(sums) - 1):
                ada_sum(i, DVE_ADA[i], sums[i])

            dve.wait_ge(*tile_done(AT["w_in", 1]))
            for k in DVE_SLICES:
                dve.tensor_copy(cols(hT, k * T, T), bank(k // 2, (k % 2) * T, T)).then_inc(S("u_dve"), 1)
            dve.wait_ge(S("bb_turned"), 2)
            dve.tensor_copy(bbT[0], psum[:, 4 * BANK:6 * BANK]).then_inc(S("bbT_re"), 1)
            dve.wait_ge(S("rope_tab"), 2)
            dve.wait_ge(S("sum_turned"), 1)
            ada_sum(len(sums) - 1, DVE_ADA[len(sums) - 1], sums[-1])
            shape = [P, PAIRS_KT, 2, CHUNK]

            def skip(k):
                dve.wait_ge(S("y_ssm"), k + 1)
                dve.scalar_tensor_tensor(cols(hT, k * T, T), cols(hT, k * T, T), cols(vec, V_SSMD + k),
                                         bank(4, 0, T), ALU.mult, ALU.add).then_inc(S("y_skip"), 1)

            def slice_sum(t):
                dve.wait_ge(S("sum_turned"), DVE_ADA.index(t))
                ada_sum(DVE_ADA.index(t), t, part_sum)

            for k in range(KD):
                cos, sin = tabs[k % 2]
                v_re, v_im = (psum[:, 0:4 * BANK].rearrange("p (q i c t) -> p q i c t", q=PAIRS_KT, i=2, c=2)[:, :, i]
                              for i in range(2))
                if k >= 1:
                    dve.wait_ge(S("scan"), 8 * k)
                dve.wait_ge(S("v"), k + 1)
                dve.wait_ge(S("table"), 2 * (k + 1))
                for i, (dst, v1, v2, op) in enumerate(((rot[0], v_re, v_im, ALU.add), (rot[2], v_im, v_re,
                                                                                       ALU.subtract))):
                    dve.tensor_tensor(four(dst), wide(cos, shape), v1, ALU.mult).then_inc(S("v_read"), 1)
                    dve.tensor_tensor(four(rot[1]), wide(sin, shape), v2, ALU.mult).then_inc(S("v_read"), 1)
                    dve.wait_ge(S("v_read"), 4 * k + 2 * i + 2)
                    link(dve.tensor_tensor(dst, dst, rot[1], op))
                slice_sum(DVE_ADA_SLICE[k][0])
                if k >= 1:
                    dve.wait_ge(S("rotated"), 4 * k)

                def scan(g, r, j, ch, first):
                    o = j * T + ch * CHUNK
                    i = PAIRS_KT * k + j
                    return dve.tensor_tensor_scan(cols(g, o, CHUNK), cols(mag, i).broadcast_to([P, CHUNK]),
                                                  cols(r, o, CHUNK), first, ALU.mult, ALU.add)
                for j in range(PAIRS_KT):
                    for g, r in ((g_re, rot[0]), (g_im, rot[2])):
                        last = scan(g, r, j, 0, 0.0)
                        last.then_inc(S("dve_chain"), 1)
                        chained[0] += 1
                dve.wait_ge(S("dve_chain"), chained[0])
                ends = [four(g)[:, :, 0, CHUNK - 1] for g in (g_re, g_im)]
                last_t = [t_.rearrange("p (q t) -> p q t", t=CHUNK)[:, :, CHUNK - 1] for t_ in (cos, sin)]
                cc = [cols(carry, i * PAIRS_KT, PAIRS_KT) for i in range(6)]
                for dst, t_, g in ((cc[0], 0, 0), (cc[1], 1, 1), (cc[2], 0, 1), (cc[3], 1, 0)):
                    chained[0] += 1
                    dve.tensor_tensor(dst, last_t[t_], ends[g], ALU.mult).then_inc(S("dve_chain"), 1)
                dve.wait_ge(S("dve_chain"), chained[0])
                link(dve.tensor_tensor(cc[0], cc[0], cc[1], ALU.subtract))
                link(dve.tensor_tensor(cc[2], cc[2], cc[3], ALU.add))
                for j in range(PAIRS_KT):
                    for g, r, c in ((g_re, rot[0], cc[0]), (g_im, rot[2], cc[2])):
                        scan(g, r, j, 1, cols(c, j)).then_inc(S("scan"), 1)
                if k == KD - 1:
                    for i, (tab, g) in enumerate(((cos, g_re), (sin, g_im))):
                        if i == 0:
                            dve.wait_ge(S("scan"), 8 * KD)
                            dve.wait_ge(S("y_ssm"), k)
                        dve.tensor_tensor(four(prods[i]), wide(tab, shape), four(g), ALU.mult
                                          ).then_inc(S("rotated_dve"), 1)
                for t in DVE_ADA_SLICE[k][1:]:
                    slice_sum(t)
                if k >= 1:
                    skip(k - 1)
            def split(q0, n, quarters, j=0, first=0, last=True):
                for i in range(first, quarters):
                    qn = q0 + i
                    dve.wait_ge(S("w_hi"), qn + 1 + j * E_QUARTERS)
                    ins = dve.tensor_tensor(w_lo[qn % 4][:, :], tile(n, i * QUARTER, QUARTER), w_hi[qn % 4][:, :],
                                            ALU.subtract)
                    ins.then_inc(S("w_lo"), 1)
                if last:
                    dve.wait_ge(S("w_lo"), q0 + quarters + j * E_QUARTERS)
                    dve.nop().then_inc(S("tile_used"), 1)

            for k in range(KD):
                if k == KD // 2:
                    skip(KD - 1)
                dve.wait_ge(S("s_hi"), k + 1)
                dve.tensor_tensor(s_lo[:, k * T:(k + 1) * T], cols(hT, k * T, T), s_hi[:, k * T:(k + 1) * T],
                                  ALU.subtract).then_inc(S("s_lo"), 1)
            split(Q_OUT, AT["w_out", 0], 4)
            ada_cols(4, ADA_TILES, ADA_TILES - len(DVE_ADA), len(DVE_ADA))
            for dst, scale, gain in ((8, A_SCF, V_FFNPRE), (16, 48 + A_SCM, V_MIXPRE + 8), (24, A_KV + 8, V_KVNORM),
                                     (32, 48 + A_SCF, V_FFNPRE + 8)):
                gains(dst, scale, gain).then_inc(S("mcols"), 1)
            for i, (g, gain) in enumerate(((A_GM, V_MIXPOST), (A_GF, V_FFNPOST), (48 + A_GM, V_MIXPOST + 8),
                                           (48 + A_GF, V_FFNPOST + 8))):
                dve.tensor_tensor(cols(gcol, i * KD, KD), cols(adaC, g, KD), cols(vec, gain, KD), ALU.mult
                                  ).then_inc(S("mcols"), 1)
            dve.wait_ge(S("mcols"), 8)
            for i in range(4):
                if i < 3:
                    split(Q_OUT + 4 * (i + 1), AT["w_out", i + 1], 4)
                for b in range(TB):
                    dve.wait_ge(S("z_sigmoid"), TB * i + b + 1)
                    dve.tensor_tensor(cols(zz, b * D + i * FG, FG), bank(Z_BANKS[i % 2][b], 0, FG),
                                      cols(f_sg, b * FG, FG), ALU.mult).then_inc(S("z_gated"), 1)
            dve.wait_ge(S("z_gated"), 4 * TB)
            for b in range(TB):
                last = cols(zz, b * D + 3 * FG, FG)
                link(dve.scalar_tensor_tensor(cols(f_h, 2 * FG + b * FG, FG), last, 1.0, last, ALU.mult, ALU.mult,
                                              accum_out=cols(z_squares, 4 * b + 3)))
            dve.wait_ge(S("z_squares"), 3 * TB)
            link(dve.reduce_sum(cols(stat, NORMS["mix0p"], TB), z_squares[:, :].rearrange("p (b i) -> p b i", b=TB), AX.X))
            mean_root("mix0p", D)
            dve.wait_ge(S("gates"), 1)
            residual("mix0p", [cols(zz, b * D, D) for b in range(TB)], psum[:, 6 * BANK:8 * BANK], zz)
            normed("ffn0")
            split(Q_FFN, AT["ffn_gu", 0], 2, last=False)
            modulate("ffn0", 8, A_SHF, hT)

            for k in range(KD):
                dve.wait_ge(S("s_hi"), KD + k + 1)
                dve.tensor_tensor(s_lo[:, k * T:(k + 1) * T], cols(hT, k * T, T), s_hi[:, k * T:(k + 1) * T],
                                  ALU.subtract).then_inc(S("s_lo"), 1)

            split(Q_FFN, AT["ffn_gu", 0], 4, first=2)

            def swiglu(tag, blocks_, groups, h_, h_hi, h_lo, sg, n0, q0, j):
                wide_ = blocks_ * P

                def part(kind, g, i0=0, i1=4):
                    q1 = q0 + quarters_before(groups, kind, g)
                    if kind == "gu":
                        split(q1, n0 + place(groups, kind, g), i1, j, i0, i1 == 4)
                    else:
                        h = 2 * (g % 2)
                        split(q1 - h, n0 + place(groups, kind, g // 2), h + 2, j, h, g % 2 == 1 or g == groups - 1)

                def product(g):
                    for b in range(blocks_):
                        dve.wait_ge(S(tag + "_silu"), blocks_ * g + b + 1 + j * groups * blocks_)
                        if g >= 2 and b == 0:
                            dve.wait_ge(S(tag + "_turned"), g - 1 + j * groups)
                        i, bk = (b, 2 * (g % 2) + b) if blocks_ == 2 else (g % 2, g % 2)
                        dve.tensor_tensor(cols(h_, ((g % 2) * blocks_ + b) * FG, FG), bank(bk, FG, FG),
                                          cols(sg, i * FG, FG), ALU.mult).then_inc(S(tag + "_h"), 1)

                def turned(g):
                    dve.wait_ge(S(tag + "_hi"), g + 1 + j * groups)
                    o = (g % 2) * 2 * wide_
                    dve.tensor_tensor(h_lo[:, o:o + 2 * wide_], bank(TURN_BANK[blocks_][g % 2], 0, 2 * wide_),
                                      h_hi[:, o:o + 2 * wide_], ALU.subtract).then_inc(S(tag + "_lo"), 1)

                if blocks_ == 1:
                    part("gu", 0)
                    gated_result(j)
                    part("gu", 1, 0, 2)
                    add_result(j)
                    turned_places(j)
                    dve.wait_ge(S("w_lo_pool"), 2 * (j + 1))
                    dve.nop().then_inc(S("w_lo"), 2)
                    dve.wait_ge(S("w_lo"), q0 + 8 + j * E_QUARTERS)
                    dve.nop().then_inc(S("tile_used"), 1)
                    product(0)
                    item_places(j + 1)
                else:
                    part("gu", 1)
                    product(0)
                part("gu", 2, 0, 2)
                product(1)
                turned(0)
                part("gu", 2, 2, 4)
                for g in range(groups):
                    if 3 <= g + 2 < groups:
                        part("gu", g + 2)
                    if g + 1 < groups:
                        part("dn", g)
                    if g + 2 < groups:
                        product(g + 2)
                    elif g + 2 == groups:
                        part("dn", g + 1)
                    if g + 1 < groups:
                        turned(g + 1)
                    if g + 2 == groups and blocks_ == 1:
                        item_tokens(j + 1)

            swiglu("f", TB, F_GROUPS, f_h, f_hi, f_lo, f_sg, AT["ffn_gu", 0], Q_FFN, 0)
            y_ = [psum[:, (4 + 2 * b) * BANK:(6 + 2 * b) * BANK] for b in range(TB)]
            mean_root("ffn0p", D)
            residual("ffn0p", y_, cols(zz, 0, D), hsT)
            normed("mix1")
            modulate("mix1", 24, A_KV, hsT)
            modulate("mix1", 16, 48 + A_SHM, hT)

            W3 = KVLORA + 2 * ROPE
            R = KVLORA + ROPE

            def turn(dst1, dst2, x1, x2, b, lead, t1, t2):
                c_, s_ = cols(rope, b * HALF, HALF), cols(rope, 64 + b * HALF, HALF)
                if lead:
                    c_, s_ = (v_.unsqueeze(1).broadcast_to([P, lead, HALF]) for v_ in (c_, s_))
                for dst, u1, u2, f1, f2, op in ((dst1, x1, x2, c_, s_, ALU.subtract), (dst2, x1, x2, s_, c_, ALU.add)):
                    link(dve.tensor_tensor(t1, u1, f1, ALU.mult))
                    link(dve.tensor_tensor(t2, u2, f2, ALU.mult))
                    link(dve.tensor_tensor(dst, t1, t2, op))

            for b in range(TB):
                dve.wait_ge(S("ckr"), b + 1)
                o = b * W3
                link(dve.tensor_copy(cols(ckv, o, KVLORA), bank(6 + b, 0, KVLORA)))
                k1, k2 = o + KVLORA, o + KVLORA + HALF
                turn(cols(ckv, k1, HALF), cols(ckv, k2, HALF), bank(6 + b, KVLORA, HALF), bank(6 + b, KVLORA + HALF, HALF),
                     b, 0, cols(ratmp, 0, HALF), cols(ratmp, HALF, HALF))
                dve.tensor_copy(cols(ckv, o + R, ROPE), cols(ckv, k1, ROPE)).then_inc(S("ckv"), 1)
            latent_normed("kvl", ckv, KVLORA, W3)
            for b in range(TB):
                dve.wait_ge(S("cq_"), b + 1)
                dve.tensor_copy(cols(cq, b * QLORA, QLORA), bank(4 + b, 0, QLORA)).then_inc(S("cq"), 1)
            dve.wait_ge(S("cq"), 2)
            latent_normed("ql", cq, QLORA, QLORA)
            dve.wait_ge(S("ckv_turned"), 1)
            dve.tensor_copy(krT, bank(3, 0, T)).then_inc(S("krT"), 1)
            for i in range(TB * 2):
                dve.wait_ge(S("v_kv"), i + 1)
                dve.tensor_copy(cols(vv, i * BANK, BANK), bank(4 + i)).then_inc(S("vv"), 1)
            heads = lambda ap, o: ap.rearrange("p (h d) -> p h d", h=HEADS)[:, :, o:o + HALF]
            rt = [cols(xn, i * 256, 256).rearrange("p (h d) -> p h d", h=HEADS) for i in range(2)]
            for b in range(TB):
                dve.wait_ge(S("qr_"), b + 1)
                dst = cols(qr, b * 512, 512)
                turn(heads(dst, 0), heads(dst, HALF), heads(bank(4 + b), 0), heads(bank(4 + b), HALF), b, HEADS,
                     rt[0], rt[1])
                dve.nop().then_inc(S("qr"), 1)
            for b in range(TB):
                dve.wait_ge(S("qr_turned"), b + 1)
                dve.tensor_copy(cols(qrT, b * 512, 512), bank(6 + b)).then_inc(S("qrT"), 1)

            def step_max(s):
                blk, h0, n, nk = STEPS[s]
                i = STEP_AT[s]
                dve.wait_ge(S("score"), s + 1)
                if s >= 2:
                    dve.wait_ge(S("p_turned"), s - 1)
                sc = cols(sc_, (s % 2) * BANK, BANK).rearrange("p (h t) -> p h t", h=n)
                ps = bank(s % 2).rearrange("p (h t) -> p h t", h=n)
                if blk:
                    link(dve.tensor_copy(sc[:, :, 0:P], ps[:, :, 0:P]))
                link(dve.tensor_tensor(sc[:, :, nk - P:nk], ps[:, :, nk - P:nk],
                                       cols(cons, C_MASK, P).unsqueeze(1).broadcast_to([P, n, P]), ALU.add))
                link(dve.reduce_max(cols(smx, i, n), sc, AX.X))
                dve.tensor_scalar(cols(smx, 16 + i, n), cols(smx, i, n), -SCALE, None, ALU.mult
                                  ).then_inc(S("score_max"), 1)

            def step_probs(s):
                blk, h0, n, nk = STEPS[s]
                i = STEP_AT[s]
                dve.wait_ge(S("score_exp"), STEP_AT[s + 1])
                link(dve.reciprocal(cols(smx, 48 + i, n), cols(smx, 32 + i, n)))
                sc = cols(sc_, (s % 2) * BANK, BANK).rearrange("p (h t) -> p h t", h=n)
                dve.tensor_tensor(sc, sc, cols(smx, 48 + i, n).unsqueeze(2).broadcast_to([P, n, nk]), ALU.mult
                                  ).then_inc(S("probs"), 1)

            def step_out(s):
                blk, h0, n, nk = STEPS[s]
                dve.wait_ge(S("o"), s + 1)
                dve.tensor_copy(oT.rearrange("p (h t) -> p h t", t=T)[:, h0:h0 + 2 * n - 1:2,
                                                                  blk * P:(blk + 1) * P],
                                bank(4 + s % 2, 0, n * P).rearrange("p (h t) -> p h t", h=n)).then_inc(S("oT"), 1)

            step_max(0)
            for s in range(len(STEPS)):
                if s + 1 < len(STEPS):
                    step_max(s + 1)
                step_probs(s)
                if s >= 1:
                    step_out(s - 1)
            step_out(len(STEPS) - 1)
            mean_root("mix1p", D)
            dve.wait_ge(S("gate_row"), 2)
            residual("mix1p", y_, cols(xn, D, D), hsT)
            normed("ffn1")
            modulate("ffn1", 32, 48 + A_SHF, hT)

            def item_tokens(j):
                for c in range(2):
                    dve.wait_ge(S("xe_hi"), 2 * j + c + 1)
                    dve.tensor_tensor(xe_lo[:, c * BANK:(c + 1) * BANK], bank(6 + c), xe_hi[:, c * BANK:(c + 1) * BANK],
                                      ALU.subtract).then_inc(S("xe_lo"), 1)

            def item_places(j):
                for b in range(TB):
                    col = b * (ITEMS + 1) + j
                    col = slice(col, col + 1) if isinstance(j, int) else bass.ds(col, 1)
                    dve.tensor_scalar(cols(pm, b * P, P), iota, posj[:, col], None, ALU.is_equal
                                      ).then_inc(S("places_of_item"), 1)
                    dve.tensor_copy(cols(gate_t, b), gj[:, col]).then_inc(S("places_of_item"), 1)

            dve.wait_ge(S("rows"), 2)
            for b in range(TB):
                dve.wait_ge(S("turned"), 4 * len(TURNED))
                link(dve.tensor_tensor(cols(xn, b * D, D), cols(xn, b * D, D), psum[:, 4 * BANK:6 * BANK], ALU.mult))
                link(dve.tensor_tensor(cols(xn, b * D, D), cols(xn, b * D, D), psum[:, 6 * BANK:8 * BANK], ALU.add))

            dve.wait_ge(S("logits"), 2)
            link(dve.memset(ones8, 1.0))
            link(dve.tensor_copy(lg, bank(0, 0, TB * 8)))
            by_block = lambda ap: ap.rearrange("p (b e) -> p b e", b=TB)
            iota8 = cols(iota, 0, 8)
            iota8b = iota8.unsqueeze(1).broadcast_to([P, TB, 8])
            for b in range(TB):
                link(dve.max(cols(mx, b * 8, 8), cols(lg, b * 8, 8)))
                link(dve.max_index(cols(idx8, b * 8, 8), cols(mx, b * 8, 8), cols(lg, b * 8, 8)))
            gap = gg[:, 0:TB]
            dve.tensor_tensor(gap.unsqueeze(2), by_block(mx)[:, :, 1:2], by_block(mx)[:, :, 0:1], ALU.subtract
                              ).then_inc(S("top_gap"), 1)
            link(dve.tensor_copy(ixf, idx8[:, :]))
            for dst, c in ((oh1, 0), (oh2, 1)):
                link(dve.tensor_tensor(by_block(dst), iota8b, by_block(ixf)[:, :, c:c + 1].broadcast_to([P, TB, 8]),
                                       ALU.is_equal))
            dve.tensor_tensor(msel, oh1, oh2, ALU.add).then_inc(S("chosen"), 1)
            dve.wait_ge(S("chosen"), 1)
            dve.wait_ge(S("gap_exp"), 1)
            gate1, gate2 = cols(gg, TB, TB), cols(gg, 2 * TB, TB)
            link(dve.tensor_scalar(gate1, gap, 1.0, None, ALU.add))
            link(dve.reciprocal(gate1, gate1))
            link(dve.tensor_tensor(gate2, gate1, gap, ALU.mult))
            link(dve.tensor_tensor(by_block(gsel), by_block(oh1), gate1.unsqueeze(2).broadcast_to([P, TB, 8]),
                                   ALU.mult))
            link(dve.tensor_tensor(by_block(ixf), by_block(oh2), gate2.unsqueeze(2).broadcast_to([P, TB, 8]),
                                   ALU.mult))
            link(dve.tensor_tensor(gsel, gsel, ixf, ALU.add))
            by_item = lambda ap: ap.rearrange("p (b i) -> p b i", b=TB)
            link(dve.memset(posj, -1.0))
            link(dve.memset(gj, 0.0))
            link(dve.tensor_copy(by_item(gj)[:, :, 0:8], by_block(gsel)))
            dve.wait_ge(S("places"), 1)
            link(dve.scalar_tensor_tensor(posn, bank(1, 0, TB * 8), 1.0, msel, ALU.add, ALU.mult))
            link(dve.tensor_scalar(by_item(posj)[:, :, 0:8], by_block(posn), -1.0, None, ALU.add))
            item_places(0)
            link(dve.tensor_copy(cnt, bank(1, 2 * 8, 8)))
            link(dve.tensor_scalar(over, cnt, float(P), None, ALU.is_gt))
            link(dve.tensor_tensor_scan(incl, ones8, over, 0.0, ALU.mult, ALU.add))
            link(dve.tensor_tensor(rank, incl, over, ALU.subtract))
            link(dve.tensor_scalar(cols(eid, 0), cols(incl, 7), float(EXPERTS), None, ALU.add))
            by_rank = lambda ap: ap.rearrange("p (r e) -> p r e", r=3)
            over_rank = lambda ap: ap.unsqueeze(1).broadcast_to([P, 3, 8])
            link(dve.tensor_tensor(by_rank(sel), over_rank(rank), cols(iota, 0, 3).unsqueeze(2)
                                   .broadcast_to([P, 3, 8]), ALU.is_equal))
            link(dve.tensor_tensor(by_rank(sel), by_rank(sel), over_rank(over), ALU.mult))
            link(dve.tensor_tensor(by_rank(tmp24), by_rank(sel), over_rank(iota8), ALU.mult))
            link(dve.reduce_sum(cols(eid, 1, 3), by_rank(tmp24), AX.X))
            link(dve.tensor_copy(reg_i[:, 0:1], cols(eid, 0)))
            dve.tensor_copy(reg_i[:, 8:11], cols(eid, 1, 3)).then_inc(S("items_ready"), 1)
            dve.wait_ge(S("items_ready"), 1)
            for b in range(TB):
                for dst, src in ((posj, posn), (gj, gsel)):
                    link(dve.tensor_tensor(by_rank(tmp24), by_rank(sel), over_rank(cols(src, b * 8, 8)), ALU.mult))
                    link(dve.reduce_sum(cols(dst, b * (ITEMS + 1) + 8, 3), by_rank(tmp24), AX.X))
            link(dve.tensor_scalar(by_item(posj)[:, :, 8:11], by_item(posj)[:, :, 8:11], -1.0 - P, None, ALU.add))
            item_tokens(0)
            n_items = dve.value_load(reg_i[0:1, 0:1], min_val=EXPERTS, max_val=ITEMS)

            def turned_places(j):
                dve.wait_ge(S("places_turned"), j + 1)
                dve.tensor_copy(pT[:, :], bank(2, 0, T)).then_inc(S("pT_e"), 1)
                dve.tensor_copy(gate_s, bank(3, 0, 1)).then_inc(S("gate_s"), 1)

            def gated_result(j):
                dve.wait_ge(S("quarter_used"), Q_EXP + E_QUARTERS * j)
                dve.wait_ge(S("gate_s"), j + 1)
                dve.tensor_scalar(ye_hi[:, BANK:D], bank(5), gate_s, None, ALU.mult).then_inc(S("ye_hi_dve"), 1)
                dve.wait_ge(S("ye_hi_dve"), j + 1)
                dve.scalar_tensor_tensor(ye_lo[:, BANK:D], bank(5), gate_s, ye_hi[:, BANK:D], ALU.mult,
                                         ALU.subtract).then_inc(S("ye_lo"), 1)
                dve.wait_ge(S("ye_hi"), j + 1)
                dve.scalar_tensor_tensor(ye_lo[:, 0:BANK], bank(4), gate_s, ye_hi[:, 0:BANK], ALU.mult,
                                         ALU.subtract).then_inc(S("ye_lo"), 1)

            def add_result(j):
                for i in range(4):
                    dve.wait_ge(S("combined"), 4 * j + i + 1)
                    dve.tensor_tensor(cols(acc, i * BANK, BANK), cols(acc, i * BANK, BANK), bank(COMB[i]),
                                      ALU.add).then_inc(S("added"), 1)
                dve.wait_ge(S("added"), 4 * (j + 1))

            dve.tensor_scalar(pT[:, :], cols(cons, 0, T), 0.0, None, ALU.mult).then_inc(S("pT_e"), 1)
            dve.memset(gate_s, 0.0).then_inc(S("gate_s"), 1)
            dve.wait_ge(S("acc_zeroed"), 1)
            with dve.Fori(0, ITEMS) as j:
                with dve.If(j < n_items):
                    swiglu("e", 1, E_GROUPS, e_h, e_hi, e_lo, e_sg, N0, Q_EXP, j)
                    dve.memset(tmp8, 0.0)
                with dve.Else():
                    dve.nop()
            gated_result(n_items)
            add_result(n_items)
            dve.nop().then_inc(S("experts_done"), 1)
            mean_root("ffn1p", D, cols(acc, D, D), cols(hsT, D, D))
            dve.wait_ge(S("gates"), 4)
            for b in range(TB):
                k = NORMS["ffn1p"] + 2
                link(dve.scalar_tensor_tensor(cols(acc, b * D, D), cols(acc, b * D, D), cols(stat, k + b),
                                              psum[:, 0:2 * BANK], ALU.mult, ALU.mult))
                dve.tensor_tensor(cols(x, b * D, D), cols(x, b * D, D), cols(acc, b * D, D), ALU.add
                                  ).then_inc(S("result"), 1)

        @block.tensor
        def _(pe):
            def turned(tag, src):
                for k in range(KD):
                    for b in range(TB):
                        if k == 0:
                            pe.wait_ge(*((S("normed"), NORMED[tag]) if b == 0 else
                                         (S("normed_act"), TURNED.index(tag) + 1)))
                        mm = pe.transpose(bank(k // 2, (k % 2) * T + b * P, P), cols(src, b * D + k * P, P), ident)
                    if k % 2:
                        mm.then_inc(S("turned"), 1)

            def ada(i, t):
                n = AT["ada", t]
                if i >= 2:
                    pe.wait_ge(S("ada_row"), i - 1)
                tile_wait(pe, n)
                for k in range(KD):
                    mm = pe.matmul(bank(6 + i % 2, 0, BANK, 0, 1), cols(cact, k), tile(n, k * BANK, BANK),
                                   start=(k == 0), stop=(k == KD - 1))
                mm.then_inc(S("tile_used"), 1)
                if i >= 1 and i != EARLY_ADA:
                    ada_turn(i - 1)

            def ada_turn(i):
                pe.wait_ge(S("ada_row"), i + 1)
                for c in range(4):
                    mm = pe.matmul(bank(5, PE_ROWS[i] * 4 + c, 1), rowbuf[0:1, c * P:(c + 1) * P], ones[0:1, 0:1],
                                   start=True, stop=True)
                mm.then_inc(S("ada_turned"), 1)

            def sum_turn(i, src):
                pe.wait_ge(S("ada_summed"), i + 1)
                for c in range(4):
                    mm = pe.matmul(bank(5, DVE_ADA[i] * 4 + c, 1), cols(src, c * P, P), cols(ones, 0),
                                   start=True, stop=True)
                mm.then_inc(S("sum_turned"), 1)

            def modulated(tag):
                pe.wait_ge(S("mod_act"), 4 * MODULATED.index(tag) + 4)
                pe.wait_ge(S("mod_dve"), 4 * MODULATED.index(tag) + 4)

            def row(columns, b0, done):
                for k in range(KD):
                    mm = pe.matmul(bank(b0 + k // 4, (k % 4) * P, P), cols(columns, k).broadcast_to([P, P]),
                                   ident, start=True, stop=True)
                mm.then_inc(S(done), 1)

            def gates(i, b0):
                row(cols(gcol, i * KD, KD), b0, "gates")

            def split_product(dst, hi, lo, qn, o, first, last):
                pe.matmul(dst, hi, w_hi[qn % 4][:, o:o + BANK], start=first, stop=False)
                pe.matmul(dst, lo, w_hi[qn % 4][:, o:o + BANK], start=False, stop=False)
                return pe.matmul(dst, hi, w_lo[qn % 4][:, o:o + BANK], start=False, stop=last)

            def up_product(q0, banks, hi, lo, width, j, parts=None):
                for i in range(4):
                    if parts is not None:
                        pe.wait_ge(S("s_lo"), parts + 2 * i + 2)
                    pe.wait_ge(S("w_lo"), q0 + i + 1 + j * E_QUARTERS)
                    for b, bk in enumerate(banks):
                        for c in range(2):
                            k = 2 * i + c
                            x0 = k * width + b * P
                            mm = split_product(bank(bk), hi[:, x0:x0 + P], lo[:, x0:x0 + P], q0 + i, c * BANK,
                                               k == 0, k == KD - 1)
                    mm.then_inc(S("quarter_used"), 1)

            pe.wait_ge(S("cons_loaded"), 16)
            turned("mix0", xn)
            pe.wait_ge(S("cact"), 1)
            for t in range(EARLY_ADA):
                ada(t, t)
            ada_turn(EARLY_ADA - 1)
            sum_turn(0, sums[0])
            modulated("mix0")
            n = AT["w_in", 0]
            tile_wait(pe, n)
            tile_wait(pe, n + 1)
            for c in range(KD):
                for k in range(KD):
                    mm = pe.matmul(bank(c // 2, (c % 2) * T, T), tile(n + k // 4, (k % 4) * D + c * P, P),
                                   cols(hT, k * T, T), start=(k == 0), stop=(k == KD - 1))
                    if c == KD - 1 and k in (3, 7):
                        mm.then_inc(S("tile_used"), 1)

            pe.wait_ge(S("mcol0"), 1)
            for i in range(2):
                pe.wait_ge(S("bb"), i + 1)
                for k in range(KD):
                    mm = pe.transpose(bank(4 + 2 * i + k // 4, (k % 4) * P, P), cols(bb[i], k * P, P), ident)
                    if k % 4 == 3:
                        mm.then_inc(S("bb_turned"), 1)

            def v(k):
                if k >= 1:
                    pe.wait_ge(S("v_read"), 4 * k)
                for i in range(2):
                    for j in range(PAIRS_KT):
                        r = slice(32 * j, 32 * j + 32)
                        mm = pe.matmul(bank(j, i * T, T),
                                       bbT[i][r, k * P:(k + 1) * P], hT[r, k * T:(k + 1) * T],
                                       start=True, stop=True)
                mm.then_inc(S("v"), 1)

            def y(k):
                pe.wait_ge(S("c_negated"), 2)
                if k >= 1:
                    pe.wait_ge(S("y_skip"), k)
                for j in range(PAIRS_KT):
                    o = (PAIRS_KT * k + j) * 32
                    for i, c in enumerate((c_re, cn_re, c_im, c_im)):
                        if j == 0 and k < KD - 1:
                            pe.wait_ge(S("rotated"), 4 * k + i + 1)
                        elif j == 0:
                            pe.wait_ge(S("rotated_dve" if i < 2 else "rotated"), i + 1 if i < 2 else 4 * k + i - 1)
                        mm = pe.matmul(bank(4, 0, T, 32 * j, 32 * j + 32), cols(c, o, 32),
                                       cols(prods[i], j * T, T), start=(i == 0), stop=(i == 3))
                mm.then_inc(S("y_ssm"), 1)

            pe.wait_ge(S("bbT_re"), 1)
            pe.wait_ge(S("bbT_im"), 1)
            pe.wait_ge(S("u_act"), 4)
            pe.wait_ge(S("u_dve"), 4)
            v(0)
            for i in range(1, len(sums)):
                sum_turn(i, sums[i])
            i = EARLY_ADA
            for k in range(KD):
                if k + 1 < KD:
                    v(k + 1)
                sum_turn(DVE_ADA.index(DVE_ADA_SLICE[k][0]), part_sum)
                for n_, t in enumerate(PE_ADA[k]):
                    ada(i, t)
                    i += 1
                    if n_ == 0:
                        for t in DVE_ADA_SLICE[k][1:]:
                            sum_turn(DVE_ADA.index(t), part_sum)
                y(k)
            ada_turn(i - 1)
            for i in range(4):
                if i == 1:
                    pe.wait_ge(S("mcols"), 8)
                    gates(0, 6)
                if i >= 2:
                    pe.wait_ge(S("z_gated"), TB * (i - 1))
                up_product(Q_OUT + 4 * i, Z_BANKS[i % 2], s_hi, s_lo, T, 0, 0 if i == 0 else None)
            pe.wait_ge(S("z_gated"), 4 * TB)
            gates(1, 4)
            turned("ffn0", xn)

            def swiglu(tag, blocks_, groups, x_hi, x_lo, width, h_, h_hi, h_lo, q0, j):
                wide_ = blocks_ * P

                def up(g):
                    if blocks_ == 2 and g >= 2:
                        pe.wait_ge(S(tag + "_lo"), g - 1)
                    elif blocks_ == 1 and g >= 2:
                        pe.wait_ge(S(tag + "_h"), g - 1 + j * groups)
                    up_product(q0 + quarters_before(groups, "gu", g),
                               (2 * (g % 2), 2 * (g % 2) + 1) if blocks_ == 2 else (g % 2,), x_hi, x_lo, width, j,
                               KD if blocks_ == 2 and g == 0 else None)

                def turn(g):
                    pe.wait_ge(S(tag + "_h"), blocks_ * (g + 1 + j * groups))
                    if g >= 2:
                        pe.wait_ge(S(tag + "_lo"), g - 1 + j * groups)
                    if blocks_ == 1 and g == 0:
                        pe.wait_ge(S("gate_s"), j + 2)
                    for i in range(2):
                        for b in range(blocks_):
                            mm = pe.transpose(bank(TURN_BANK[blocks_][g % 2], i * wide_ + b * P, P),
                                              cols(h_, ((g % 2) * blocks_ + b) * FG + i * P, P), ident)
                    mm.then_inc(S(tag + "_turned"), 1)

                def down(g):
                    pe.wait_ge(S(tag + "_lo"), g + 1 + j * groups)
                    if blocks_ == 2 and g == 0:
                        pe.wait_ge(S("gate_row"), 1)
                    for i in range(2):
                        qn = q0 + quarters_before(groups, "dn", g) + i
                        pe.wait_ge(S("w_lo"), qn + 1 + j * E_QUARTERS)
                        for b in range(blocks_):
                            x0 = (g % 2) * 2 * wide_ + i * wide_ + b * P
                            for c in range(2):
                                mm = split_product(bank(4 + 2 * b + c), h_hi[:, x0:x0 + P], h_lo[:, x0:x0 + P], qn,
                                                   c * BANK, g == 0 and i == 0, g == groups - 1 and i == 1)
                        mm.then_inc(S("quarter_used"), 1)

                up(0)
                if blocks_ == 1:
                    combine(j)
                    turn_places(j)
                up(1)
                turn(0)
                if blocks_ == 1:
                    pe.wait_ge(S("added"), 4 * (j + 1))
                for g in range(groups):
                    if g + 2 < groups:
                        up(g + 2)
                    elif g + 2 == groups and blocks_ == 1:
                        dispatch(j + 1)
                    if g + 1 < groups:
                        turn(g + 1)
                    down(g)

            swiglu("f", TB, F_GROUPS, s_hi, s_lo, T, f_h, f_hi, f_lo, Q_FFN, 0)
            turned("mix1", xn)

            for tag, src, name, done, width, b0 in (("kv", hsT, "dkv", "ckr", KVLORA + ROPE, 6),
                                                    ("mix1", hT, "dq", "cq_", QLORA, 4)):
                n = AT[name, 0]
                modulated(tag)
                tile_wait(pe, n)
                for b in range(TB):
                    for k in range(KD):
                        mm = pe.matmul(bank(b0 + b, 0, width), cols(src, k * T + b * P, P),
                                       tile(n, k * width, width), start=(k == 0), stop=(k == KD - 1))
                    mm.then_inc(S(done), 1)
            W3 = KVLORA + 2 * ROPE
            pe.wait_ge(S("normed"), NORMED["kvl"])
            for b in range(TB):
                for k in range(2):
                    pe.transpose(bank(2, k * T + b * P, P), cols(ckv, b * W3 + k * P, P), ident)
                mm = pe.transpose(bank(3, b * P, P), cols(ckv, b * W3 + KVLORA, P), ident)
            mm.then_inc(S("ckv_turned"), 1)
            pe.wait_ge(S("cq"), 2)
            for _ in range(2):
                pe.nop().then_inc(S("tile_used"), 1)

            def keys_or_queries(i, n, width, src, kk):
                if i >= 2:
                    pe.wait_ge(S("kq_out"), i - 1)
                for h in range(2):
                    for k in range(kk):
                        mm = pe.matmul(bank(i % 2, h * T, T), tile(n, k * width + (2 * (i % 4) + h) * P, P),
                                       cols(src, k * T, T), start=(k == 0), stop=(k == kk - 1))
                mm.then_inc(S("kq"), 1)

            n = AT["ukv", 0]
            tile_wait(pe, n)
            pe.wait_ge(S("ckvT"), 2)
            for i in range(4):
                keys_or_queries(i, n, 2 * D, ckvT, 2)
            pe.wait_ge(S("normed"), NORMED["ql"])
            pe.wait_ge(S("krT"), 1)
            for b in range(TB):
                for k in range(3):
                    mm = pe.transpose(psum[:, 2 * BANK + k * T + b * P:2 * BANK + k * T + (b + 1) * P],
                                      cols(cq, b * QLORA + k * P, P), ident)
            mm.then_inc(S("cq_turned"), 1)
            for b in range(TB):
                for c in range(2):
                    for k in range(2):
                        mm = pe.matmul(bank(4 + 2 * b + c), cols(ckvT, k * T + b * P, P),
                                       tile(n, k * 2 * D + D + c * BANK, BANK), start=(k == 0), stop=(k == 1))
                    mm.then_inc(S("v_kv"), 1)
            n = AT["uqr", 0]
            tile_wait(pe, n)
            pe.wait_ge(S("cqT"), 3)
            for b in range(TB):
                pe.wait_ge(S("vv"), b + 1)
                for k in range(3):
                    mm = pe.matmul(bank(4 + b), cols(cqT, k * T + b * P, P), tile(n, k * 512, 512), start=(k == 0),
                                   stop=(k == 2))
                mm.then_inc(S("qr_"), 1)
            pe.wait_ge(S("vv"), 4)
            pe.wait_ge(S("qr_"), 2)
            for _ in range(2):
                pe.nop().then_inc(S("tile_used"), 1)
            n = AT["uqn", 0]
            tile_wait(pe, n)
            for i in range(4, 8):
                keys_or_queries(i, n, D, cqT, 3)
            pe.wait_ge(S("qr"), 2)
            for b in range(TB):
                for k in range(4):
                    mm = pe.transpose(bank(6 + b, k * P, P), cols(qr, b * 512 + k * P, P), ident)
                mm.then_inc(S("qr_turned"), 1)
            pe.wait_ge(S("kq_out"), 8)
            pe.nop().then_inc(S("tile_used"), 1)
            pe.wait_ge(S("qrT"), 2)

            def scores(s):
                blk, h0, n, nk = STEPS[s]
                if s >= 2:
                    pe.wait_ge(S("score_max"), s - 1)
                for h in range(h0, h0 + 2 * n, 2):
                    dst = bank(s % 2, (h - h0) // 2 * nk, nk)
                    pe.matmul(dst, cols(qT, h * T + blk * P, P), cols(kT, h * T, nk), start=True, stop=False)
                    r = slice(64 * (h % 2), 64 * (h % 2) + 64)
                    mm = pe.matmul(dst, qrT[r, blk * 512 + (h // 2) * P:blk * 512 + (h // 2 + 1) * P],
                                   krT[r, 0:nk], start=False, stop=True)
                mm.then_inc(S("score"), 1)

            def turn_probs(s):
                blk, h0, n, nk = STEPS[s]
                pe.wait_ge(S("probs"), s + 1)
                if s >= 2:
                    pe.wait_ge(S("pT"), s - 1)
                for c in range(BANK // P):
                    mm = pe.transpose(bank(2 + s % 2, c * P, P), cols(sc_, (s % 2) * BANK + c * P, P), ident)
                mm.then_inc(S("p_turned"), 1)

            def attend(s):
                blk, h0, n, nk = STEPS[s]
                pe.wait_ge(S("pT"), s + 1)
                if s >= 2:
                    pe.wait_ge(S("oT"), s - 1)
                for h in range(n):
                    for kb in range(blk + 1):
                        mm = pe.matmul(bank(4 + s % 2, h * P, P), cols(vv, kb * D + (h0 + 2 * h) * VD, VD),
                                       cols(probT, (s % 2) * BANK + (h * (blk + 1) + kb) * P, P),
                                       start=(kb == 0), stop=(kb == blk))
                mm.then_inc(S("o"), 1)

            scores(0)
            scores(1)
            gates(2, 6)
            for s in range(len(STEPS)):
                if s + 2 < len(STEPS):
                    scores(s + 2)
                turn_probs(s)
                attend(s)
            pe.wait_ge(S("oT"), len(STEPS))
            n = AT["wo", 0]
            pe.wait_ge(S("gate_row"), 2)
            tile_wait(pe, n)
            tile_wait(pe, n + 1)
            for b in range(TB):
                for c in range(2):
                    for k in range(KD):
                        mm = pe.matmul(bank(4 + 2 * b + c), cols(oT, k * T + b * P, P),
                                       tile(n + k // 4, (k % 4) * D + c * BANK, BANK),
                                       start=(k == 0), stop=(k == KD - 1))
                        if b == TB - 1 and c == 1 and k in (3, 7):
                            mm.then_inc(S("tile_used"), 1)
            pe.wait_ge(S("scaled"), 3)
            row(cols(mcol, 32, KD), 4, "rows")
            pe.wait_ge(S("scaled_1"), 3)
            row(cols(adaC, 48 + A_SHF, KD), 6, "rows")
            turned("ffn1", xn)
            modulated("ffn1")
            pe.wait_ge(S("router_loaded"), 16)
            for b in range(TB):
                for k in range(KD):
                    mm = pe.matmul(bank(0, b * 8, 8), cols(hT, k * T + b * P, P), cols(routerW, k * 8, 8),
                                   start=(k == 0), stop=(k == KD - 1))
                mm.then_inc(S("logits"), 1)
            pe.wait_ge(S("chosen"), 1)
            tri = cols(cons, C_TRI, P)
            m0, m1 = cols(msel, 0, 8), cols(msel, 8, 8)
            for dst, parts in ((0, ((tri, m0),)), (8, ((tri, m1), (ones, m0))), (16, ((ones, m0), (ones, m1)))):
                for i, (l, r) in enumerate(parts):
                    mm = pe.matmul(bank(1, dst, 8), l, r, start=(i == 0), stop=(i == len(parts) - 1))
            mm.then_inc(S("places"), 1)

            def dispatch(j):
                pe.wait_ge(S("places_of_item"), 4 * (j + 1))
                for k in range(KD):
                    for b in range(TB):
                        mm = pe.matmul(psum[:, 6 * BANK + k * P:6 * BANK + (k + 1) * P],
                                       cols(xn, b * D + k * P, P), cols(pm, b * P, P),
                                       start=(b == 0), stop=(b == TB - 1))
                    if k % 4 == 3:
                        mm.then_inc(S("dispatched"), 1)

            def turn_places(j):
                for b in range(TB):
                    pe.transpose(bank(2, b * P, P), cols(pm, b * P, P), ident)
                for b in range(TB):
                    mm = pe.matmul(bank(3, 0, 1), cols(pm, b * P, P), cols(gate_t, b), start=(b == 0),
                                   stop=(b == TB - 1))
                mm.then_inc(S("places_turned"), 1)

            def combine(j):
                pe.wait_ge(S("ye_lo"), 2 * (j + 1))
                pe.wait_ge(S("pT_e"), j + 1)
                for i in range(4):
                    b, c = divmod(i, 2)
                    for part in (ye_hi, ye_lo):
                        mm = pe.matmul(bank(COMB[i]), pT[:, b * P:(b + 1) * P], part[:, c * BANK:(c + 1) * BANK],
                                       start=(part is ye_hi), stop=(part is ye_lo))
                    mm.then_inc(S("combined"), 1)

            dispatch(0)
            pe.wait_ge(S("items_ready"), 1)
            n_items = pe.value_load(reg_i[0:1, 0:1], min_val=EXPERTS, max_val=ITEMS)
            with pe.Fori(0, ITEMS) as j:
                with pe.If(j < n_items):
                    pe.wait_ge(S("xe_lo"), 2 * (j + 1))
                    swiglu("e", 1, E_GROUPS, xe_hi, xe_lo, P, e_h, e_hi, e_lo, Q_EXP, j)
                with pe.Else():
                    pe.nop()
            gates(3, 0)
            combine(n_items)


def by_partition(v):
    return np.asarray(v).reshape(-1, P).T


def column_tiles(w, width):
    k, n = w.shape
    return np.ascontiguousarray(w.reshape(k // P, P, n // width, width).transpose(2, 1, 0, 3)).reshape(
        n // width, P, -1)


def row_tiles(w, rows):
    k, n = w.shape
    return np.ascontiguousarray(w.reshape(k // rows, rows // P, P, n).transpose(0, 2, 1, 3)).reshape(k // rows, P, -1)


def paired(w, half):
    k = w.shape[0]
    return np.ascontiguousarray(w.reshape(k, 2, half // FG, FG).transpose(0, 2, 1, 3)).reshape(k, 2 * half)


def lay_out(i):
    i = {k: np.asarray(v) for k, v in i.items()}
    c = np.zeros((P, C_N), np.float32)
    r = np.arange(P)
    c[:, C_ID:C_ID + P] = np.eye(P)
    c[:, C_MASK:C_MASK + P] = np.where(r[None, :] <= r[:, None], 0.0, -1e30)
    c[:, C_TRI:C_TRI + P] = r[:, None] < r[None, :]
    c[:, C_ONES:C_ONES + P] = 1.0
    c[:, C_IOTA:C_IOTA + P] = r[None, :]
    c[:, C_FREQ:C_FREQ + HALF] = (10000.0 ** (-np.arange(0, ROPE, 2, dtype=np.float64) / ROPE)).astype(np.float32)
    c[:, C_STEP:C_STEP + CHUNK] = r[None, :] + 1

    def states(v):
        return v.reshape(PAIRS, P).T

    parts = [by_partition(i[n].reshape(-1)) for n in ("norm_mix_pre", "norm_mix_post", "norm_ffn_pre",
                                                      "norm_ffn_post", "kv_norm", "mla_kv_norm")]
    parts += [by_partition(i["mla_q_norm"][0]), by_partition(i["ssm_d"][0]), by_partition(i["ada_b"].reshape(-1)),
              by_partition(i["kv_ada_b"]), by_partition(i["c"][0]),
              states(np.repeat(i["ssm_log_step"][0][:, None], STATES, 1)), states(i["ssm_a_re"][0]),
              states(i["ssm_a_im"][0])]

    def block_diagonal(v):
        d = np.zeros((2, STATES, PAIRS, 2, GC), np.float32)
        v = v.reshape(PAIRS, 2, STATES, GC)
        for g in range(2):
            d[g, :, :, g, :] = v[:, g].transpose(1, 0, 2)
        return d.reshape(P, PAIRS * 32)

    blocks = [block_diagonal(i["ssm_b_re"][0]), block_diagonal(i["ssm_b_im"][0]),
              block_diagonal(i["ssm_c_re"][0].transpose(0, 2, 1)), block_diagonal(i["ssm_c_im"][0].transpose(0, 2, 1))]
    ukv = i["mla_w_ukv"].reshape(KVLORA, HEADS, 2, P).transpose(0, 2, 1, 3).reshape(KVLORA, 2 * D)
    uq = i["mla_w_uq"][0].reshape(QLORA, HEADS, NOPE + ROPE)
    return {
        "x": i["x"][0],
        "vec": np.ascontiguousarray(np.concatenate(parts, 1)),
        "cons": c,
        "blocks": np.ascontiguousarray(np.concatenate(blocks, 1)),
        "router": row_tiles(i["moe_router"][0], D)[0],
        "pos": np.ascontiguousarray(i["positions"].astype(np.int32).reshape(TB, P).T),
        "ada": column_tiles(np.concatenate([i["ada_w"][0], i["ada_w"][1], i["kv_ada_w"]], 1), BANK),
        "w_in": row_tiles(i["ssm_w_in"][0], 512),
        "w_out": column_tiles(paired(i["ssm_w_out"][0], D), BANK),
        "ffn_gu": column_tiles(paired(i["ffn_w_gu"][0], DFF), BANK),
        "ffn_dn": row_tiles(np.concatenate([i["ffn_w_down"][0], np.zeros((FG, D), np.float32)], 0), 512),
        "dkv": row_tiles(i["mla_w_dkv"], D),
        "dq": row_tiles(i["mla_w_dq"][0], D),
        "ukv": row_tiles(ukv, KVLORA),
        "uqn": row_tiles(np.ascontiguousarray(uq[:, :, :NOPE].reshape(QLORA, D)), QLORA),
        "uqr": row_tiles(np.ascontiguousarray(uq[:, :, NOPE:].reshape(QLORA, 512)), QLORA),
        "wo": row_tiles(i["mla_w_o"][0], 512),
        "e_gu": np.stack([column_tiles(paired(w, EFF), BANK) for w in i["moe_w_gu"][0]]),
        "e_dn": np.stack([row_tiles(w, 512) for w in i["moe_w_down"][0]]),
    }


def kernel(**inputs):
    import concourse.bacc as bacc
    from concourse.bass_utils import run_bass_kernel_spmd

    nc = bacc.Bacc("TRN2", target_bir_lowering=False, num_devices=1)
    arrays = lay_out(inputs)
    aps = {n: nc.dram_tensor("in_" + n, v.shape, mybir.dt.from_np(v.dtype), kind="ExternalInput").ap()
           for n, v in arrays.items()}
    out = nc.dram_tensor("out_x", (T, D), FP32, kind="ExternalOutput").ap()
    build(nc, aps, out)
    r = run_bass_kernel_spmd(nc, [{"in_" + n: v for n, v in arrays.items()}], core_ids=[0])
    return r.results[0]["out_x"].reshape(1, T, D)
```
